# Optimizing a Trainium2 kernel written in Bass

```python
import math
import jax, jax.numpy as jnp
from jax import lax
import numpy as np

D_MODEL = 1024
BATCH = 1
SEQ = 1024
DEPTH = 1

N_META = 16
POOL_GROUPS = 4
POOL_GROUP_DIM = 128
POOL_WIDTH = POOL_GROUPS * POOL_GROUP_DIM
POOL_WINDOWS = (2, 4, 8, 16)
DN_HEADS = 8
DN_HEAD_DIM = 128
DN_WIDTH = DN_HEADS * DN_HEAD_DIM
CONV_WIDTH = 4
CHUNK = 64
PEER_HEADS = 8
PEER_QUERY_DIM = 256
N_KEYS = 128
N_EXPERTS = N_KEYS * N_KEYS
PEER_TOPK = 16
PEER_BLOCK = 128
N_IN = POOL_WIDTH + 4 * DN_WIDTH + 2 * DN_HEADS + 2 * D_MODEL
LN_EPS = 1e-5
RMS_EPS = 1e-6
L2_EPS = 1e-6
ALPHA = (2 * DEPTH) ** 0.25
BETA_INIT = (8 * DEPTH) ** -0.25

kernel_name = 'hybrid_pool_deltanet_peer_block'

def _layer_norm(x, g, b):
    xf = x.astype(jnp.float32)
    mu = jnp.mean(xf, axis=-1, keepdims=True)
    var = jnp.mean(jnp.square(xf - mu), axis=-1, keepdims=True)
    y = (xf - mu) * lax.rsqrt(var + LN_EPS)
    return (y * g.astype(jnp.float32) + b.astype(jnp.float32)).astype(x.dtype)

def _l2norm(t):
    return t * lax.rsqrt(jnp.sum(t * t, axis=-1, keepdims=True) + L2_EPS)

def _causal_multiscale_pool(xp, pool_w):
    bsz, length, _ = xp.shape
    xg = xp.reshape(bsz, length, POOL_GROUPS, POOL_GROUP_DIM)
    csum = jnp.cumsum(xg, axis=1)
    count = jnp.arange(1, length + 1, dtype=xp.dtype)
    outs = []
    for gi, w in enumerate(POOL_WINDOWS):
        cg = csum[:, :, gi]
        lagged = jnp.pad(cg, ((0, 0), (w, 0), (0, 0)))[:, :length]
        mean = (cg - lagged) / jnp.minimum(count, w)[None, :, None]
        outs.append(mean - xg[:, :, gi])
    pooled = jnp.stack(outs, axis=2)
    mixed = jnp.einsum('blgc,gcd->blgd', pooled, pool_w)
    return mixed.reshape(bsz, length, POOL_WIDTH)

def _causal_depthwise_conv(x, w):
    ch = x.shape[-1]
    return lax.conv_general_dilated(x, w[:, None, :], window_strides=(1,), padding=[(CONV_WIDTH - 1, 0)], dimension_numbers=('NWC', 'WIO', 'NWC'), feature_group_count=ch)

def _gated_delta_rule_chunked(q, k, v, beta, g):
    bsz, total, heads, dk = q.shape
    dv = v.shape[-1]
    n_chunks = total // CHUNK

    def to_chunks(t):
        t = t.reshape((bsz, n_chunks, CHUNK, heads) + t.shape[3:])
        return jnp.moveaxis(t, (1, 3), (0, 2))

    qc, kc, vc, bc, gch = [to_chunks(t) for t in (q, k, v, beta, g)]
    gcum = jnp.cumsum(gch, axis=-1)
    causal = jnp.tril(jnp.ones((CHUNK, CHUNK), dtype=bool))
    strict = jnp.tril(jnp.ones((CHUNK, CHUNK), dtype=bool), -1)
    diff = gcum[..., :, None] - gcum[..., None, :]
    decay = jnp.where(causal, jnp.exp(jnp.where(causal, diff, 0.0)), 0.0)
    kb = kc * bc[..., None]
    a_mat = jnp.where(strict, jnp.einsum('nbhid,nbhjd->nbhij', kb, kc) * decay, 0.0)
    eye = jnp.eye(CHUNK, dtype=q.dtype)
    rhs = jnp.concatenate([vc * bc[..., None], kb * jnp.exp(gcum)[..., None]], axis=-1)
    sol = lax.linalg.triangular_solve(eye + a_mat, rhs, left_side=True, lower=True, unit_diagonal=True)
    u_c, w_c = sol[..., :dv], sol[..., dv:]
    attn = jnp.einsum('nbhid,nbhjd->nbhij', qc, kc) * decay
    q_dec = qc * jnp.exp(gcum)[..., None]
    k_dec = kc * jnp.exp(gcum[..., -1:] - gcum)[..., None]
    chunk_decay = jnp.exp(gcum[..., -1])

    def step(state, inp):
        qd, kd, uu, ww, at, cd = inp
        v_new = uu - jnp.einsum('bhck,bhkv->bhcv', ww, state)
        out = jnp.einsum('bhck,bhkv->bhcv', qd, state) + jnp.einsum('bhij,bhjv->bhiv', at, v_new)
        state = state * cd[..., None, None] + jnp.einsum('bhck,bhcv->bhkv', kd, v_new)
        return state, out

    s0 = jnp.zeros((bsz, heads, dk, dv), q.dtype)
    _, o = lax.scan(step, s0, (q_dec, k_dec, u_c, w_c, attn, chunk_decay))
    return jnp.moveaxis(o, (0, 2), (1, 3)).reshape(bsz, total, heads, dv)

def _hybrid_mixer(h, w_in, pool_w, pool_scale, w_br_pool, conv_w, a_log, dt_bias, onorm_g, w_br_delta, w_out):
    bsz, length, _ = h.shape
    f32 = jnp.float32
    proj = jnp.einsum('bld,dn->bln', h, w_in)
    sizes = [POOL_WIDTH, 3 * DN_WIDTH, DN_WIDTH, DN_HEADS, DN_HEADS, D_MODEL, D_MODEL]
    cuts = [int(c) for c in np.cumsum(sizes)[:-1]]
    xp, qkv, z, b_logit, a_logit, gate_pool, gate_delta = jnp.split(proj, cuts, axis=-1)
    y_pool = _causal_multiscale_pool(xp.astype(f32), pool_w.astype(f32)) * pool_scale.astype(f32)
    y_a = jnp.einsum('blc,cd->bld', y_pool.astype(h.dtype), w_br_pool)
    qkv = jax.nn.silu(_causal_depthwise_conv(qkv.astype(f32), conv_w.astype(f32)))
    q, k, v = jnp.split(qkv, 3, axis=-1)
    to_heads = lambda t: t.reshape(bsz, length, DN_HEADS, DN_HEAD_DIM)
    q = _l2norm(to_heads(q)) * (DN_HEAD_DIM ** -0.5)
    k = _l2norm(to_heads(k))
    v = to_heads(v)
    beta = jax.nn.sigmoid(b_logit.astype(f32))
    g = -jnp.exp(a_log.astype(f32)) * jax.nn.softplus(a_logit.astype(f32) + dt_bias.astype(f32))
    pad = CHUNK - N_META
    padt = lambda t: jnp.pad(t, ((0, 0), (pad, 0)) + ((0, 0),) * (t.ndim - 2))
    o = _gated_delta_rule_chunked(padt(q), padt(k), padt(v), padt(beta), padt(g))[:, pad:]
    o = o * lax.rsqrt(jnp.mean(jnp.square(o), axis=-1, keepdims=True) + RMS_EPS) * onorm_g.astype(f32)
    o = o * jax.nn.silu(to_heads(z).astype(f32))
    y_b = jnp.einsum('blc,cd->bld', o.reshape(bsz, length, DN_WIDTH).astype(h.dtype), w_br_delta)
    merged = jax.nn.sigmoid(gate_pool) * y_a + jax.nn.sigmoid(gate_delta) * y_b
    return jnp.einsum('bld,de->ble', merged, w_out)

def _peer(h, wq, sub_k1, sub_k2, u_tab, v_tab):
    bsz, length, d = h.shape
    f32 = jnp.float32
    n_tok = bsz * length
    xt = h.reshape(n_tok, d)
    q = jnp.einsum('td,dq->tq', xt, wq).astype(f32).reshape(n_tok, PEER_HEADS, PEER_QUERY_DIM)
    half = PEER_QUERY_DIM // 2
    s1 = jnp.einsum('thc,hnc->thn', q[..., :half], sub_k1.astype(f32))
    s2 = jnp.einsum('thc,hnc->thn', q[..., half:], sub_k2.astype(f32))
    v1, i1 = lax.top_k(s1, PEER_TOPK)
    v2, i2 = lax.top_k(s2, PEER_TOPK)
    cand = (v1[..., :, None] + v2[..., None, :]).reshape(n_tok, PEER_HEADS, PEER_TOPK * PEER_TOPK)
    score, ci = lax.top_k(cand, PEER_TOPK)
    ia = jnp.take_along_axis(i1, ci // PEER_TOPK, axis=-1)
    ib = jnp.take_along_axis(i2, ci % PEER_TOPK, axis=-1)
    idx = ia * N_KEYS + ib
    gate = jax.nn.softmax(score, axis=-1)
    n_blk = -(-n_tok // PEER_BLOCK)
    extra = n_blk * PEER_BLOCK - n_tok
    xb = jnp.pad(xt, ((0, extra), (0, 0))).reshape(n_blk, PEER_BLOCK, d)
    idb = jnp.pad(idx, ((0, extra), (0, 0), (0, 0))).reshape(n_blk, PEER_BLOCK, PEER_HEADS, PEER_TOPK)
    gb = jnp.pad(gate, ((0, extra), (0, 0), (0, 0))).reshape(n_blk, PEER_BLOCK, PEER_HEADS, PEER_TOPK)

    def block(args):
        xx, ii, gg = args
        u = jnp.take(u_tab, ii, axis=0)
        hid = jnp.einsum('thkd,td->thk', u, xx).astype(f32)
        act = jax.nn.gelu(hid, approximate=False) * gg
        vv = jnp.take(v_tab, ii, axis=0)
        return jnp.einsum('thk,thkd->td', act.astype(vv.dtype), vv)

    out = lax.map(block, (xb, idb, gb)).reshape(n_blk * PEER_BLOCK, d)[:n_tok]
    return out.reshape(bsz, length, d)

def setup_inputs(seed: int = 0) -> dict:
    key = jax.random.key(seed)
    ks = jax.random.split(key, 24)
    f32 = jnp.float32
    nrm = lambda k, shape, scale: jax.random.normal(k, shape, f32) * scale
    x = nrm(ks[0], (BATCH, SEQ, D_MODEL), 1.0)
    meta = nrm(ks[1], (N_META, D_MODEL), 1.0)
    ln0_g = 1.0 + nrm(ks[2], (D_MODEL,), 0.02)
    ln0_b = nrm(ks[3], (D_MODEL,), 0.02)
    w_in = nrm(ks[4], (DEPTH, D_MODEL, N_IN), D_MODEL ** -0.5)
    pool_w = nrm(ks[5], (DEPTH, POOL_GROUPS, POOL_GROUP_DIM, POOL_GROUP_DIM), POOL_GROUP_DIM ** -0.5)
    pool_scale = 1.0 + nrm(ks[6], (DEPTH, POOL_WIDTH), 0.02)
    w_br_pool = nrm(ks[7], (DEPTH, POOL_WIDTH, D_MODEL), POOL_WIDTH ** -0.5)
    conv_w = nrm(ks[8], (DEPTH, CONV_WIDTH, 3 * DN_WIDTH), CONV_WIDTH ** -0.5)
    a_log = jnp.log(jax.random.uniform(ks[9], (DEPTH, DN_HEADS), f32, 1.0, 16.0))
    dt = jnp.exp(jax.random.uniform(ks[10], (DEPTH, DN_HEADS), f32, math.log(1e-3), math.log(1e-1)))
    dt_bias = dt + jnp.log(-jnp.expm1(-dt))
    onorm_g = 1.0 + nrm(ks[11], (DEPTH, DN_HEAD_DIM), 0.02)
    w_br_delta = nrm(ks[12], (DEPTH, DN_WIDTH, D_MODEL), DN_WIDTH ** -0.5)
    w_out = nrm(ks[13], (DEPTH, D_MODEL, D_MODEL), (D_MODEL ** -0.5) * BETA_INIT)
    ln1_g = 1.0 + nrm(ks[14], (DEPTH, D_MODEL), 0.02)
    ln1_b = nrm(ks[15], (DEPTH, D_MODEL), 0.02)
    peer_wq = nrm(ks[16], (DEPTH, D_MODEL, PEER_HEADS * PEER_QUERY_DIM), D_MODEL ** -0.5)
    peer_k1 = nrm(ks[17], (DEPTH, PEER_HEADS, N_KEYS, PEER_QUERY_DIM // 2), (PEER_QUERY_DIM // 2) ** -0.5)
    peer_k2 = nrm(ks[18], (DEPTH, PEER_HEADS, N_KEYS, PEER_QUERY_DIM // 2), (PEER_QUERY_DIM // 2) ** -0.5)
    peer_u = nrm(ks[19], (DEPTH, N_EXPERTS, D_MODEL), D_MODEL ** -0.5)
    peer_v = nrm(ks[20], (DEPTH, N_EXPERTS, D_MODEL), BETA_INIT)
    ln2_g = 1.0 + nrm(ks[21], (DEPTH, D_MODEL), 0.02)
    ln2_b = nrm(ks[22], (DEPTH, D_MODEL), 0.02)
    return {'x': x, 'meta': meta, 'ln0_g': ln0_g, 'ln0_b': ln0_b, 'w_in': w_in, 'pool_w': pool_w, 'pool_scale': pool_scale, 'w_br_pool': w_br_pool, 'conv_w': conv_w, 'a_log': a_log, 'dt_bias': dt_bias, 'onorm_g': onorm_g, 'w_br_delta': w_br_delta, 'w_out': w_out, 'ln1_g': ln1_g, 'ln1_b': ln1_b, 'peer_wq': peer_wq, 'peer_k1': peer_k1, 'peer_k2': peer_k2, 'peer_u': peer_u, 'peer_v': peer_v, 'ln2_g': ln2_g, 'ln2_b': ln2_b}

def reference(x, meta, ln0_g, ln0_b, w_in, pool_w, pool_scale, w_br_pool, conv_w, a_log, dt_bias, onorm_g, w_br_delta, w_out, ln1_g, ln1_b, peer_wq, peer_k1, peer_k2, peer_u, peer_v, ln2_g, ln2_b):
    bsz = x.shape[0]
    meta_b = jnp.broadcast_to(meta[None].astype(x.dtype), (bsz, N_META, D_MODEL))
    h = jnp.concatenate([meta_b, x], axis=1)
    h = _layer_norm(h, ln0_g, ln0_b)
    for i in range(DEPTH):
        mix = _hybrid_mixer(h, w_in[i], pool_w[i], pool_scale[i], w_br_pool[i], conv_w[i], a_log[i], dt_bias[i], onorm_g[i], w_br_delta[i], w_out[i])
        h = _layer_norm(ALPHA * h + mix, ln1_g[i], ln1_b[i])
        if i == DEPTH - 1:
            h = h[:, N_META:]
        h = _layer_norm(ALPHA * h + _peer(h, peer_wq[i], peer_k1[i], peer_k2[i], peer_u[i], peer_v[i]), ln2_g[i], ln2_b[i])
    return h


_drawn_inputs = setup_inputs


def setup_inputs(seed=0):
    import zlib

    import numpy as np

    out = dict(_drawn_inputs(seed))
    spreads = {}
    factors = {'meta': 3.473, 'pool_scale': 3.113, 'onorm_g': 3.724, 'ln2_g': 2.75, 'ln2_b': 2.828}
    for name, (base, spread) in spreads.items():
        noise = np.random.default_rng([zlib.crc32(name.encode()), seed]).standard_normal(out[name].shape)
        drawn = base * np.exp(spread * noise) if base else spread * noise
        out[name] = __import__('jax').numpy.asarray(drawn.astype(out[name].dtype))
    for name, factor in factors.items():
        out[name] = (out[name] * factor).astype(out[name].dtype)
    return out
```

```python
from contextlib import ExitStack

import numpy as np
import concourse.bass as bass
from concourse import mybir

F32 = mybir.dt.float32
F32R = mybir.dt.float32r
U32 = mybir.dt.uint32
ACT = mybir.ActivationFunctionType
ALU = mybir.AluOpType
AX = mybir.AxisListType

P = 128
D = 1024
DB = D // P
N_META = 16
SEQ = 1024
T = N_META + SEQ
XT = SEQ // P
HEADS = 8
HD = 128
PAIRS = HEADS // 2
CHUNK = 64
PAD = CHUNK - N_META
N_CHUNKS = (T + PAD) // CHUNK
POOL_GROUPS = 4
POOL_WINDOWS = (2, 4, 8, 16)
TAPS = 4
N_KEYS = 128
TOPK = 16
ALPHA = 2.0 ** 0.25
LN_EPS, RMS_EPS, L2_EPS = 1e-5, 1e-6, 1e-6
LOWEST = -3.0e38

BLK_Q, BLK_K, BLK_V = 0, HEADS, 2 * HEADS
BLK_Z = 3 * HEADS
BLK_GATE = BLK_Z + HEADS
BLK_POOL = BLK_GATE + 2 * DB
N_BLK = BLK_POOL + POOL_GROUPS
PIECES = 4
PIECE = T // PIECES


class Chain:

    def __init__(self, eng, sem):
        self.eng, self.sem, self.n = eng, sem, 0

    def step(self, ins):
        self.mark(ins)
        self.wait()

    def mark(self, ins):
        self.n += 1
        ins.then_inc(self.sem, 1)

    def wait(self):
        self.eng.wait_ge(self.sem, self.n)

    def restart(self):
        self.wait()
        self.eng.sem_clear(self.sem)
        self.n = 0


class Phase:

    def __init__(self, nc, name):
        self.nc, self.name, self.ctx, self.taken = nc, name, ExitStack(), []

    def __enter__(self):
        self.ctx.__enter__()
        return self

    def __exit__(self, *a):
        done = self.ctx.__exit__(*a)
        if self.taken:
            self.nc.clear_and_free_semaphores(self.taken)
            self.nc.all_engine_barrier()
        return done

    def sb(self, name, shape, dt=F32):
        return self.ctx.enter_context(self.nc.sbuf_tensor(f"{self.name}_{name}", shape, dt))

    def ps(self, name, shape, dt=F32):
        return self.ctx.enter_context(self.nc.psum_tensor(f"{self.name}_{name}", shape, dt))

    def sem(self, name):
        self.taken.append(self.nc.alloc_semaphore(f"{self.name}_{name}"))
        return self.taken[-1]

    def sems(self, name, n=2):
        return [self.sem(f"{name}{i}") for i in range(n)]

    def block(self):
        return self.ctx.enter_context(self.nc.Block())


def row_bcast(ap, n=P):
    return ap.rearrange("(a k) -> a k", a=1).partition_broadcast(n) if ap.ndim == 1 else ap.partition_broadcast(n)


def make_constants(nc, k):
    with Phase(nc, "const") as ph:
        made = ph.sem("made")
        block = ph.block()

        @block.gpsimd
        def _(pool):
            ch = Chain(pool, made)

            def select(ap, op, fill, base, pattern, mult):
                ch.step(pool.affine_select(out=ap, in_=ap, compare_op=op, fill=fill, base=base,
                                           pattern=pattern, channel_multiplier=mult))

            ch.mark(pool.memset(k["ones"][:], 1.0))
            ch.step(pool.memset(k["ident"][:], 0.0))
            select(k["ident"][:], ALU.not_equal, 1.0, 0, [[-1, P]], 1)

            def keep_blocks(m, size):
                v = m[:].rearrange("p (g e) -> p g e", e=size)
                select(v, ALU.is_ge, 0.0, 0, [[-size, P // size], [0, size]], 1)
                select(v, ALU.is_ge, 0.0, size - 1, [[size, P // size], [0, size]], -1)

            for m in (k["upper"], k["lower"], k["same_head"], k["in16"], k["in32"]):
                ch.step(pool.memset(m[:], 1.0))
            select(k["upper"][:], ALU.is_ge, 0.0, 0, [[1, P]], -1)
            select(k["lower"][:], ALU.is_gt, 0.0, 0, [[-1, P]], 1)
            for m, size in ((k["upper"], CHUNK), (k["lower"], CHUNK), (k["same_head"], CHUNK), (k["in16"], 16), (k["in32"], 32)):
                keep_blocks(m, size)


def embed_norm_phase(nc, k, io):
    with Phase(nc, "ln0") as ph:
        X = [ph.sb(f"x{u}", [P, D]) for u in range(2)]
        H = [ph.sb(f"h{u}", [P, D]) for u in range(2)]
        gain, bias = ph.sb("gain", [P, D]), ph.sb("bias", [P, D])
        stats, mv = ph.sb("stats", [P, 2, 6]), ph.sb("mv", [P, 2])
        veps, std, rstd = ph.sb("veps", [P, 1]), ph.sb("std", [P, 1]), ph.sb("rstd", [P, 1])
        TP = [ph.ps(f"t{u}", [P, DB, P]) for u in range(2)]
        consts_in = ph.sem("consts_in")
        x_in, h_out = ph.sems("x_in"), ph.sems("h_out")
        x_free, var_ready, std_ready, h_ready = (ph.sem(n) for n in ("x_free", "var_ready", "std_ready", "h_ready"))
        t_ready, t_free, hi_ready = (ph.sem(n) for n in ("t_ready", "t_free", "hi_ready"))
        own = ph.sem("dve_own")
        block = ph.block()

        @block.sync
        def _(sp):
            sp.dma_start(gain[:], row_bcast(io["ln0_g"])).then_inc(consts_in, 16)
            sp.dma_start(bias[:], row_bcast(io["ln0_b"])).then_inc(consts_in, 16)
            sp.dma_start(X[1][0:N_META, :], io["meta"][:, :]).then_inc(x_in[1], 16)
            with sp.Fori(0, XT // 2) as i:
                for u in range(2):
                    n = 2 * i + u + 1
                    sp.wait_ge(x_free, n + 1)
                    sp.dma_start(X[u][:], io["x"][bass.ts(n - 1, P), :]).then_inc(x_in[u], 16)

        @block.vector
        def _(dve):
            ch = Chain(dve, own)
            dve.sem_inc(x_free, 2)
            dve.wait_ge(consts_in, 32)

            def tile(n, u, rows, loads, cols):
                x, h = X[u][0:rows, :], H[u][0:rows, :]
                dve.wait_ge(x_in[u], 16 * loads)
                for s in range(2):
                    ch.mark(nc.vector.bn_stats(stats[0:rows, s, :], x[:, s * 512:(s + 1) * 512]))
                ch.wait()
                ch.step(nc.vector.bn_aggr(mv[0:rows, :], stats[0:rows]))
                nc.vector.tensor_scalar(veps[0:rows], mv[0:rows, 1:2], LN_EPS, None, ALU.add).then_inc(var_ready, 1)
                dve.wait_ge(std_ready, n + 1)
                ch.step(nc.vector.reciprocal(rstd[0:rows], std[0:rows]))
                if rows == P:
                    dve.wait_ge(h_out[u], 16 * (loads - u))
                    dve.wait_ge(t_ready, n - 1 + (u == 0))
                nc.vector.tensor_scalar(h, x, mv[0:rows, 0:1], rstd[0:rows], ALU.subtract, ALU.mult).then_inc(x_free, 1)
                dve.wait_ge(x_free, n + 3)
                ch.step(nc.vector.tensor_tensor(h, h, gain[0:rows, :], ALU.mult))
                nc.vector.tensor_tensor(h, h, bias[0:rows, :], ALU.add).then_inc(h_ready, 1)
                dve.wait_ge(hi_ready, n + 1)
                nc.vector.tensor_tensor(k["hT_lo"][:, :, cols], TP[u][:, :, 0:rows],
                                        k["hT_hi"][:, :, cols].bitcast(F32), ALU.subtract).then_inc(t_free, 1)
                ch.restart()

            for u in range(2):
                dve.sem_inc(h_out[u], 16)
            tile(0, 1, N_META, 1, slice(0, N_META))
            with dve.Fori(0, XT // 2) as i:
                for u in range(2):
                    tile(2 * i + u + 1, u, P, i + 1 + u, bass.ds((2 * i + u) * P + N_META, P))

        @block.scalar
        def _(act):
            def tile(n, u, rows, cols):
                act.wait_ge(var_ready, n + 1)
                nc.scalar.activation(std[0:rows], veps[0:rows], ACT.Sqrt).then_inc(std_ready, 1)
                if rows == P:
                    act.wait_ge(h_ready, n + 1)
                    act.dma_start(io["h_rows"][bass.ts(n - 1, P), :], H[u][:]).then_inc(h_out[u], 16)
                act.wait_ge(t_ready, n + 1)
                nc.scalar.copy(k["hT_hi"][:, :, cols], TP[u][:, :, 0:rows]).then_inc(hi_ready, 1)

            tile(0, 1, N_META, slice(0, N_META))
            with act.Fori(0, XT // 2) as i:
                for u in range(2):
                    tile(2 * i + u + 1, u, P, bass.ds((2 * i + u) * P + N_META, P))
            for u in range(2):
                act.wait_ge(h_out[u], 16 * (XT // 2 + 1))

        @block.tensor
        def _(pe):
            pe.sem_inc(t_free, 2)

            def tile(n, u, rows):
                pe.wait_ge(h_ready, n + 1)
                pe.wait_ge(t_free, n + 1)
                for b in range(DB):
                    last = nc.tensor.transpose(TP[u][:, b, 0:rows], H[u][0:rows, bass.ts(b, P)], k["ident"][0:rows, 0:rows])
                last.then_inc(t_ready, 1)

            tile(0, 1, N_META)
            with pe.Fori(0, XT // 2) as i:
                for u in range(2):
                    tile(2 * i + u + 1, u, P)


def mm3(nc, out, lhs, rhs, first=True, last=True):
    (lh, ll), (rh, rl) = lhs, rhs
    nc.tensor.matmul(out, lh, rh, start=first, stop=False)
    nc.tensor.matmul(out, lh, rl, start=False, stop=False)
    return nc.tensor.matmul(out, ll, rh, start=False, stop=last)


def project_phase(nc, k, io):
    with Phase(nc, "proj") as ph:
        W = [ph.sb(f"w{u}", [P, DB, P]) for u in range(2)]
        Wh = [ph.sb(f"wh{u}", [P, DB, P], F32R) for u in range(2)]
        Wl = [ph.sb(f"wl{u}", [P, DB, P], F32R) for u in range(2)]
        Y = [ph.sb(f"y{u}", [P, TAPS - 1 + T]) for u in range(2)]
        C = [ph.sb(f"c{u}", [P, T]) for u in range(2)]
        S = [ph.sb(f"s{u}", [P, T]) for u in range(2)]
        SQ = ph.sb("sq", [P, T])
        taps = ph.sb("taps", [P, 3 * HEADS, TAPS])
        epsq, epsk = ph.sb("epsq", [P, 1]), ph.sb("epsk", [P, 1])
        onorm = ph.sb("onorm", [P, 1])
        wba = ph.sb("wba", [P, DB, 16])
        wbah, wbal = ph.sb("wbah", [P, DB, 16], F32R), ph.sb("wbal", [P, DB, 16], F32R)
        ba = ph.sb("ba", [16, T])
        bat = ph.sb("bat", [P, 9, 16])
        aexp, dtb, ea = ph.sb("aexp", [P, 8]), ph.sb("dtb", [P, 8]), ph.sb("ea", [P, 9, 8])
        beta, gate = ph.sb("beta", [P, 9, 8]), ph.sb("gate", [P, 9, 8])
        M = [ph.ps(f"m{u}", [P, PIECES, 512]) for u in range(2)]
        consts_in = ph.sem("consts_in")
        w_in, s_ready, y_out = ph.sems("w_in"), ph.sems("s_ready"), ph.sems("y_out")
        wl_ready, mm_ready, c_ready = ph.sem("wl_ready"), ph.sem("mm_ready"), ph.sem("c_ready")
        wh_ready, y_ready, mm_free, silu_ready, sq_ready, norm_ready, root_ready = (
            ph.sem(n) for n in ("wh_ready", "y_ready", "mm_free", "silu_ready", "sq_ready", "norm_ready", "root_ready"))
        own = ph.sem("dve_own")
        ba_sem = {n: ph.sem(n) for n in ("ba_split", "ba_mm", "ba_rows", "ba_t", "ba_copy", "ba_act", "ba_dve", "ba_out")}
        setup, passed = ph.sem("setup"), ph.sem("passed")
        block = ph.block()
        pieces = lambda ap: ap.rearrange("p (a b) -> p a b", a=PIECES)
        banks = lambda u: M[u][:, :, 0:PIECE]
        @block.sync
        def _(sp):
            sp.dma_start(taps[:], io["conv_taps"].rearrange("p (n j) -> p n j", j=TAPS)).then_inc(consts_in, 16)
            sp.dma_start(onorm[:], io["onorm_g"].rearrange("(p a) -> p a", a=1)).then_inc(consts_in, 16)
            sp.dma_start(wba[:], io["w_ba"].rearrange("p (b c) -> p b c", c=16)).then_inc(consts_in, 16)
            sp.dma_start(aexp[:], row_bcast(io["a_log"])).then_inc(consts_in, 16)
            sp.dma_start(dtb[:], row_bcast(io["dt_bias"])).then_inc(consts_in, 16)

            with sp.Fori(0, N_BLK // 2) as r:
                for u in range(2):
                    sp.wait_ge(s_ready[u], r + 1)
                    sp.dma_start(io["proj"][bass.ds(2 * r + u, 1)].rearrange("a p t -> (a p) t"), S[u][:]).then_inc(y_out[u], 16)
            for u in range(2):
                sp.wait_ge(y_out[u], 16 * (N_BLK // 2 + 1))

        @block.gpsimd
        def _(pool):
            pool.memset(epsq[:], HD * L2_EPS).then_inc(setup, 1)
            pool.memset(epsk[:], L2_EPS).then_inc(setup, 1)
            for u in range(2):
                pool.memset(Y[u][:, 0:TAPS - 1], 0.0).then_inc(setup, 1)
            pool.sem_inc(wl_ready, 2)

            def split(n, r, u):
                pool.wait_ge(w_in[u], 16 * (r + 1))
                pool.wait_ge(mm_ready, n + 1)
                pool.sem_inc(passed, 1)
                nc.gpsimd.tensor_copy(Wh[u][:], W[u][:]).then_inc(wh_ready, 1)
                pool.wait_ge(wh_ready, n + 1)
                nc.gpsimd.tensor_tensor(Wl[u][:], W[u][:], Wh[u][:].bitcast(F32), ALU.subtract).then_inc(wl_ready, 1)

            def load(n, u):
                pool.wait_ge(wl_ready, n + 1)
                pool.dma_start(W[u][:], io["w_blocks"][bass.ds(n, 1)].rearrange("a p (b c) -> (a p) b c", c=P)).then_inc(w_in[u], 16)

            for u in range(2):
                load(u, u)
            with pool.Fori(0, N_BLK // 2 - 1) as r:
                for u in range(2):
                    split(2 * r + u, r, u)
                    load(2 * r + u + 2, u)
            for u in range(2):
                split(N_BLK - 2 + u, N_BLK // 2 - 1, u)
            pool.wait_ge(ba_sem["ba_dve"], 5)
            for src, c0 in ((beta, 0), (gate, 8)):
                dst = io["bg"][:, c0:c0 + 8]
                pool.dma_start(dst[0:N_META, :], src[0:N_META, 8, :]).then_inc(ba_sem["ba_out"], 16)
                pool.dma_start(dst[N_META:T, :].rearrange("(n p) c -> p n c", p=P), src[:, 0:8, :]).then_inc(ba_sem["ba_out"], 16)
            pool.wait_ge(ba_sem["ba_out"], 64)

        @block.tensor
        def _(pe):
            pe.sem_inc(mm_free, 2)
            pe.sem_inc(mm_ready, 2)

            def main(n, u):
                pe.wait_ge(wl_ready, n + 3)
                pe.wait_ge(mm_free, n + 1)
                for b in range(DB):
                    for wpart, hparts in ((Wh[u], (k["hT_hi"], k["hT_lo"])), (Wl[u], (k["hT_hi"],))):
                        for hpart in hparts:
                            for c in range(PIECES):
                                last = nc.tensor.matmul(M[u][:, c, 0:PIECE], wpart[:, b, :],
                                                        hpart[:, b, c * PIECE:(c + 1) * PIECE],
                                                        start=(b == 0 and wpart is Wh[u] and hpart is k["hT_hi"]),
                                                        stop=(b == DB - 1 and wpart is Wl[u]))
                last.then_inc(mm_ready, 1)

            def norm(n, u):
                pe.wait_ge(sq_ready, n + 1)
                for c in range(PIECES):
                    last = nc.tensor.matmul(M[u][:, c, 0:PIECE], k["ones"][:], SQ[:, c * PIECE:(c + 1) * PIECE], start=True, stop=True)
                last.then_inc(norm_ready, 1)

            main(0, 0)
            main(1, 1)
            norm(0, 0)
            with pe.Fori(1, BLK_V // 2) as r:
                main(2 * r, 0)
                norm(2 * r - 1, 1)
                main(2 * r + 1, 1)
                norm(2 * r, 0)
            main(BLK_V, 0)
            norm(BLK_V - 1, 1)
            main(BLK_V + 1, 1)
            with pe.Fori(BLK_V // 2 + 1, N_BLK // 2) as r:
                for u in range(2):
                    main(2 * r + u, u)
            pe.wait_ge(ba_sem["ba_split"], 2)
            pe.wait_ge(mm_free, N_BLK + 2)
            for b in range(DB):
                for c in range(PIECES):
                    cols = slice(c * PIECE, (c + 1) * PIECE)
                    last = mm3(nc, M[0][0:16, c, 0:PIECE], (wbah[:, b, :], wbal[:, b, :]), (k["hT_hi"][:, b, cols], k["hT_lo"][:, b, cols]), b == 0, b == DB - 1)
            last.then_inc(ba_sem["ba_mm"], 1)
            pe.wait_ge(ba_sem["ba_rows"], 1)
            for t in range(XT):
                nc.tensor.transpose(M[1][:, 0, t * 16:(t + 1) * 16], ba[:, N_META + t * P:N_META + (t + 1) * P], k["ident"][0:16, 0:16])
            nc.tensor.transpose(M[1][0:N_META, 0, XT * 16:(XT + 1) * 16], ba[:, 0:N_META], k["ident"][0:16, 0:16]).then_inc(ba_sem["ba_t"], 1)

        @block.scalar
        def _(act):
            act.wait_ge(setup, 4)
            act.wait_ge(consts_in, 80)

            def take(n, u):
                act.wait_ge(mm_ready, n + 3)
                act.wait_ge(c_ready, n + 1)
                nc.scalar.copy(pieces(Y[u][:, TAPS - 1:]), banks(u)).then_inc(y_ready, 1)

            def silu_square(n, u):
                act.wait_ge(c_ready, n + 3)
                nc.scalar.activation(C[u][:], C[u][:], ACT.Silu).then_inc(silu_ready, 1)
                act.wait_ge(silu_ready, n + 1)
                nc.scalar.activation(SQ[:], C[u][:], ACT.Square).then_inc(sq_ready, 1)

            def root(n, r, u, scale, eps):
                act.wait_ge(norm_ready, n + 1)
                act.wait_ge(y_out[u], 16 * (r + 1))
                nc.scalar.activation(pieces(S[u][:]), banks(u), ACT.Sqrt, bias=eps[:], scale=scale).then_inc(root_ready, 1)
                act.wait_ge(root_ready, n + 1)
                act.sem_inc(mm_free, 1)

            take(0, 0)
            silu_square(0, 0)
            for first, last, scale, eps in ((BLK_Q, BLK_K, float(HD), epsq), (BLK_K, BLK_V, 1.0, epsk)):
                with act.Fori(first // 2, last // 2 - 1) as r:
                    take(2 * r + 1, 1)
                    root(2 * r, r, 0, scale, eps)
                    silu_square(2 * r + 1, 1)
                    take(2 * r + 2, 0)
                    root(2 * r + 1, r, 1, scale, eps)
                    silu_square(2 * r + 2, 0)
                take(last - 1, 1)
                root(last - 2, last // 2 - 1, 0, scale, eps)
                silu_square(last - 1, 1)
                take(last, 0)
                root(last - 1, last // 2 - 1, 1, scale, eps)
                if last < BLK_V:
                    silu_square(last, 0)

            def rest(kind, n, r, u, taken=False):
                if kind == "v":
                    if not taken:
                        take(n, u)
                    act.wait_ge(y_ready, n + 1)
                    act.sem_inc(mm_free, 1)
                    act.wait_ge(c_ready, n + 3)
                    act.wait_ge(y_out[u], 16 * (r + 1))
                    nc.scalar.activation(S[u][:], C[u][:], ACT.Silu).then_inc(s_ready[u], 1)
                    return
                act.wait_ge(mm_ready, n + 3)
                act.wait_ge(y_out[u], 16 * (r + 1))
                if kind == "z":
                    nc.scalar.activation(pieces(C[u][:]), banks(u), ACT.Silu).then_inc(silu_ready, 1)
                    act.wait_ge(silu_ready, n + 1 - HEADS)
                    act.sem_inc(mm_free, 1)
                    nc.scalar.mul(S[u][:], C[u][:], onorm[:]).then_inc(s_ready[u], 1)
                else:
                    func = ACT.Sigmoid if kind == "gate" else ACT.Copy
                    nc.scalar.activation(pieces(S[u][:]), banks(u), func).then_inc(s_ready[u], 1)
                    act.wait_ge(s_ready[u], r + 1)
                    act.sem_inc(mm_free, 1)
            rest("v", BLK_V, BLK_V // 2, 0, taken=True)
            rest("v", BLK_V + 1, BLK_V // 2, 1)
            for kind, first, count in (("v", BLK_V + 2, HEADS - 2), ("z", BLK_Z, HEADS), ("gate", BLK_GATE, 2 * DB), ("pool", BLK_POOL, POOL_GROUPS)):
                with act.Fori(first // 2, (first + count) // 2) as r:
                    for u in range(2):
                        rest(kind, 2 * r + u, r, u)
            nc.scalar.copy(wbah[:], wba[:]).then_inc(ba_sem["ba_split"], 1)
            act.wait_ge(ba_sem["ba_mm"], 1)
            nc.scalar.copy(pieces(ba[:]), M[0][0:16, :, 0:PIECE]).then_inc(ba_sem["ba_rows"], 1)
            act.wait_ge(ba_sem["ba_copy"], 1)
            nc.scalar.activation(beta[:], bat[:, :, 0:8], ACT.Exp, scale=-1.0).then_inc(ba_sem["ba_act"], 1)
            act.wait_ge(ba_sem["ba_dve"], 1)
            nc.scalar.activation(gate[:], ea[:], ACT.Abs).then_inc(ba_sem["ba_act"], 1)
            act.wait_ge(ba_sem["ba_act"], 2)
            nc.scalar.activation(gate[:], gate[:], ACT.Exp, scale=-1.0).then_inc(ba_sem["ba_act"], 1)
            nc.scalar.activation(aexp[:], aexp[:], ACT.Exp).then_inc(ba_sem["ba_act"], 1)
            act.wait_ge(ba_sem["ba_act"], 4)
            nc.scalar.activation(gate[:], gate[:], ACT.Ln, bias=1.0).then_inc(ba_sem["ba_act"], 1)

        @block.vector
        def _(dve):
            ch = Chain(dve, own)
            dve.sem_inc(c_ready, 2)
            for u in range(2):
                dve.sem_inc(y_out[u], 16)
            dve.wait_ge(consts_in, 80)

            def convolve(n, r, u):
                tap = lambda j: taps[:, bass.ds(n, 1), j:j + 1].rearrange("p a b -> p (a b)")
                dve.wait_ge(y_ready, n + 1)
                dve.wait_ge(y_out[u], 16 * (r + 1))
                ch.step(nc.vector.tensor_scalar(C[u][:], Y[u][:, 0:T], tap(0), None, ALU.mult))
                for j in range(1, TAPS):
                    ins = nc.vector.scalar_tensor_tensor(out=C[u][:], in0=Y[u][:, j:j + T], scalar=tap(j), in1=C[u][:], op0=ALU.mult, op1=ALU.add)
                    if j < TAPS - 1:
                        ch.step(ins)
                ins.then_inc(c_ready, 1)
                ch.restart()

            def normalise(n, u):
                dve.wait_ge(root_ready, n + 1)
                ch.step(nc.vector.reciprocal(S[u][:], S[u][:]))
                nc.vector.tensor_tensor(S[u][:], S[u][:], C[u][:], ALU.mult).then_inc(s_ready[u], 1)
                ch.restart()

            convolve(0, 0, 0)
            with dve.Fori(0, BLK_V // 2 - 1) as r:
                convolve(2 * r + 1, r, 1)
                normalise(2 * r, 0)
                convolve(2 * r + 2, r + 1, 0)
                normalise(2 * r + 1, 1)
            convolve(BLK_V - 1, BLK_V // 2 - 1, 1)
            normalise(BLK_V - 2, 0)
            convolve(BLK_V, BLK_V // 2, 0)
            normalise(BLK_V - 1, 1)
            convolve(BLK_V + 1, BLK_V // 2, 1)
            with dve.Fori(BLK_V // 2 + 1, BLK_Z // 2) as r:
                for u in range(2):
                    convolve(2 * r + u, r, u)
            dve.wait_ge(ba_sem["ba_split"], 1)
            nc.vector.tensor_tensor(wbal[:], wba[:], wbah[:].bitcast(F32), ALU.subtract).then_inc(ba_sem["ba_split"], 1)
            dve.wait_ge(ba_sem["ba_t"], 1)
            ch.step(nc.vector.memset(bat[:, XT, :], 0.0))
            nc.vector.tensor_copy(bat[0:N_META, XT, :], M[1][0:N_META, 0, XT * 16:(XT + 1) * 16])
            nc.vector.tensor_copy(bat[:, 0:XT, :], M[1][:, 0, 0:XT * 16].rearrange("p (t c) -> p t c", c=16)).then_inc(ba_sem["ba_copy"], 1)
            dve.wait_ge(ba_sem["ba_copy"], 1)
            nc.vector.tensor_tensor(ea[:], bat[:, :, 8:16], dtb[:].unsqueeze(1).to_broadcast([P, XT + 1, 8]), ALU.add).then_inc(ba_sem["ba_dve"], 1)
            dve.wait_ge(ba_sem["ba_act"], 5)
            ch.step(nc.vector.tensor_scalar(ea[:], ea[:], 0.0, None, ALU.max))
            ch.step(nc.vector.tensor_tensor(gate[:], gate[:], ea[:], ALU.add))
            ch.step(nc.vector.tensor_scalar(aexp[:], aexp[:], -1.0, None, ALU.mult))
            nc.vector.tensor_tensor(gate[:], gate[:], aexp[:].unsqueeze(1).to_broadcast([P, XT + 1, 8]), ALU.mult).then_inc(ba_sem["ba_dve"], 2)
            ch.step(nc.vector.tensor_scalar(beta[:], beta[:], 1.0, None, ALU.add))
            nc.vector.reciprocal(beta[:], beta[:]).then_inc(ba_sem["ba_dve"], 2)


def delta_phase(nc, k, io):
    CH = CHUNK
    with Phase(nc, "delta") as ph:
        W = PAIRS * P
        pair3 = lambda ap: ap.rearrange("p (m e) -> p m e", m=PAIRS)

        def two(name, shape=(P, W)):
            return [ph.sb(f"{name}{u}", list(shape)) for u in range(2)]

        KT, QT, VT = (two(n, (P, HEADS, CH)) for n in ("kT", "qT", "vT"))
        BG = two("bg", (P, 16))
        GP, BP = two("g_pair", (P, PAIRS)), two("beta_pair", (P, PAIRS))
        KR, VR = two("k_rows"), two("v_rows")
        R, E1, E2, ECB = two("r"), two("e1"), two("e2"), two("ecb")
        CUM = two("cum", (P, 2 * PAIRS))
        EC, KS, BE = two("exp_cum", (P, PAIRS)), two("k_scale", (P, PAIRS)), two("beta_exp", (P, PAIRS))
        A, AT_T, QD = two("a"), two("attn_t"), two("q_dec")
        KBE, KD, VB = two("kbe"), two("k_dec"), two("vb")
        Dm, DT, M32, M64, Z = two("d"), two("dT"), two("m32"), two("m64"), two("z")
        PW, PWT = two("pw"), two("pwT")
        U, WT, VN, O = two("u"), two("wT"), two("vn"), two("o")
        S = ph.sb("state", [P, HEADS, HD])
        BANK = ph.ps("bank", [P, 8, 512])
        X = lambda u, j: BANK[:, 3 * u + j, :]
        WS = BANK[:, 6, :]

        loaded, o_out = ph.sems("loaded"), ph.sems("o_out")
        own = ph.sem("dve_own")

        signals = {n: ph.sems(n) for n in ("gates_in", "r_ready", "kv_rows", "k_copied", "v_copied", "decay_raw", "cum_ready", "diff_ready", "exp_ready",
                  "grams", "masked1", "a_ready", "attn_ready", "qd_ready", "rows_scaled", "at_raw", "d_ready",
                  "sq1", "p2", "p2t", "sq2", "z2", "p4", "p4t", "sq3", "z4", "p8", "sq4", "z8",
                  "lv1", "x1", "t1", "lv1b", "z32", "lv2", "x2", "t2", "lv2b", "z64", "uw_raw", "u_ready", "w_ready",
                  "ws_raw", "vn_ready", "out_raw", "o_ready", "upd_raw", "state_done")}
        zeroed = ph.sem("zeroed")
        block = ph.block()

        def chunks(eng, body):
            body(0, {1: 1}, (1,))
            with eng.Fori(0, (N_CHUNKS - 1) // 2) as r:
                body(2 * r + 1, {0: r + 1, 1: r + 2}, (0, 1))

        @block.sync
        def _(sp):
            sp.wait_ge(zeroed, 5)
            for dst, first in ((KT, BLK_K), (QT, BLK_Q), (VT, BLK_V)):
                sp.dma_start(dst[1][:, :, PAD:CH], io["proj"][first:first + HEADS, :, 0:N_META].rearrange("h p t -> p h t")).then_inc(loaded[1], 16)
            for half in range(2):
                sp.dma_start(BG[1][half * CH + PAD:(half + 1) * CH, :], io["bg"][0:N_META, :]).then_inc(loaded[1], 16)
            with sp.Fori(0, (N_CHUNKS - 1) // 2) as r:
                for u, n in ((0, r + 1), (1, r + 2)):
                    t0 = (2 * r + u) * CH + N_META
                    sp.wait_ge(signals["state_done"][u], n)
                    for dst, first in ((KT, BLK_K), (QT, BLK_Q), (VT, BLK_V)):
                        sp.dma_start(dst[u][:], io["proj"][first:first + HEADS, :, bass.ds(t0, CH)].rearrange("h p t -> p h t")).then_inc(loaded[u], 16)
                    for half in range(2):
                        sp.dma_start(BG[u][half * CH:(half + 1) * CH, :], io["bg"][bass.ds(t0, CH), :]).then_inc(loaded[u], 16)

        @block.gpsimd
        def _(pool):
            pool.memset(S[:], 0.0).then_inc(zeroed, 1)
            for t in (KT[1], QT[1], VT[1], BG[1]):
                pool.memset(t[:], 0.0).then_inc(zeroed, 1)
            mul = lambda out, a, b: nc.gpsimd.tensor_tensor(out, a, b, ALU.mult)

            def body(c, n, slots):
                for u in slots:
                    pool.wait_ge(signals["gates_in"][u], n[u])
                    mul(pair3(R[u][:]), k["upper"][:].unsqueeze(1).to_broadcast([P, PAIRS, P]),
                        GP[u][:].unsqueeze(2).to_broadcast([P, PAIRS, P])).then_inc(signals["r_ready"][u], 1)
                for u in slots:
                    pool.wait_ge(signals["exp_ready"][u], n[u])
                    mul(pair3(E1[u][:]), pair3(E1[u][:]), k["upper"][:].unsqueeze(1).to_broadcast([P, PAIRS, P])).then_inc(signals["masked1"][u], 1)
                    mul(BE[u][:], BP[u][:], EC[u][:]).then_inc(signals["qd_ready"][u], 1)
                    mul(QD[u][:], QT[u][:].rearrange("p h t -> p (h t)"), ECB[u][:]).then_inc(signals["qd_ready"][u], 1)
                    wide = lambda s: s[:].unsqueeze(2).to_broadcast([P, PAIRS, P])
                    pool.wait_ge(signals["v_copied"][u], n[u])
                    mul(pair3(VB[u][:]), pair3(VR[u][:]), wide(BP[u])).then_inc(signals["rows_scaled"][u], 1)
                    mul(pair3(KD[u][:]), pair3(KR[u][:]), wide(KS[u])).then_inc(signals["rows_scaled"][u], 1)
                    pool.wait_ge(signals["qd_ready"][u], 2 * n[u])
                    mul(pair3(KBE[u][:]), pair3(KR[u][:]), wide(BE[u])).then_inc(signals["rows_scaled"][u], 1)
            chunks(pool, body)

        @block.tensor
        def _(pe):
            def pairs(fn, out, a, b=None, lo=True):
                for m in range(PAIRS):
                    cs = slice(m * P, (m + 1) * P)
                    if b is None:
                        last = nc.tensor.transpose(out[:, cs], a[:, cs], k["ident"][:])
                    else:
                        last = nc.tensor.matmul(out[:, cs], a[:, cs], b[:, cs], start=True, stop=True)
                return last

            def body(c, n, slots):
                on = lambda name, u: pe.wait_ge(signals[name][u], n[u])
                flat = lambda t: t[:].rearrange("p h t -> p (h t)")
                for u in slots:
                    pe.wait_ge(loaded[u], 80 * n[u])
                    pe.wait_ge(signals["state_done"][u], n[u])
                    pairs(None, X(u, 0), flat(KT[u]))
                    pairs(None, X(u, 1), flat(VT[u])).then_inc(signals["kv_rows"][u], 1)
                for u in slots:
                    on("r_ready", u)
                    nc.tensor.matmul(X(u, 2), k["ones"][:], R[u][:], start=True, stop=True)
                    on("k_copied", u)
                    nc.tensor.matmul(X(u, 0)[:, 0:PAIRS], k["upper"][:], GP[u][:], start=True, stop=True)
                    nc.tensor.matmul(X(u, 0)[:, PAIRS:2 * PAIRS], k["same_head"][:], GP[u][:], start=True, stop=True).then_inc(signals["decay_raw"][u], 1)
                for u in slots:
                    on("cum_ready", u)
                    on("v_copied", u)
                    pairs(None, X(u, 0), flat(KT[u]), flat(KT[u]))
                    pairs(None, X(u, 1), flat(KT[u]), flat(QT[u])).then_inc(signals["grams"][u], 1)
                for u in slots:
                    on("a_ready", u)
                    pairs(None, X(u, 2), A[u]).then_inc(signals["at_raw"][u], 1)
                for u in slots:
                    on("d_ready", u)
                    on("attn_ready", u)
                    pairs(None, X(u, 0), DT[u], Dm[u])
                    pairs(None, X(u, 1), Dm[u], DT[u]).then_inc(signals["sq1"][u], 1)
                for u in slots:
                    on("p2", u)
                    on("p2t", u)
                    pairs(None, X(u, 2), PW[u], Z[u])
                    pairs(None, X(u, 0), PWT[u], PW[u])
                    pairs(None, X(u, 1), PW[u], PWT[u]).then_inc(signals["sq2"][u], 1)
                for u in slots:
                    on("p4", u)
                    on("p4t", u)
                    on("z2", u)
                    pairs(None, X(u, 2), PW[u], Z[u])
                    pairs(None, X(u, 0), PWT[u], PW[u]).then_inc(signals["sq3"][u], 1)
                for u in slots:
                    on("p8", u)
                    on("z4", u)
                    pairs(None, X(u, 2), PW[u], Z[u]).then_inc(signals["sq4"][u], 1)
                for before, M, products, xs, ts, joined in (("z8", M32, "lv1", "x1", "t1", "lv1b"), ("z32", M64, "lv2", "x2", "t2", "lv2b")):
                    for u in slots:
                        on(before, u)
                        pairs(None, X(u, 0), Z[u])
                        pairs(None, X(u, 1), M[u], Z[u]).then_inc(signals[products][u], 1)
                    for u in slots:
                        on(xs, u)
                        on(ts, u)
                        pairs(None, X(u, 2), PW[u], PWT[u]).then_inc(signals[joined][u], 1)
                for u in slots:
                    on("z64", u)
                    pe.wait_ge(signals["rows_scaled"][u], 3 * n[u])
                    pairs(None, X(u, 0), Z[u], VB[u])
                    pairs(None, X(u, 1), KBE[u], Z[u]).then_inc(signals["uw_raw"][u], 1)
                for u in slots:
                    on("w_ready", u)
                    pe.wait_ge(signals["state_done"][1 - u], n[u] + (u == 0))
                    for h in range(HEADS):
                        m, half = h // 2, h % 2
                        last = nc.tensor.matmul(WS[half * CH:(half + 1) * CH, m * P:(m + 1) * P], WT[u][:, h * CH:(h + 1) * CH],
                                                S[:, h, :], start=True, stop=True)
                    last.then_inc(signals["ws_raw"][u], 1)
                    pe.wait_ge(signals["qd_ready"][u], 2 * n[u])
                    for m in range(PAIRS):
                        cs = slice(m * P, (m + 1) * P)
                        for half in range(2):
                            h = 2 * m + half
                            nc.tensor.matmul(X(u, 2)[half * CH:(half + 1) * CH, cs], QD[u][:, h * CH:(h + 1) * CH], S[:, h, :],
                                             start=True, stop=False, skip_group_check=True)
                        if m == 0:
                            on("vn_ready", u)
                        last = nc.tensor.matmul(X(u, 2)[:, cs], AT_T[u][:, cs], VN[u][:, cs], start=False, stop=True, skip_group_check=True)
                    last.then_inc(signals["out_raw"][u], 1)
                    for h in range(HEADS):
                        m, rows = h // 2, slice((h % 2) * CH, (h % 2 + 1) * CH)
                        last = nc.tensor.matmul(X(u, h % 2)[:, m * P:(m + 1) * P], KD[u][rows, m * P:(m + 1) * P],
                                                VN[u][rows, m * P:(m + 1) * P], start=True, stop=True)
                    last.then_inc(signals["upd_raw"][u], 1)
            chunks(pe, body)

        @block.scalar
        def _(act):
            def body(c, n, slots):
                on = lambda name, u: act.wait_ge(signals[name][u], n[u])
                for u in slots:
                    on("kv_rows", u)
                    nc.scalar.copy(KR[u][:], X(u, 0)).then_inc(signals["k_copied"][u], 1)
                    nc.scalar.copy(VR[u][:], X(u, 1)).then_inc(signals["v_copied"][u], 1)
                for u in slots:
                    on("diff_ready", u)
                    nc.scalar.activation(ECB[u][:], X(u, 2), ACT.Exp)
                    nc.scalar.activation(E1[u][:], E1[u][:], ACT.Exp)
                    nc.scalar.activation(E2[u][:], E2[u][:], ACT.Exp, scale=-1.0)
                    nc.scalar.activation(EC[u][:], CUM[u][:, 0:PAIRS], ACT.Exp)
                    nc.scalar.activation(KS[u][:], KS[u][:], ACT.Exp).then_inc(signals["exp_ready"][u], 1)
                for src, done in (("sq1", "p2"), ("sq2", "p4"), ("sq3", "p8")):
                    for u in slots:
                        on(src, u)
                        nc.scalar.copy(PW[u][:], X(u, 0)).then_inc(signals[done][u], 1)
                for src, done in (("lv1", "x1"), ("lv2", "x2")):
                    for u in slots:
                        on(src, u)
                        nc.scalar.copy(PW[u][:], X(u, 0)).then_inc(signals[done][u], 1)
                for u in slots:
                    on("uw_raw", u)
                    nc.scalar.copy(WT[u][:], X(u, 1)).then_inc(signals["w_ready"][u], 1)
                for u in slots:
                    on("out_raw", u)
                    if slots == (0, 1):
                        act.wait_ge(o_out[u], 16 * n[0])
                    nc.scalar.copy(O[u][:], X(u, 2)).then_inc(signals["o_ready"][u], 1)
                    if slots == (0, 1):
                        on("o_ready", u)
                        act.dma_start(io["o_rows"][bass.ds(c + u - 1, 1)].rearrange("a p e -> (a p) e"), O[u][:]).then_inc(o_out[u], 16)
            for u in range(2):
                act.sem_inc(o_out[u], 16)
            chunks(act, body)
            for u in range(2):
                act.wait_ge(o_out[u], 16 * ((N_CHUNKS - 1) // 2 + 1))

        @block.vector
        def _(dve):
            ch = Chain(dve, own)
            tt = nc.vector.tensor_tensor
            for u in range(2):
                dve.sem_inc(signals["state_done"][u], 1)
            dve.wait_ge(zeroed, 5)

            def body(c, n, slots):
                on = lambda name, u: dve.wait_ge(signals[name][u], n[u])
                over_pairs = lambda m: m[:].unsqueeze(1).to_broadcast([P, PAIRS, P])
                wide = lambda s: s.unsqueeze(2).to_broadcast([P, PAIRS, P])
                for u in slots:
                    dve.wait_ge(loaded[u], 80 * n[u])
                    for half in range(2):
                        rows = slice(half * CH, (half + 1) * CH)
                        of_pair = lambda c0: BG[u][rows, c0:c0 + 8].rearrange("p (m e) -> p e m", e=2)[:, half, :]
                        nc.vector.tensor_copy(BP[u][rows, :], of_pair(0))
                        last = nc.vector.tensor_copy(GP[u][rows, :], of_pair(8))
                    last.then_inc(signals["gates_in"][u], 1)
                for u in slots:
                    on("decay_raw", u)
                    nc.vector.tensor_copy(CUM[u][:], X(u, 0)[:, 0:2 * PAIRS]).then_inc(signals["cum_ready"][u], 1)
                    on("cum_ready", u)
                    cum, whole = CUM[u][:, 0:PAIRS], CUM[u][:, PAIRS:]
                    tt(KS[u][:], whole, cum, ALU.subtract)
                    ch.step(tt(pair3(E2[u][:]), pair3(X(u, 2)), wide(cum), ALU.subtract))
                    nc.vector.tensor_scalar(E1[u][:], E2[u][:], 0.0, None, ALU.min)
                    nc.vector.tensor_scalar(E2[u][:], E2[u][:], 0.0, None, ALU.max).then_inc(signals["diff_ready"][u], 1)
                for u in slots:
                    on("exp_ready", u)
                    ch.step(tt(pair3(E2[u][:]), pair3(E2[u][:]), over_pairs(k["lower"]), ALU.mult))
                    ch.step(tt(pair3(E2[u][:]), pair3(E2[u][:]), wide(BP[u][:]), ALU.mult))
                    on("grams", u)
                    tt(A[u][:], X(u, 0), E2[u][:], ALU.mult).then_inc(signals["a_ready"][u], 1)
                    on("masked1", u)
                    tt(AT_T[u][:], X(u, 1), E1[u][:], ALU.mult).then_inc(signals["attn_ready"][u], 1)
                    on("a_ready", u)
                    tt(pair3(Dm[u][:]), pair3(A[u][:]), over_pairs(k["in16"]), ALU.mult)
                    ch.step(tt(pair3(M32[u][:]), pair3(A[u][:]), over_pairs(k["in32"]), ALU.mult))
                    tt(M64[u][:], A[u][:], M32[u][:], ALU.subtract)
                    ch.step(tt(M32[u][:], M32[u][:], Dm[u][:], ALU.subtract))
                for u in slots:
                    on("at_raw", u)
                    ch.step(tt(pair3(DT[u][:]), pair3(X(u, 2)), over_pairs(k["in16"]), ALU.mult))
                    tt(pair3(Z[u][:]), over_pairs(k["ident"]), pair3(DT[u][:]), ALU.subtract).then_inc(signals["d_ready"][u], 1)
                for u in slots:
                    on("sq1", u)
                    nc.vector.tensor_copy(PWT[u][:], X(u, 1)).then_inc(signals["p2t"][u], 1)
                for u in slots:
                    on("sq2", u)
                    nc.vector.tensor_copy(PWT[u][:], X(u, 1)).then_inc(signals["p4t"][u], 1)
                    tt(Z[u][:], X(u, 2), Z[u][:], ALU.add).then_inc(signals["z2"][u], 1)
                for src, done in (("sq3", "z4"), ("sq4", "z8")):
                    for u in slots:
                        on(src, u)
                        tt(Z[u][:], X(u, 2), Z[u][:], ALU.add).then_inc(signals[done][u], 1)
                for products, ts, joined, done in (("lv1", "t1", "lv1b", "z32"), ("lv2", "t2", "lv2b", "z64")):
                    for u in slots:
                        on(products, u)
                        nc.vector.tensor_copy(PWT[u][:], X(u, 1)).then_inc(signals[ts][u], 1)
                    for u in slots:
                        on(joined, u)
                        tt(Z[u][:], Z[u][:], X(u, 2), ALU.subtract).then_inc(signals[done][u], 1)
                for u in slots:
                    on("uw_raw", u)
                    nc.vector.tensor_copy(U[u][:], X(u, 0)).then_inc(signals["u_ready"][u], 1)
                for u in slots:
                    on("ws_raw", u)
                    on("u_ready", u)
                    tt(VN[u][:], U[u][:], WS, ALU.subtract).then_inc(signals["vn_ready"][u], 1)
                    on("upd_raw", u)
                    whole = ECB[u][:].rearrange("p (h t) -> p h t", t=CH)[:, :, CH - 1:CH].to_broadcast([P, HEADS, HD])
                    ch.step(tt(S[:], S[:], whole, ALU.mult))
                    on("o_ready", u)
                    by_half = S[:].rearrange("p (m b) e -> p b m e", b=2)
                    tt(by_half, by_half, BANK[:, 3 * u:3 * u + 2, :].rearrange("p b (m e) -> p b m e", e=HD), ALU.add).then_inc(signals["state_done"][u], 1)
                ch.restart()
            chunks(dve, body)


def split_on_pool(nc, pool, raw, hi, lo, hi_ready, count, lo_ready, passed=None):
    if passed is not None:
        pool.sem_inc(passed, 1)
    nc.gpsimd.tensor_copy(hi, raw).then_inc(hi_ready, 1)
    pool.wait_ge(hi_ready, count)
    return nc.gpsimd.tensor_tensor(lo, raw, hi.bitcast(F32), ALU.subtract).then_inc(lo_ready, 1)


def branch_phase(nc, k, io):
    NG, NC = POOL_GROUPS, SEQ // CHUNK
    LEAD = max(POOL_WINDOWS)
    HALVES = SEQ // 512
    with Phase(nc, "branch") as ph:
        oT = [ph.sb(f"oT_{p}", [P, HEADS, SEQ], F32R) for p in ("hi", "lo")]
        yp = [ph.sb(f"yp_{p}", [P, NG, SEQ], F32R) for p in ("hi", "lo")]
        with ExitStack() as first_scope:
            ph1 = Phase(nc, "brin")
            first_scope.enter_context(ph1)
            XP = [ph1.sb(f"xp{u}", [P, LEAD + T]) for u in range(2)]
            SA, SB = ph1.sb("sa", [P, LEAD + T]), ph1.sb("sb", [P, LEAD + T])
            PL = ph1.sb("pooled", [P, SEQ])
            PLs = [ph1.sb(f"pooled_{p}", [P, SEQ], F32R) for p in ("hi", "lo")]
            PWr = ph1.sb("pool_w", [P, NG, P])
            PWs = [ph1.sb(f"pool_w_{p}", [P, NG, P], F32R) for p in ("hi", "lo")]
            scale = ph1.sb("pool_scale", [P, NG])
            YP = ph1.sb("yp", [P, SEQ])
            OR = [ph1.sb(f"or{u}", [P, PAIRS * HD]) for u in range(2)]
            ON = [ph1.sb(f"on{u}", [P, PAIRS * HD]) for u in range(2)]
            ZC = [ph1.sb(f"zc{u}", [P, HEADS, CHUNK]) for u in range(2)]
            OZ = [ph1.sb(f"oz{u}", [P, HEADS, CHUNK]) for u in range(2)]
            SQ = ph1.sb("sq", [P, PAIRS * HD])
            ms, root = ph1.sb("ms", [P, PAIRS]), ph1.sb("root", [P, PAIRS])
            MP = ph1.ps("mixed", [P, HALVES, 512])
            TP = [ph1.ps(f"t{u}", [P, PAIRS * P]) for u in range(2)]
            consts_in, pads = ph1.sem("consts_in"), ph1.sem("pads")
            xp_in, o_in = ph1.sems("xp_in"), ph1.sems("o_in")
            names = ("pooled", "pooled_hi", "pooled_lo", "pw_hi", "pw_lo", "mixed", "yp_ready", "yp_hi", "yp_lo",
                     "squared", "ms_ready", "root_ready", "on_ready", "t_ready", "oz_ready", "o_hi", "o_lo")
            sig = {n: ph1.sem(n) for n in names}
            own = ph1.sem("dve_own")
            block = ph1.block()

            @block.sync
            def _(sp):
                sp.dma_start(PWr[:], io["pool_w"].rearrange("p (g c) -> p g c", g=NG)).then_inc(consts_in, 16)
                sp.dma_start(scale[:], io["pool_scale"]).then_inc(consts_in, 16)
                for g in range(NG):
                    if g >= 2:
                        sp.wait_ge(sig["pooled"], g - 1)
                    sp.dma_start(XP[g % 2][:, LEAD:], io["proj"][BLK_POOL + g]).then_inc(xp_in[g % 2], 16)
                with sp.Fori(0, NC // 2) as r:
                    for u in range(2):
                        n = 2 * r + u
                        sp.wait_ge(sig["oz_ready"], n + 1)
                        sp.dma_start(OR[u][:], io["o_rows"][bass.ds(n, 1)].rearrange("a p e -> (a p) e")).then_inc(o_in[u], 16)
                        sp.dma_start(ZC[u][:], io["proj"][BLK_Z:BLK_Z + HEADS, :, bass.ds(n * CHUNK + N_META, CHUNK)].rearrange("h p t -> p h t")).then_inc(o_in[u], 16)

            @block.gpsimd
            def _(pool):
                for u in range(2):
                    pool.memset(XP[u][:, 0:LEAD], 0.0).then_inc(pads, 1)
                pool.wait_ge(consts_in, 32)
                split_on_pool(nc, pool, PWr[:], PWs[0][:], PWs[1][:], sig["pw_hi"], 1, sig["pw_lo"])

            @block.vector
            def _(dve):
                ch = Chain(dve, own)
                tt = nc.vector.tensor_tensor
                dve.sem_inc(sig["oz_ready"], 2)
                dve.sem_inc(sig["o_lo"], 2)
                dve.wait_ge(pads, 2)
                for g, w in enumerate(POOL_WINDOWS):
                    x = XP[g % 2]
                    dve.wait_ge(xp_in[g % 2], 16 * (g // 2 + 1))
                    src, size = x, 1
                    while size < w:
                        dst = SA if src is not SA else SB
                        first = 2 * size - 1
                        ch.step(tt(dst[:, first:], src[:, first:], src[:, first - size:LEAD + T - size], ALU.add))
                        src, size = dst, 2 * size
                    cols = slice(LEAD + N_META, LEAD + T)
                    if g:
                        dve.wait_ge(sig["pooled_lo"], g)
                    nc.vector.scalar_tensor_tensor(out=PL[:], in0=src[:, cols], scalar=1.0 / w, in1=x[:, cols],
                                                   op0=ALU.mult, op1=ALU.subtract).then_inc(sig["pooled"], 1)
                    dve.wait_ge(sig["pooled_hi"], g + 1)
                    tt(PLs[1][:], PL[:], PLs[0][:].bitcast(F32), ALU.subtract).then_inc(sig["pooled_lo"], 1)
                    dve.wait_ge(sig["yp_hi"], g + 1)
                    tt(yp[1][:, g, :], YP[:], yp[0][:, g, :].bitcast(F32), ALU.subtract).then_inc(sig["yp_lo"], 1)
                ch.restart()
                pairs = lambda t: t[:].rearrange("p (m e) -> p m e", e=HD)
                with dve.Fori(0, NC // 2) as r:
                    for u in range(2):
                        n = 2 * r + u
                        dve.wait_ge(sig["squared"], n + 1)
                        ch.step(nc.vector.tensor_reduce(ms[:], pairs(SQ), AX.X, ALU.add))
                        nc.vector.tensor_scalar(ms[:], ms[:], 1.0 / HD, RMS_EPS, ALU.mult, ALU.add).then_inc(sig["ms_ready"], 1)
                        dve.wait_ge(sig["root_ready"], n + 1)
                        ch.step(nc.vector.reciprocal(root[:], root[:]))
                        dve.wait_ge(sig["oz_ready"], n + 1)
                        tt(pairs(ON[u]), pairs(OR[u]), root[:].unsqueeze(2).to_broadcast([P, PAIRS, HD]), ALU.mult).then_inc(sig["on_ready"], 1)
                        dve.wait_ge(sig["t_ready"], n + 1)
                        dve.wait_ge(sig["o_lo"], n + 1)
                        tt(OZ[u][:].rearrange("p h t -> p (h t)"), TP[u][:], ZC[u][:].rearrange("p h t -> p (h t)"), ALU.mult).then_inc(sig["oz_ready"], 1)
                        dve.wait_ge(sig["o_hi"], n + 1)
                        cols = bass.ds(n * CHUNK, CHUNK)
                        tt(oT[1][:, :, cols], OZ[u][:], oT[0][:, :, cols].bitcast(F32), ALU.subtract).then_inc(sig["o_lo"], 1)
                        ch.restart()

            @block.scalar
            def _(act):
                act.wait_ge(consts_in, 32)
                for g in range(NG):
                    act.wait_ge(sig["pooled"], g + 1)
                    if g:
                        act.wait_ge(sig["mixed"], g)
                    nc.scalar.copy(PLs[0][:], PL[:]).then_inc(sig["pooled_hi"], 1)
                    act.wait_ge(sig["mixed"], g + 1)
                    if g:
                        act.wait_ge(sig["yp_lo"], g)
                    nc.scalar.mul(YP[:].rearrange("p (a b) -> p a b", a=HALVES), MP[:], scale[:, g:g + 1]).then_inc(sig["yp_ready"], 1)
                    act.wait_ge(sig["yp_ready"], g + 1)
                    nc.scalar.copy(yp[0][:, g, :], YP[:]).then_inc(sig["yp_hi"], 1)
                with act.Fori(0, NC // 2) as r:
                    for u in range(2):
                        n = 2 * r + u
                        act.wait_ge(o_in[u], 32 * (r + 1))
                        nc.scalar.activation(SQ[:], OR[u][:], ACT.Square).then_inc(sig["squared"], 1)
                        act.wait_ge(sig["ms_ready"], n + 1)
                        nc.scalar.activation(root[:], ms[:], ACT.Sqrt).then_inc(sig["root_ready"], 1)
                        act.wait_ge(sig["oz_ready"], n + 3)
                        nc.scalar.copy(oT[0][:, :, bass.ds(n * CHUNK, CHUNK)], OZ[u][:]).then_inc(sig["o_hi"], 1)

            @block.tensor
            def _(pe):
                pe.wait_ge(sig["pw_lo"], 1)
                for g in range(NG):
                    pe.wait_ge(sig["pooled_lo"], g + 1)
                    if g:
                        pe.wait_ge(sig["yp_ready"], g)
                    for c in range(HALVES):
                        cs = slice(c * 512, (c + 1) * 512)
                        last = mm3(nc, MP[:, c, :], (PWs[0][:, g, :], PWs[1][:, g, :]), (PLs[0][:, cs], PLs[1][:, cs]))
                    last.then_inc(sig["mixed"], 1)
                with pe.Fori(0, NC // 2) as r:
                    for u in range(2):
                        n = 2 * r + u
                        pe.wait_ge(sig["on_ready"], n + 1)
                        pe.wait_ge(sig["oz_ready"], n + 1)
                        for m in range(PAIRS):
                            last = nc.tensor.transpose(TP[u][:, m * P:(m + 1) * P], ON[u][:, m * P:(m + 1) * P], k["ident"][:])
                        last.then_inc(sig["t_ready"], 1)

        ph2 = Phase(nc, "brout")
        with ph2:
            NB = HEADS + NG
            Wr = [ph2.sb(f"w{u}", [P, NB, P]) for u in range(2)]
            Ws = [[ph2.sb(f"w{p}{u}", [P, NB, P], F32R) for p in ("hi", "lo")] for u in range(2)]
            GP = [ph2.sb(f"gp{u}", [P, SEQ]) for u in range(2)]
            GD = [ph2.sb(f"gd{u}", [P, SEQ]) for u in range(2)]
            YA = [ph2.ps(f"ya{u}", [P, HALVES, 512]) for u in range(2)]
            YB = [ph2.ps(f"yb{u}", [P, HALVES, 512]) for u in range(2)]
            loaded, stored = ph2.sems("loaded"), ph2.sems("stored")
            w_hi, w_lo, passed, products, merged = (ph2.sem(n) for n in ("w_hi", "w_lo", "passed", "products", "merged"))
            own = ph2.sem("dve_own")
            block = ph2.block()

            @block.sync
            def _(sp):
                with sp.Fori(0, DB // 2) as r:
                    for u in range(2):
                        n = 2 * r + u
                        sp.wait_ge(w_lo, n + 1)
                        sp.dma_start(Wr[u][:], io["w_branches"][bass.ds(n, 1)].rearrange("a p (b c) -> (a p) b c", c=P)).then_inc(loaded[u], 16)
                        sp.wait_ge(stored[u], 16 * (r + 1))
                        sp.dma_start(GP[u][:], io["proj"][bass.ds(n + BLK_GATE, 1), :, N_META:T].rearrange("a p t -> (a p) t")).then_inc(loaded[u], 16)
                        sp.dma_start(GD[u][:], io["proj"][bass.ds(n + BLK_GATE + DB, 1), :, N_META:T].rearrange("a p t -> (a p) t")).then_inc(loaded[u], 16)

            @block.gpsimd
            def _(pool):
                pool.sem_inc(w_lo, 2)
                with pool.Fori(0, DB // 2) as r:
                    for u in range(2):
                        n = 2 * r + u
                        pool.wait_ge(loaded[u], 48 * (r + 1))
                        pool.wait_ge(products, n + 1)
                        split_on_pool(nc, pool, Wr[u][:], Ws[u][0][:], Ws[u][1][:], w_hi, n + 1, w_lo, passed)

            @block.tensor
            def _(pe):
                pe.sem_inc(products, 2)
                with pe.Fori(0, DB // 2) as r:
                    for u in range(2):
                        n = 2 * r + u
                        pe.wait_ge(w_lo, n + 3)
                        pe.wait_ge(merged, n + 1)
                        for dst, src, b0, count in ((YA[u], yp, HEADS, NG), (YB[u], oT, 0, HEADS)):
                            for b in range(count):
                                for c in range(HALVES):
                                    cs = slice(c * 512, (c + 1) * 512)
                                    last = mm3(nc, dst[:, c, :], (Ws[u][0][:, b0 + b, :], Ws[u][1][:, b0 + b, :]),
                                               (src[0][:, b, cs], src[1][:, b, cs]), b == 0, b == count - 1)
                        last.then_inc(products, 1)

            @block.vector
            def _(dve):
                ch = Chain(dve, own)
                dve.sem_inc(merged, 2)
                with dve.Fori(0, DB // 2) as r:
                    for u in range(2):
                        n = 2 * r + u
                        halves = lambda t: t[:].rearrange("p (a b) -> p a b", a=HALVES)
                        dve.wait_ge(loaded[u], 48 * (r + 1))
                        dve.wait_ge(products, n + 3)
                        ch.mark(nc.vector.tensor_tensor(halves(GP[u]), YA[u][:], halves(GP[u]), ALU.mult))
                        ch.step(nc.vector.tensor_tensor(halves(GD[u]), YB[u][:], halves(GD[u]), ALU.mult))
                        nc.vector.tensor_tensor(GP[u][:], GP[u][:], GD[u][:], ALU.add).then_inc(merged, 1)
                        ch.restart()

            @block.scalar
            def _(act):
                for u in range(2):
                    act.sem_inc(stored[u], 16)
                with act.Fori(0, DB // 2) as r:
                    for u in range(2):
                        n = 2 * r + u
                        act.wait_ge(merged, n + 3)
                        act.dma_start(io["merged"][bass.ds(n, 1)].rearrange("a p t -> (a p) t"), GP[u][:]).then_inc(stored[u], 16)
                for u in range(2):
                    act.wait_ge(stored[u], 16 * (DB // 2 + 1))


def mix_phase(nc, k, io):
    NH = D // 512
    with Phase(nc, "mix") as ph:
        Wr = [ph.sb(f"w{u}", [P, D]) for u in range(2)]
        Ws = [ph.sb(f"w_{p}", [P, DB, D], F32R) for p in ("hi", "lo")]
        gain, bias = ph.sb("gain", [P, D]), ph.sb("bias", [P, D])
        MR = [ph.sb(f"m{u}", [P, DB, P]) for u in range(2)]
        MS = [[ph.sb(f"m{p}{u}", [P, DB, P], F32R) for p in ("hi", "lo")] for u in range(2)]
        HR = [ph.sb(f"h{u}", [P, D]) for u in range(2)]
        HT = [ph.sb(f"hT{u}", [P, DB, P]) for u in range(2)]
        stats, mv = ph.sb("stats", [P, NH, 6]), ph.sb("mv", [P, 2])
        std, rstd = ph.sb("std", [P, 1]), ph.sb("rstd", [P, 1])
        MX = [ph.ps(f"mx{u}", [P, NH, 512]) for u in range(2)]
        TP = [ph.ps(f"t{u}", [P, DB, P]) for u in range(2)]
        consts_in = ph.sem("consts_in")
        w_in, m_in, h_in, rows_out, t_out = (ph.sems(n) for n in ("w_in", "m_in", "h_in", "rows_out", "t_out"))
        sig = {n: ph.sem(n) for n in ("w_hi", "w_lo", "m_hi", "m_lo", "passed", "mixed", "summed", "var_ready", "std_ready", "h_ready", "t_ready", "t_copied")}
        own = ph.sem("dve_own")
        block = ph.block()

        def tiles(eng, body):
            with eng.Fori(0, XT // 2) as r:
                for u in range(2):
                    body(2 * r + u, r, u)

        @block.sync
        def _(sp):
            sp.dma_start(gain[:], row_bcast(io["ln1_g"])).then_inc(consts_in, 16)
            sp.dma_start(bias[:], row_bcast(io["ln1_b"])).then_inc(consts_in, 16)
            for b in range(DB):
                if b >= 2:
                    sp.wait_ge(sig["w_lo"], b - 1)
                sp.dma_start(Wr[b % 2][:], io["w_out"][b * P:(b + 1) * P, :]).then_inc(w_in[b % 2], 16)

            def body(n, r, u):
                sp.wait_ge(sig["m_lo"], n + 1)
                sp.dma_start(MR[u][:], io["merged"][:, :, bass.ts(n, P)].rearrange("b p t -> p b t")).then_inc(m_in[u], 16)
                sp.wait_ge(rows_out[u], 16 * (r + 1))
                sp.wait_ge(sig["t_ready"], n + 1)
                sp.dma_start(HR[u][:], io["h_rows"][bass.ts(n, P), :]).then_inc(h_in[u], 16)
            tiles(sp, body)

        @block.gpsimd
        def _(pool):
            pool.sem_inc(sig["m_lo"], 2)
            for b in range(DB):
                pool.wait_ge(w_in[b % 2], 16 * (b // 2 + 1))
                split_on_pool(nc, pool, Wr[b % 2][:], Ws[0][:, b, :], Ws[1][:, b, :], sig["w_hi"], b + 1, sig["w_lo"])

            def body(n, r, u):
                pool.wait_ge(m_in[u], 16 * (r + 1))
                pool.wait_ge(sig["mixed"], n + 1)
                split_on_pool(nc, pool, MR[u][:], MS[u][0][:], MS[u][1][:], sig["m_hi"], n + 1, sig["m_lo"], sig["passed"])
            tiles(pool, body)

        @block.tensor
        def _(pe):
            pe.sem_inc(sig["mixed"], 2)
            pe.sem_inc(sig["t_ready"], 2)
            pe.wait_ge(sig["w_lo"], DB)

            def body(n, r, u):
                pe.wait_ge(sig["m_lo"], n + 3)
                pe.wait_ge(sig["summed"], n + 1)
                for c in range(NH):
                    for b in range(DB):
                        last = mm3(nc, MX[u][:, c, :], (MS[u][0][:, b, :], MS[u][1][:, b, :]),
                                   (Ws[0][:, b, c * 512:(c + 1) * 512], Ws[1][:, b, c * 512:(c + 1) * 512]), b == 0, b == DB - 1)
                last.then_inc(sig["mixed"], 1)
                pe.wait_ge(sig["h_ready"], n + 1)
                pe.wait_ge(sig["t_copied"], n + 1)
                for b in range(DB):
                    last = nc.tensor.transpose(TP[u][:, b, :], HR[u][:, b * P:(b + 1) * P], k["ident"][:])
                last.then_inc(sig["t_ready"], 1)
            tiles(pe, body)

        @block.vector
        def _(dve):
            ch = Chain(dve, own)
            dve.sem_inc(sig["summed"], 2)
            dve.wait_ge(consts_in, 32)

            def body(n, r, u):
                h = HR[u][:]
                halves = h.rearrange("p (a b) -> p a b", a=NH)
                dve.wait_ge(h_in[u], 16 * (r + 1))
                dve.wait_ge(sig["mixed"], n + 3)
                nc.vector.scalar_tensor_tensor(out=halves, in0=halves, scalar=ALPHA, in1=MX[u][:], op0=ALU.mult, op1=ALU.add).then_inc(sig["summed"], 1)
                dve.wait_ge(sig["summed"], n + 3)
                for s in range(NH):
                    ch.mark(nc.vector.bn_stats(stats[:, s, :], h[:, s * 512:(s + 1) * 512]))
                ch.wait()
                ch.step(nc.vector.bn_aggr(mv[:], stats[:]))
                nc.vector.tensor_scalar(std[:], mv[:, 1:2], LN_EPS, None, ALU.add).then_inc(sig["var_ready"], 1)
                dve.wait_ge(sig["std_ready"], n + 1)
                ch.step(nc.vector.reciprocal(rstd[:], std[:]))
                ch.step(nc.vector.tensor_scalar(h, h, mv[:, 0:1], rstd[:], ALU.subtract, ALU.mult))
                ch.step(nc.vector.tensor_tensor(h, h, gain[:], ALU.mult))
                nc.vector.tensor_tensor(h, h, bias[:], ALU.add).then_inc(sig["h_ready"], 1)
                ch.restart()
            tiles(dve, body)

        @block.scalar
        def _(act):
            act.sem_inc(sig["t_copied"], 2)
            for u in range(2):
                act.sem_inc(rows_out[u], 16)
                act.sem_inc(t_out[u], 16)

            def body(n, r, u):
                act.wait_ge(sig["var_ready"], n + 1)
                nc.scalar.activation(std[:], std[:], ACT.Sqrt).then_inc(sig["std_ready"], 1)
                act.wait_ge(sig["h_ready"], n + 1)
                act.dma_start(io["h1_rows"][bass.ts(n, P), :], HR[u][:]).then_inc(rows_out[u], 16)
                act.wait_ge(sig["t_ready"], n + 3)
                act.wait_ge(t_out[u], 16 * (r + 1))
                nc.scalar.copy(HT[u][:], TP[u][:]).then_inc(sig["t_copied"], 1)
                act.wait_ge(sig["t_copied"], n + 3)
                act.dma_start(io["h1_t"][:, :, bass.ts(n, P)].rearrange("b p t -> p b t"), HT[u][:]).then_inc(t_out[u], 16)
            tiles(act, body)
            for u in range(2):
                act.wait_ge(rows_out[u], 16 * (XT // 2 + 1))
                act.wait_ge(t_out[u], 16 * (XT // 2 + 1))


def query_phase(nc, k, io):
    NQ = 2 * HEADS
    HALVES = SEQ // 512
    with Phase(nc, "query") as ph:
        XS = [ph.sb(f"x_{p}", [P, DB, SEQ], F32R) for p in ("hi", "lo")]
        XR = [ph.sb(f"xr{u}", [P, SEQ]) for u in range(2)]
        W = [ph.sb(f"w{u}", [P, DB, P]) for u in range(2)]
        WS = [[ph.sb(f"w{p}{u}", [P, DB, P], F32R) for p in ("hi", "lo")] for u in range(2)]
        KEYS = ph.sb("keys", [P, NQ, P])
        QT = [ph.sb(f"q{u}", [P, SEQ]) for u in range(2)]
        SC = [ph.sb(f"s{u}", [P, XT, P]) for u in range(2)]
        QP = [ph.ps(f"qp{u}", [P, HALVES, 512]) for u in range(2)]
        SP_ = [ph.ps(f"sp{u}", [P, XT, P]) for u in range(2)]
        keys_in = ph.sem("keys_in")
        x_in, w_in, s_out = ph.sems("x_in"), ph.sems("w_in"), ph.sems("s_out")
        sig = {n: ph.sem(n) for n in ("x_hi", "x_lo", "w_hi", "w_lo", "passed", "q_raw", "q_ready", "s_raw", "s_ready")}
        block = ph.block()

        @block.sync
        def _(sp):
            for b in range(DB):
                if b >= 2:
                    sp.wait_ge(sig["x_lo"], b - 1)
                sp.dma_start(XR[b % 2][:], io["h1_t"][b]).then_inc(x_in[b % 2], 16)
            sp.dma_start(KEYS[:], io["keys"].rearrange("n c e -> c n e")).then_inc(keys_in, 16)
            with sp.Fori(0, NQ // 2) as r:
                for u in range(2):
                    sp.wait_ge(sig["w_lo"], 2 * r + u + 1)
                    sp.dma_start(W[u][:], io["wq_blocks"][bass.ds(2 * r + u, 1)].rearrange("a p (b c) -> (a p) b c", c=P)).then_inc(w_in[u], 16)

        @block.gpsimd
        def _(pool):
            pool.sem_inc(sig["w_lo"], 2)
            with pool.Fori(0, NQ // 2) as r:
                for u in range(2):
                    n = 2 * r + u
                    pool.wait_ge(w_in[u], 16 * (r + 1))
                    pool.wait_ge(sig["q_raw"], n + 1)
                    split_on_pool(nc, pool, W[u][:], WS[u][0][:], WS[u][1][:], sig["w_hi"], n + 1, sig["w_lo"], sig["passed"])

        @block.tensor
        def _(pe):
            pe.sem_inc(sig["q_raw"], 2)
            pe.wait_ge(sig["x_lo"], DB)
            pe.wait_ge(keys_in, 16)

            def queries(n, u):
                pe.wait_ge(sig["w_lo"], n + 3)
                pe.wait_ge(sig["q_ready"], n + 1)
                for b in range(DB):
                    for c in range(HALVES):
                        cs = slice(c * 512, (c + 1) * 512)
                        last = mm3(nc, QP[u][:, c, :], (WS[u][0][:, b, :], WS[u][1][:, b, :]), (XS[0][:, b, cs], XS[1][:, b, cs]), b == 0, b == DB - 1)
                last.then_inc(sig["q_raw"], 1)

            def scores(n, u):
                pe.wait_ge(sig["q_ready"], n + 3)
                pe.wait_ge(sig["s_ready"], n + 1)
                for t in range(XT):
                    keys = KEYS[:, bass.ds(n, 1), :].rearrange("p a e -> p (a e)")
                    last = nc.tensor.matmul(SP_[u][:, t, :], QT[u][:, t * P:(t + 1) * P], keys, start=True, stop=True)
                last.then_inc(sig["s_raw"], 1)

            queries(0, 0)
            with pe.Fori(0, NQ // 2 - 1) as r:
                queries(2 * r + 1, 1)
                scores(2 * r, 0)
                queries(2 * r + 2, 0)
                scores(2 * r + 1, 1)
            queries(NQ - 1, 1)
            scores(NQ - 2, 0)
            scores(NQ - 1, 1)

        @block.scalar
        def _(act):
            act.sem_inc(sig["q_ready"], 2)
            for b in range(DB):
                act.wait_ge(x_in[b % 2], 16 * (b // 2 + 1))
                nc.scalar.copy(XS[0][:, b, :], XR[b % 2][:]).then_inc(sig["x_hi"], 1)

            def copy(n, u):
                act.wait_ge(sig["q_raw"], n + 3)
                act.wait_ge(sig["s_raw"], n + 1)
                nc.scalar.copy(QT[u][:].rearrange("p (a b) -> p a b", a=HALVES), QP[u][:]).then_inc(sig["q_ready"], 1)

            def store(n, u):
                act.wait_ge(sig["s_ready"], n + 3)
                act.dma_start(io["scores"][:, :, bass.ds(n, 1), :].rearrange("t p a e -> p (t a) e"), SC[u][:]).then_inc(s_out[u], 16)

            copy(0, 0)
            with act.Fori(0, NQ // 2 - 1) as r:
                copy(2 * r + 1, 1)
                store(2 * r, 0)
                copy(2 * r + 2, 0)
                store(2 * r + 1, 1)
            copy(NQ - 1, 1)
            store(NQ - 2, 0)
            store(NQ - 1, 1)
            for u in range(2):
                act.wait_ge(s_out[u], 16 * (NQ // 2 + 1))

        @block.vector
        def _(dve):
            dve.sem_inc(sig["s_raw"], 2)
            dve.sem_inc(sig["s_ready"], 2)
            for b in range(DB):
                dve.wait_ge(sig["x_hi"], b + 1)
                nc.vector.tensor_tensor(XS[1][:, b, :], XR[b % 2][:], XS[0][:, b, :].bitcast(F32), ALU.subtract).then_inc(sig["x_lo"], 1)
            for u in range(2):
                dve.sem_inc(s_out[u], 16)
            with dve.Fori(0, NQ // 2) as r:
                for u in range(2):
                    n = 2 * r + u
                    dve.wait_ge(sig["s_raw"], n + 3)
                    dve.wait_ge(s_out[u], 16 * (r + 1))
                    nc.vector.tensor_copy(SC[u][:], SP_[u][:]).then_inc(sig["s_ready"], 1)


def gates_phase(nc, k, io):
    NQ, K = 2 * HEADS, TOPK
    BF16 = mybir.dt.bfloat16
    PARTS = 3
    GROUP = 8
    ROUNDS = P // GROUP
    with Phase(nc, "gates") as ph:
        SC, S2 = ph.sb("scores", [P, NQ, P]), ph.sb("rest", [P, NQ, P])
        V, I, IF = ph.sb("v", [P, NQ, K]), ph.sb("i", [P, NQ, K], U32), ph.sb("if", [P, NQ, K])
        CA, CB = ph.sb("cand", [P, HEADS, K * K]), ph.sb("cand_rest", [P, HEADS, K * K])
        SO, CI = ph.sb("score", [P, HEADS, K]), ph.sb("ci", [P, HEADS, K], U32)
        AB = [ph.sb(f"{n}_int", [P, HEADS, K], U32) for n in "ab"]
        ABF = [ph.sb(f"{n}_float", [P, HEADS, K]) for n in "ab"]
        EQ = ph.sb("eq", [P, HEADS, K, K])
        SEL = ph.sb("sel", [P, 3, HEADS * K])
        SELT = ph.sb("selT", [P, 3, P])
        RM, SUM = ph.sb("rm", [P, HEADS]), ph.sb("sum", [P, HEADS])
        iota16, iota_i = ph.sb("iota16", [P, K]), ph.sb("iota_i", [P, P], mybir.dt.int32)
        iota = ph.sb("iota", [P, P], BF16)
        GB = ph.sb("gate_bf", [P, PARTS, P], BF16)
        GF = ph.sb("gate_parts", [P, PARTS, P])
        GR = ph.sb("gate_rest", [P, P])
        OH = [ph.sb(f"onehot{u}", [P, GROUP, 1 + PARTS, P], BF16) for u in range(2)]
        GS = ph.sb("g", [P, P, P])
        TP = ph.ps("t", [P, 3, P])
        GP = [ph.ps(f"gp{u}", [P, GROUP, P]) for u in range(2)]
        s_in, g_out = ph.sem("s_in"), ph.sem("g_out")
        sig = {n: ph.sem(n) for n in ("s_read", "exp_in", "exp_ready", "sel_ready", "t_ready", "onehots", "g_raw", "g_copied", "iota_ready", "passed")}
        own = ph.sem("dve_own")
        block = ph.block()

        @block.sync
        def _(sp):
            with sp.Fori(0, XT) as n:
                sp.wait_ge(sig["s_read"], n + 1)
                sp.dma_start(SC[:], io["scores"][bass.ds(n, 1)].rearrange("a p n e -> (a p) n e")).then_inc(s_in, 16)
                sp.wait_ge(sig["g_copied"], ROUNDS * (n + 1) + 2)
                sp.dma_start(io["g"][bass.ds(n, 1)].rearrange("a i j t -> (a i) j t"), GS[:]).then_inc(g_out, 16)
            sp.wait_ge(g_out, 16 * (XT + 1))

        @block.gpsimd
        def _(pool):
            ch = Chain(pool, sig["iota_ready"])
            ch.mark(nc.gpsimd.iota(iota_i[:], pattern=[[1, P]], base=0, channel_multiplier=0))

        @block.vector
        def _(dve):
            ch = Chain(dve, own)
            tt, ts = nc.vector.tensor_tensor, nc.vector.tensor_scalar
            dve.sem_inc(sig["s_read"], 1)
            dve.wait_ge(sig["iota_ready"], 1)
            ch.mark(nc.vector.tensor_copy(iota[:], iota_i[:]))
            ch.step(nc.vector.tensor_copy(iota16[:], iota_i[:, 0:K]))
            ch.restart()

            def top16(src, rest, v, i, count):
                for s in range(count):
                    ch.mark(nc.vector.max(v[:, s, 0:8], src[:, s, :]))
                ch.wait()
                for s in range(count):
                    ch.mark(nc.vector.max_index(i[:, s, 0:8], v[:, s, 0:8], src[:, s, :]))
                    ch.mark(nc.vector.match_replace(rest[:, s, :], v[:, s, 0:8], src[:, s, :], LOWEST))
                ch.wait()
                for s in range(count):
                    ch.mark(nc.vector.max(v[:, s, 8:16], rest[:, s, :]))
                ch.wait()
                for s in range(count):
                    ch.mark(nc.vector.max_index(i[:, s, 8:16], v[:, s, 8:16], rest[:, s, :]))

            with dve.Fori(0, XT) as n:
                dve.wait_ge(s_in, 16 * (n + 1))
                dve.sem_inc(sig["exp_in"], 1)
                top16(SC, S2, V, I, NQ)
                ch.wait()
                dve.sem_inc(sig["s_read"], 1)
                ch.mark(nc.vector.tensor_copy(IF[:], I[:]))
                sides = V[:].rearrange("p (h s) k -> p s h k", s=2)
                grid = CA[:].rearrange("p h (a b) -> p h a b", a=K)
                ch.step(tt(grid, sides[:, 0].unsqueeze(3).to_broadcast([P, HEADS, K, K]),
                           sides[:, 1].unsqueeze(2).to_broadcast([P, HEADS, K, K]), ALU.add))
                top16(CA, CB, SO, CI, HEADS)
                ch.wait()
                ch.mark(ts(AB[0][:], CI[:], 4, None, ALU.logical_shift_right))
                ch.step(ts(AB[1][:], CI[:], K - 1, None, ALU.bitwise_and))
                for s in range(2):
                    ch.mark(nc.vector.tensor_copy(ABF[s][:], AB[s][:]))
                top = SO[:, :, 0:1]
                ch.step(nc.vector.tensor_copy(RM[:], top.rearrange("p h a -> p (h a)")))
                tt(SO[:], SO[:], RM[:].unsqueeze(2).to_broadcast([P, HEADS, K]), ALU.subtract).then_inc(sig["exp_in"], 1)
                found = IF[:].rearrange("p (h s) k -> p s h k", s=2)
                for s in range(2):
                    ch.step(tt(EQ[:], ABF[s][:].unsqueeze(3).to_broadcast([P, HEADS, K, K]),
                               iota16[:].unsqueeze(1).unsqueeze(1).to_broadcast([P, HEADS, K, K]), ALU.is_equal))
                    ch.step(tt(EQ[:], EQ[:], found[:, s].unsqueeze(2).to_broadcast([P, HEADS, K, K]), ALU.mult))
                    ch.step(nc.vector.tensor_reduce(SEL[:, s, :].rearrange("p (h k) -> p h k", k=K), EQ[:], AX.X, ALU.add))
                dve.wait_ge(sig["exp_ready"], n + 1)
                ch.step(nc.vector.tensor_reduce(SUM[:], SO[:], AX.X, ALU.add))
                ch.step(nc.vector.reciprocal(SUM[:], SUM[:]))
                tt(SEL[:, 2, :].rearrange("p (h k) -> p h k", k=K), SO[:], SUM[:].unsqueeze(2).to_broadcast([P, HEADS, K]), ALU.mult).then_inc(sig["sel_ready"], 1)
                dve.wait_ge(sig["t_ready"], n + 1)
                ch.step(nc.vector.tensor_copy(SELT[:], TP[:]))
                left = SELT[:, 2, :]
                for q in range(PARTS):
                    ch.step(nc.vector.tensor_copy(GB[:, q, :], left))
                    ch.step(nc.vector.tensor_copy(GF[:, q, :], GB[:, q, :]))
                    if q < PARTS - 1:
                        ch.step(tt(GR[:], left, GF[:, q, :], ALU.subtract))
                        left = GR[:]
                with dve.Fori(0, ROUNDS // 2) as i:
                    for u in range(2):
                        done = ROUNDS * n + 2 * i + u
                        dve.wait_ge(sig["g_raw"], done + 1)
                        for t in range(GROUP):
                            tok = bass.ds((2 * i + u) * GROUP + t, 1)
                            ts(OH[u][:, t, 0, :], iota[:], SELT[:, 0, tok], None, ALU.is_equal)
                            for q in range(PARTS):
                                last = ts(OH[u][:, t, 1 + q, :], iota[:], SELT[:, 1, tok], GF[:, q, tok], ALU.is_equal, ALU.mult)
                        last.then_inc(sig["onehots"], 1)
                dve.wait_ge(sig["onehots"], ROUNDS * (n + 1))
                dve.sem_inc(sig["passed"], 1)
                ch.restart()

        @block.scalar
        def _(act):
            act.sem_inc(sig["g_copied"], 2)
            act.sem_inc(g_out, 16)
            with act.Fori(0, XT) as n:
                act.wait_ge(sig["exp_in"], 2 * (n + 1))
                nc.scalar.activation(SO[:], SO[:], ACT.Exp).then_inc(sig["exp_ready"], 1)
                act.wait_ge(g_out, 16 * (n + 1))
                with act.Fori(0, ROUNDS // 2) as i:
                    for u in range(2):
                        act.wait_ge(sig["g_raw"], ROUNDS * n + 2 * i + u + 3)
                        nc.scalar.copy(GS[:, :, bass.ds((2 * i + u) * GROUP, GROUP)].rearrange("p j t -> p t j"), GP[u][:]).then_inc(sig["g_copied"], 1)

        @block.tensor
        def _(pe):
            pe.sem_inc(sig["g_raw"], 2)
            with pe.Fori(0, XT) as n:
                pe.wait_ge(sig["sel_ready"], n + 1)
                for s in range(3):
                    last = nc.tensor.transpose(TP[:, s, :], SEL[:, s, :], k["ident"][:])
                last.then_inc(sig["t_ready"], 1)
                with pe.Fori(0, ROUNDS // 2) as i:
                    for u in range(2):
                        done = ROUNDS * n + 2 * i + u
                        pe.wait_ge(sig["onehots"], done + 1)
                        pe.wait_ge(sig["g_copied"], done + 1)
                        for t in range(GROUP):
                            for q in range(PARTS):
                                last = nc.tensor.matmul(GP[u][:, t, :], OH[u][:, t, 0, :], OH[u][:, t, 1 + q, :], start=q == 0, stop=q == PARTS - 1)
                        last.then_inc(sig["g_raw"], 1)


def experts_phase(nc, k, io, half):
    J = 4
    GROUPS = N_KEYS // J
    HT = 512
    NT = HT // P
    NH = D // 512
    COMBOS = NT * NH
    OUT_BANKS = 4
    with Phase(nc, f"experts{half}") as ph:
        XS = [ph.sb(f"x_{p}", [P, DB, HT], F32R) for p in ("hi", "lo")]
        ACC = ph.sb("acc", [P, NT, D])
        UR = [ph.sb(f"u{s}", [P, DB, P]) for s in range(2)]
        VR = [ph.sb(f"v{s}", [P, D]) for s in range(2)]
        GR = [ph.sb(f"g{s}", [P, NT, P]) for s in range(2)]
        US = [[ph.sb(f"u{p}{s}", [P, DB, P], F32R) for p in ("hi", "lo")] for s in range(2)]
        VS = [[ph.sb(f"v{p}{s}", [P, J, D], F32R) for p in ("hi", "lo")] for s in range(2)]
        AS = [[ph.sb(f"a{p}{s}", [P, J, HT], F32R) for p in ("hi", "lo")] for s in range(2)]
        AC = [ph.sb(f"act{s}", [P, HT]) for s in range(2)]
        gain, bias = ph.sb("gain", [P, D]), ph.sb("bias", [P, D])
        stats, mv, std = ph.sb("stats", [P, NH, 6]), ph.sb("mv", [P, 2]), ph.sb("std", [P, 1])
        HID = [ph.ps(f"hid{s}", [P, HT]) for s in range(2)]
        OUT = [ph.ps(f"out{q}", [P, 512]) for q in range(OUT_BANKS)]
        x_in, e_in = ph.sems("x_in"), ph.sems("e_in")
        start_in, out_stored = ph.sem("start_in"), ph.sem("out_stored")
        names = ("x_hi", "x_lo", "acc_ready", "u_hi", "v_hi", "u_lo", "v_lo", "hid", "gelu", "gated", "a_hi", "a_lo",
                 "out", "out_group", "added", "var_ready", "std_ready", "rows_ready")
        sig = {n: ph.sem(n) for n in names}
        own = ph.sem("dve_own")
        block = ph.block()
        tok = slice(half * HT, (half + 1) * HT)

        def groups(eng, body):
            for p in range(2):
                body(p, 0, p, True)
            with eng.Fori(1, GROUPS // 2) as r:
                for p in range(2):
                    body(2 * r + p, r, p, False)

        @block.sync
        def _(sp):
            sp.dma_start(gain[:], row_bcast(io["ln2_g"])).then_inc(start_in, 16)
            sp.dma_start(bias[:], row_bcast(io["ln2_b"])).then_inc(start_in, 16)
            sp.dma_start(ACC[:], io["h1_rows"][tok, :].rearrange("(n p) d -> p n d", p=P)).then_inc(start_in, 16)
            for q in range(DB // 2):
                if q >= 2:
                    sp.wait_ge(sig["x_lo"], q - 1)
                sp.dma_start(UR[q % 2][:].rearrange("p (a b) c -> p a (b c)", a=2), io["h1_t"][2 * q:2 * q + 2, :, tok].rearrange("b p t -> p b t")).then_inc(x_in[q % 2], 16)
            sp.wait_ge(sig["x_lo"], DB // 2)
            with sp.Fori(0, N_KEYS // 2) as r:
                for s in range(2):
                    m = 2 * r + s
                    sp.wait_ge(sig["v_lo"], m + 1)
                    sp.wait_ge(sig["gated"], m + 1)
                    sp.dma_start(UR[s][:], io["u_blocks"][bass.ds(m, 1)].rearrange("a p (b c) -> (a p) b c", c=P)).then_inc(e_in[s], 16)
                    sp.dma_start(VR[s][:], io["v_blocks"][bass.ds(m, 1)].rearrange("a p d -> (a p) d")).then_inc(e_in[s], 16)
                    sp.dma_start(GR[s][:], io["g"][half * NT:(half + 1) * NT, :, bass.ds(m, 1), :].rearrange("n i j t -> i (n j) t")).then_inc(e_in[s], 16)
            for n in range(NT):
                sp.wait_ge(sig["rows_ready"], n + 1)
                sp.dma_start(io["out"][half * HT + n * P:half * HT + (n + 1) * P, :], ACC[:, n, :]).then_inc(out_stored, 16)
            sp.wait_ge(out_stored, 16 * NT)

        @block.tensor
        def _(pe):
            pe.sem_inc(sig["hid"], 2)
            pe.sem_inc(sig["out_group"], 2)
            pe.wait_ge(sig["x_lo"], DB // 2)

            def hidden(m, s):
                pe.wait_ge(sig["u_lo"], m + 1)
                pe.wait_ge(sig["gelu"], m + 1)
                for b in range(DB):
                    last = mm3(nc, HID[s][:], (US[s][0][:, b, :], US[s][1][:, b, :]), (XS[0][:, b, :], XS[1][:, b, :]), b == 0, b == DB - 1)
                last.then_inc(sig["hid"], 1)

            def outputs(g, p):
                pe.wait_ge(sig["a_lo"], J * (g + 1))
                pe.wait_ge(sig["v_lo"], J * (g + 1) + 2)
                for q in range(COMBOS):
                    n, c = q // NH, q % NH
                    pe.wait_ge(sig["added"], COMBOS * g + q + 1)
                    for j in range(J):
                        last = mm3(nc, OUT[q % OUT_BANKS][:], (AS[p][0][:, j, n * P:(n + 1) * P], AS[p][1][:, j, n * P:(n + 1) * P]),
                                   (VS[p][0][:, j, c * 512:(c + 1) * 512], VS[p][1][:, j, c * 512:(c + 1) * 512]), j == 0, j == J - 1)
                    last.then_inc(sig["out"], 1)
                pe.wait_ge(sig["out"], COMBOS * (g + 1))
                pe.sem_inc(sig["out_group"], 1)

            def body(g, r, p, first):
                for j in range(J):
                    hidden(J * g + j, j % 2)
                if not (first and p == 0):
                    outputs(g - 1, 1 - p)
            groups(pe, body)
            outputs(GROUPS - 1, 1)

        @block.scalar
        def _(act):
            act.sem_inc(sig["gelu"], 2)
            act.wait_ge(start_in, 48)
            nc.scalar.mul(ACC[:], ACC[:], ALPHA).then_inc(sig["acc_ready"], 1)
            for q in range(DB // 2):
                act.wait_ge(x_in[q % 2], 16 * (q // 2 + 1))
                nc.scalar.copy(XS[0][:, 2 * q:2 * q + 2, :], UR[q % 2][:].rearrange("p (a b) c -> p a (b c)", a=2)).then_inc(sig["x_hi"], 1)

            def split_u(m, r_s, s):
                act.wait_ge(e_in[s], 48 * r_s)
                act.wait_ge(sig["hid"], m + 1)
                nc.scalar.copy(US[s][0][:], UR[s][:]).then_inc(sig["u_hi"], 1)

            def split_v(m, s, g, p, j):
                if j == 0:
                    act.wait_ge(sig["out_group"], g + 1)
                nc.scalar.copy(VS[p][0][:, j, :], VR[s][:]).then_inc(sig["v_hi"], 1)

            def activate(m, s, p, j):
                act.wait_ge(sig["hid"], m + 3)
                act.wait_ge(sig["a_lo"], m - 1) if not isinstance(m, int) or m >= 2 else None
                nc.scalar.activation(AC[s][:], HID[s][:], ACT.Gelu).then_inc(sig["gelu"], 1)
                act.wait_ge(sig["gated"], m + 3)
                nc.scalar.copy(AS[p][0][:, j, :], AC[s][:]).then_inc(sig["a_hi"], 1)

            def body(g, r, p, first):
                for j in range(J):
                    m = J * g + j
                    split_u(m, J // 2 * g + j // 2 + 1, j % 2)
                    if j:
                        activate(m - 1, (j - 1) % 2, p, j - 1)
                    elif not (first and p == 0):
                        activate(m - 1, 1, 1 - p, J - 1)
                    split_v(m, j % 2, g, p, j)
            groups(act, body)
            activate(N_KEYS - 1, 1, 1, J - 1)
            for n in range(NT):
                act.wait_ge(sig["var_ready"], n + 1)
                nc.scalar.activation(std[:], std[:], ACT.Sqrt).then_inc(sig["std_ready"], 1)

        @block.vector
        def _(dve):
            ch = Chain(dve, own)
            tt = nc.vector.tensor_tensor
            dve.sem_inc(sig["v_lo"], 2)
            dve.sem_inc(sig["gated"], 2)
            dve.sem_inc(sig["added"], OUT_BANKS)
            for q in range(DB // 2):
                dve.wait_ge(sig["x_hi"], q + 1)
                tt(XS[1][:, 2 * q:2 * q + 2, :], UR[q % 2][:].rearrange("p (a b) c -> p a (b c)", a=2),
                   XS[0][:, 2 * q:2 * q + 2, :].bitcast(F32), ALU.subtract).then_inc(sig["x_lo"], 1)
            dve.wait_ge(sig["acc_ready"], 1)

            def split_u(m, s):
                dve.wait_ge(sig["u_hi"], m + 1)
                tt(US[s][1][:], UR[s][:], US[s][0][:].bitcast(F32), ALU.subtract).then_inc(sig["u_lo"], 1)

            def split_v(m, s, p, j):
                dve.wait_ge(sig["v_hi"], m + 1)
                tt(VS[p][1][:, j, :], VR[s][:], VS[p][0][:, j, :].bitcast(F32), ALU.subtract).then_inc(sig["v_lo"], 1)

            def gate(m, s, p, j):
                dve.wait_ge(sig["gelu"], m + 3)
                tt(AC[s][:], AC[s][:], GR[s][:].rearrange("p n t -> p (n t)"), ALU.mult).then_inc(sig["gated"], 1)
                dve.wait_ge(sig["a_hi"], m + 1)
                tt(AS[p][1][:, j, :], AC[s][:], AS[p][0][:, j, :].bitcast(F32), ALU.subtract).then_inc(sig["a_lo"], 1)

            def add(g):
                for q in range(COMBOS):
                    rows = ACC[:, q // NH, (q % NH) * 512:(q % NH + 1) * 512]
                    dve.wait_ge(sig["out"], COMBOS * g + q + 1)
                    tt(rows, OUT[q % OUT_BANKS][:], rows, ALU.add).then_inc(sig["added"], 1)

            def body(g, r, p, first):
                for j in range(J):
                    m = J * g + j
                    split_u(m, j % 2)
                    if j:
                        gate(m - 1, (j - 1) % 2, p, j - 1)
                    elif not (first and p == 0):
                        gate(m - 1, 1, 1 - p, J - 1)
                        if not first:
                            add(g - 2)
                    split_v(m, j % 2, p, j)
            groups(dve, body)
            gate(N_KEYS - 1, 1, 1, J - 1)
            add(GROUPS - 2)
            add(GROUPS - 1)
            dve.wait_ge(sig["added"], COMBOS * GROUPS + OUT_BANKS)
            for n in range(NT):
                h = ACC[:, n, :]
                for c in range(NH):
                    ch.mark(nc.vector.bn_stats(stats[:, c, :], h[:, c * 512:(c + 1) * 512]))
                ch.wait()
                ch.step(nc.vector.bn_aggr(mv[:], stats[:]))
                nc.vector.tensor_scalar(std[:], mv[:, 1:2], LN_EPS, None, ALU.add).then_inc(sig["var_ready"], 1)
                dve.wait_ge(sig["std_ready"], n + 1)
                ch.step(nc.vector.reciprocal(std[:], std[:]))
                ch.step(nc.vector.tensor_scalar(h, h, mv[:, 0:1], std[:], ALU.subtract, ALU.mult))
                ch.step(tt(h, h, gain[:], ALU.mult))
                tt(h, h, bias[:], ALU.add).then_inc(sig["rows_ready"], 1)


def build(nc, io):
    with ExitStack() as ctx:
        def keep(scope, name, shape, dt=F32):
            return scope.enter_context(nc.sbuf_tensor(name, shape, dt))

        k = {m: keep(ctx, f"const_{m}", [P, P]) for m in ("ident", "ones", "upper", "lower", "same_head", "in16", "in32")}
        make_constants(nc, k)
        with ExitStack() as h_scope:
            k["hT_hi"], k["hT_lo"] = (keep(h_scope, f"hT_{p}", [P, DB, T], F32R) for p in ("hi", "lo"))
            embed_norm_phase(nc, k, io)
            project_phase(nc, k, io)
        delta_phase(nc, k, io)
        branch_phase(nc, k, io)
        mix_phase(nc, k, io)
        query_phase(nc, k, io)
        gates_phase(nc, k, io)
        for half in range(2):
            experts_phase(nc, k, io, half)


SCRATCH = {
    "h_rows": (SEQ, D),
    "proj": (N_BLK, P, T),
    "bg": (T, 16),
    "o_rows": (SEQ // CHUNK, P, PAIRS * HD),
    "merged": (DB, P, SEQ),
    "h1_rows": (SEQ, D),
    "h1_t": (DB, P, SEQ),
    "scores": (XT, P, 2 * HEADS, N_KEYS),
    "g": (XT, P, P, P),
}
INPUTS = ("x", "meta", "ln0_g", "ln0_b", "w_blocks", "conv_taps", "w_ba", "a_log", "dt_bias", "onorm_g",
          "pool_w", "pool_scale", "w_branches", "w_out", "ln1_g", "ln1_b", "wq_blocks", "keys", "u_blocks", "v_blocks", "ln2_g", "ln2_b")


def lay_out(x, meta, ln0_g, ln0_b, w_in, pool_w, pool_scale, w_br_pool, conv_w, a_log, dt_bias, onorm_g, w_br_delta,
            w_out, ln1_g, ln1_b, peer_wq, peer_k1, peer_k2, peer_u, peer_v, ln2_g, ln2_b):
    a = {}
    a["x"], a["meta"] = x[0], meta
    a["ln0_g"], a["ln0_b"] = ln0_g, ln0_b
    w = w_in[0]
    pw, dw = POOL_GROUPS * P, HEADS * HD
    q0, z0 = pw, pw + 3 * dw
    b0 = z0 + dw
    g0 = b0 + 2 * HEADS
    cols = np.concatenate([w[:, q0:z0], w[:, z0:b0], w[:, g0:], w[:, :pw]], axis=1)
    blocks = lambda m: m.reshape(-1, P, m.shape[1] // P, P).transpose(2, 1, 0, 3).reshape(m.shape[1] // P, P, -1)
    a["w_blocks"] = blocks(cols)
    a["w_ba"] = w[:, b0:g0].reshape(DB, P, 16).transpose(1, 0, 2).reshape(P, -1)
    a["conv_taps"] = conv_w[0].reshape(TAPS, 3 * HEADS, P).transpose(2, 1, 0).reshape(P, -1)
    a["a_log"], a["dt_bias"], a["onorm_g"] = a_log[0], dt_bias[0], onorm_g[0]
    a["pool_w"] = pool_w[0].transpose(1, 0, 2).reshape(P, -1)
    a["pool_scale"] = pool_scale[0].reshape(POOL_GROUPS, P).T
    a["w_branches"] = blocks(np.concatenate([w_br_delta[0], w_br_pool[0]], axis=0))
    a["w_out"], a["ln1_g"], a["ln1_b"] = w_out[0], ln1_g[0], ln1_b[0]
    a["wq_blocks"] = blocks(peer_wq[0])
    a["keys"] = np.stack([peer_k1[0], peer_k2[0]], axis=1).reshape(2 * HEADS, N_KEYS, P).transpose(0, 2, 1)
    a["u_blocks"] = peer_u[0].reshape(P, P, DB, P).transpose(1, 3, 2, 0).reshape(P, P, -1)
    a["v_blocks"] = peer_v[0].reshape(P, P, D).transpose(1, 0, 2)
    a["ln2_g"], a["ln2_b"] = ln2_g[0], ln2_b[0]
    return a


def kernel(**inputs):
    import concourse.bacc as bacc
    from concourse.bass_utils import run_bass_kernel_spmd

    nc = bacc.Bacc("TRN2", target_bir_lowering=False, num_devices=1)
    laid = lay_out(**{n: np.asarray(v) for n, v in inputs.items()})
    tensors, arrays = {}, {}
    for name in INPUTS:
        arrays[f"in_{name}"] = np.ascontiguousarray(laid[name])
        tensors[name] = nc.dram_tensor(f"in_{name}", arrays[f"in_{name}"].shape, F32, kind="ExternalInput").ap()
    for name, shape in SCRATCH.items():
        tensors[name] = nc.dram_tensor(name, shape, F32, kind="Internal").ap()
    tensors["out"] = nc.dram_tensor("out", (SEQ, D), F32, kind="ExternalOutput").ap()
    build(nc, tensors)
    r = run_bass_kernel_spmd(nc, [arrays], core_ids=[0])
    return r.results[0]["out"].reshape(1, SEQ, D)
```

```python
from contextlib import ExitStack

import numpy as np
import concourse.bass as bass
from concourse import mybir

F32 = mybir.dt.float32
F32R = mybir.dt.float32r
F16 = mybir.dt.float16
U32 = mybir.dt.uint32
ACT = mybir.ActivationFunctionType
ALU = mybir.AluOpType
AX = mybir.AxisListType

P = 128
D = 1024
DB = D // P
N_META = 16
SEQ = 1024
T = N_META + SEQ
XT = SEQ // P
HEADS = 8
HD = 128
PAIRS = HEADS // 2
CHUNK = 64
PAD = CHUNK - N_META
N_CHUNKS = (T + PAD) // CHUNK
POOL_GROUPS = 4
POOL_WINDOWS = (2, 4, 8, 16)
TAPS = 4
N_KEYS = 128
TOPK = 16
ALPHA = 2.0 ** 0.25
LN_EPS, RMS_EPS, L2_EPS = 1e-5, 1e-6, 1e-6
LOWEST = -3.0e38

BLK_Q, BLK_K, BLK_V = 0, HEADS, 2 * HEADS
BLK_Z = 3 * HEADS
BLK_GATE = BLK_Z + HEADS
BLK_POOL = BLK_GATE + 2 * DB
N_BLK = BLK_POOL + POOL_GROUPS
PIECES = 4
PIECE = T // PIECES


class Chain:

    def __init__(self, eng, sem):
        self.eng, self.sem, self.n = eng, sem, 0

    def step(self, ins):
        self.mark(ins)
        self.wait()

    def mark(self, ins):
        self.n += 1
        ins.then_inc(self.sem, 1)

    def wait(self):
        self.eng.wait_ge(self.sem, self.n)

    def restart(self):
        self.wait()
        self.eng.sem_clear(self.sem)
        self.n = 0


class Phase:

    def __init__(self, nc, name):
        self.nc, self.name, self.ctx, self.taken = nc, name, ExitStack(), []

    def __enter__(self):
        self.ctx.__enter__()
        return self

    def __exit__(self, *a):
        done = self.ctx.__exit__(*a)
        if self.taken:
            self.nc.clear_and_free_semaphores(self.taken)
            self.nc.all_engine_barrier()
        return done

    def sb(self, name, shape, dt=F32):
        return self.ctx.enter_context(self.nc.sbuf_tensor(f"{self.name}_{name}", shape, dt))

    def ps(self, name, shape, dt=F32):
        return self.ctx.enter_context(self.nc.psum_tensor(f"{self.name}_{name}", shape, dt))

    def sem(self, name):
        self.taken.append(self.nc.alloc_semaphore(f"{self.name}_{name}"))
        return self.taken[-1]

    def sems(self, name, n=2):
        return [self.sem(f"{name}{i}") for i in range(n)]

    def block(self):
        return self.ctx.enter_context(self.nc.Block())


def row_bcast(ap, n=P):
    return ap.rearrange("(a k) -> a k", a=1).partition_broadcast(n) if ap.ndim == 1 else ap.partition_broadcast(n)


def make_constants(nc, k):
    with Phase(nc, "const") as ph:
        made = ph.sem("made")
        block = ph.block()

        @block.gpsimd
        def _(pool):
            ch = Chain(pool, made)

            def select(ap, op, fill, base, pattern, mult):
                ch.step(pool.affine_select(out=ap, in_=ap, compare_op=op, fill=fill, base=base,
                                           pattern=pattern, channel_multiplier=mult))

            ch.mark(pool.memset(k["ones"][:], 1.0))
            ch.step(pool.memset(k["ident"][:], 0.0))
            select(k["ident"][:], ALU.not_equal, 1.0, 0, [[-1, P]], 1)

            def keep_blocks(m, size):
                v = m[:].rearrange("p (g e) -> p g e", e=size)
                select(v, ALU.is_ge, 0.0, 0, [[-size, P // size], [0, size]], 1)
                select(v, ALU.is_ge, 0.0, size - 1, [[size, P // size], [0, size]], -1)

            for m in (k["upper"], k["lower"], k["same_head"], k["in16"], k["in32"]):
                ch.step(pool.memset(m[:], 1.0))
            select(k["upper"][:], ALU.is_ge, 0.0, 0, [[1, P]], -1)
            select(k["lower"][:], ALU.is_gt, 0.0, 0, [[-1, P]], 1)
            for m, size in ((k["upper"], CHUNK), (k["lower"], CHUNK), (k["same_head"], CHUNK), (k["in16"], 16), (k["in32"], 32)):
                keep_blocks(m, size)


def embed_norm_phase(nc, k, io):
    with Phase(nc, "ln0") as ph:
        X = [ph.sb(f"x{u}", [P, D]) for u in range(2)]
        H = [ph.sb(f"h{u}", [P, D]) for u in range(2)]
        gain, bias = ph.sb("gain", [P, D]), ph.sb("bias", [P, D])
        stats, mv = ph.sb("stats", [P, 2, 6]), ph.sb("mv", [P, 2])
        veps, std, rstd = ph.sb("veps", [P, 1]), ph.sb("std", [P, 1]), ph.sb("rstd", [P, 1])
        TP = [ph.ps(f"t{u}", [P, DB, P]) for u in range(2)]
        consts_in = ph.sem("consts_in")
        x_in, h_out = ph.sems("x_in"), ph.sems("h_out")
        x_free, var_ready, std_ready, h_ready = (ph.sem(n) for n in ("x_free", "var_ready", "std_ready", "h_ready"))
        t_ready, t_free, hi_ready = (ph.sem(n) for n in ("t_ready", "t_free", "hi_ready"))
        own = ph.sem("dve_own")
        block = ph.block()

        @block.sync
        def _(sp):
            sp.dma_start(gain[:], row_bcast(io["ln0_g"])).then_inc(consts_in, 16)
            sp.dma_start(bias[:], row_bcast(io["ln0_b"])).then_inc(consts_in, 16)
            sp.dma_start(X[1][0:N_META, :], io["meta"][:, :]).then_inc(x_in[1], 16)
            with sp.Fori(0, XT // 2) as i:
                for u in range(2):
                    n = 2 * i + u + 1
                    sp.wait_ge(x_free, n + 1)
                    sp.dma_start(X[u][:], io["x"][bass.ts(n - 1, P), :]).then_inc(x_in[u], 16)

        @block.vector
        def _(dve):
            ch = Chain(dve, own)
            dve.sem_inc(x_free, 2)
            dve.wait_ge(consts_in, 32)

            def tile(n, u, rows, loads, cols):
                x, h = X[u][0:rows, :], H[u][0:rows, :]
                dve.wait_ge(x_in[u], 16 * loads)
                for s in range(2):
                    ch.mark(nc.vector.bn_stats(stats[0:rows, s, :], x[:, s * 512:(s + 1) * 512]))
                ch.wait()
                ch.step(nc.vector.bn_aggr(mv[0:rows, :], stats[0:rows]))
                nc.vector.tensor_scalar(veps[0:rows], mv[0:rows, 1:2], LN_EPS, None, ALU.add).then_inc(var_ready, 1)
                dve.wait_ge(std_ready, n + 1)
                ch.step(nc.vector.reciprocal(rstd[0:rows], std[0:rows]))
                if rows == P:
                    dve.wait_ge(h_out[u], 16 * (loads - u))
                    dve.wait_ge(t_ready, n - 1 + (u == 0))
                nc.vector.tensor_scalar(h, x, mv[0:rows, 0:1], rstd[0:rows], ALU.subtract, ALU.mult).then_inc(x_free, 1)
                dve.wait_ge(x_free, n + 3)
                ch.step(nc.vector.tensor_tensor(h, h, gain[0:rows, :], ALU.mult))
                nc.vector.tensor_tensor(h, h, bias[0:rows, :], ALU.add).then_inc(h_ready, 1)
                dve.wait_ge(hi_ready, n + 1)
                nc.vector.tensor_tensor(k["hT_lo"][:, :, cols], TP[u][:, :, 0:rows],
                                        k["hT_hi"][:, :, cols].bitcast(F32), ALU.subtract).then_inc(t_free, 1)
                ch.restart()

            for u in range(2):
                dve.sem_inc(h_out[u], 16)
            tile(0, 1, N_META, 1, slice(0, N_META))
            with dve.Fori(0, XT // 2) as i:
                for u in range(2):
                    tile(2 * i + u + 1, u, P, i + 1 + u, bass.ds((2 * i + u) * P + N_META, P))

        @block.scalar
        def _(act):
            def tile(n, u, rows, cols):
                act.wait_ge(var_ready, n + 1)
                nc.scalar.activation(std[0:rows], veps[0:rows], ACT.Sqrt).then_inc(std_ready, 1)
                if rows == P:
                    act.wait_ge(h_ready, n + 1)
                    act.dma_start(io["h_rows"][bass.ts(n - 1, P), :], H[u][:]).then_inc(h_out[u], 16)
                act.wait_ge(t_ready, n + 1)
                nc.scalar.copy(k["hT_hi"][:, :, cols], TP[u][:, :, 0:rows]).then_inc(hi_ready, 1)

            tile(0, 1, N_META, slice(0, N_META))
            with act.Fori(0, XT // 2) as i:
                for u in range(2):
                    tile(2 * i + u + 1, u, P, bass.ds((2 * i + u) * P + N_META, P))
            for u in range(2):
                act.wait_ge(h_out[u], 16 * (XT // 2 + 1))

        @block.tensor
        def _(pe):
            pe.sem_inc(t_free, 2)

            def tile(n, u, rows):
                pe.wait_ge(h_ready, n + 1)
                pe.wait_ge(t_free, n + 1)
                for b in range(DB):
                    last = nc.tensor.transpose(TP[u][:, b, 0:rows], H[u][0:rows, bass.ts(b, P)], k["ident"][0:rows, 0:rows])
                last.then_inc(t_ready, 1)

            tile(0, 1, N_META)
            with pe.Fori(0, XT // 2) as i:
                for u in range(2):
                    tile(2 * i + u + 1, u, P)


def mm3(nc, out, lhs, rhs, first=True, last=True):
    (lh, ll), (rh, rl) = lhs, rhs
    nc.tensor.matmul(out, lh, rh, start=first, stop=False)
    nc.tensor.matmul(out, lh, rl, start=False, stop=False)
    return nc.tensor.matmul(out, ll, rh, start=False, stop=last)


def project_phase(nc, k, io):
    with Phase(nc, "proj") as ph:
        W = [ph.sb(f"w{u}", [P, DB, P]) for u in range(2)]
        Wh = [ph.sb(f"wh{u}", [P, DB, P], F32R) for u in range(2)]
        Wl = [ph.sb(f"wl{u}", [P, DB, P], F32R) for u in range(2)]
        Y = [ph.sb(f"y{u}", [P, TAPS - 1 + T]) for u in range(2)]
        C = [ph.sb(f"c{u}", [P, T]) for u in range(2)]
        S = [ph.sb(f"s{u}", [P, T]) for u in range(2)]
        SQ = ph.sb("sq", [P, T])
        taps = ph.sb("taps", [P, 3 * HEADS, TAPS])
        epsq, epsk = ph.sb("epsq", [P, 1]), ph.sb("epsk", [P, 1])
        onorm = ph.sb("onorm", [P, 1])
        wba = ph.sb("wba", [P, DB, 16])
        wbah, wbal = ph.sb("wbah", [P, DB, 16], F32R), ph.sb("wbal", [P, DB, 16], F32R)
        ba = ph.sb("ba", [16, T])
        bat = ph.sb("bat", [P, 9, 16])
        aexp, dtb, ea = ph.sb("aexp", [P, 8]), ph.sb("dtb", [P, 8]), ph.sb("ea", [P, 9, 8])
        beta, gate = ph.sb("beta", [P, 9, 8]), ph.sb("gate", [P, 9, 8])
        M = [ph.ps(f"m{u}", [P, PIECES, 512]) for u in range(2)]
        consts_in = ph.sem("consts_in")
        w_in, s_ready, y_out = ph.sems("w_in"), ph.sems("s_ready"), ph.sems("y_out")
        wl_ready, mm_ready, c_ready = ph.sem("wl_ready"), ph.sem("mm_ready"), ph.sem("c_ready")
        wh_ready, y_ready, mm_free, silu_ready, sq_ready, norm_ready, root_ready = (
            ph.sem(n) for n in ("wh_ready", "y_ready", "mm_free", "silu_ready", "sq_ready", "norm_ready", "root_ready"))
        own = ph.sem("dve_own")
        ba_sem = {n: ph.sem(n) for n in ("ba_split", "ba_mm", "ba_rows", "ba_t", "ba_copy", "ba_act", "ba_dve", "ba_out")}
        setup, passed = ph.sem("setup"), ph.sem("passed")
        block = ph.block()
        pieces = lambda ap: ap.rearrange("p (a b) -> p a b", a=PIECES)
        banks = lambda u: M[u][:, :, 0:PIECE]
        @block.sync
        def _(sp):
            sp.dma_start(taps[:], io["conv_taps"].rearrange("p (n j) -> p n j", j=TAPS)).then_inc(consts_in, 16)
            sp.dma_start(onorm[:], io["onorm_g"].rearrange("(p a) -> p a", a=1)).then_inc(consts_in, 16)
            sp.dma_start(wba[:], io["w_ba"].rearrange("p (b c) -> p b c", c=16)).then_inc(consts_in, 16)
            sp.dma_start(aexp[:], row_bcast(io["a_log"])).then_inc(consts_in, 16)
            sp.dma_start(dtb[:], row_bcast(io["dt_bias"])).then_inc(consts_in, 16)

            with sp.Fori(0, N_BLK // 2) as r:
                for u in range(2):
                    sp.wait_ge(s_ready[u], r + 1)
                    sp.dma_start(io["proj"][bass.ds(2 * r + u, 1)].rearrange("a p t -> (a p) t"), S[u][:]).then_inc(y_out[u], 16)
            for u in range(2):
                sp.wait_ge(y_out[u], 16 * (N_BLK // 2 + 1))

        @block.gpsimd
        def _(pool):
            pool.memset(epsq[:], HD * L2_EPS).then_inc(setup, 1)
            pool.memset(epsk[:], L2_EPS).then_inc(setup, 1)
            for u in range(2):
                pool.memset(Y[u][:, 0:TAPS - 1], 0.0).then_inc(setup, 1)
            pool.sem_inc(wl_ready, 2)

            def split(n, r, u):
                pool.wait_ge(w_in[u], 16 * (r + 1))
                pool.wait_ge(mm_ready, n + 1)
                pool.sem_inc(passed, 1)
                nc.gpsimd.tensor_copy(Wh[u][:], W[u][:]).then_inc(wh_ready, 1)
                pool.wait_ge(wh_ready, n + 1)
                nc.gpsimd.tensor_tensor(Wl[u][:], W[u][:], Wh[u][:].bitcast(F32), ALU.subtract).then_inc(wl_ready, 1)

            def load(n, u):
                pool.wait_ge(wl_ready, n + 1)
                pool.dma_start(W[u][:], io["w_blocks"][bass.ds(n, 1)].rearrange("a p (b c) -> (a p) b c", c=P)).then_inc(w_in[u], 16)

            for u in range(2):
                load(u, u)
            with pool.Fori(0, N_BLK // 2 - 1) as r:
                for u in range(2):
                    split(2 * r + u, r, u)
                    load(2 * r + u + 2, u)
            for u in range(2):
                split(N_BLK - 2 + u, N_BLK // 2 - 1, u)
            pool.wait_ge(ba_sem["ba_dve"], 5)
            for src, c0 in ((beta, 0), (gate, 8)):
                dst = io["bg"][:, c0:c0 + 8]
                pool.dma_start(dst[0:N_META, :], src[0:N_META, 8, :]).then_inc(ba_sem["ba_out"], 16)
                pool.dma_start(dst[N_META:T, :].rearrange("(n p) c -> p n c", p=P), src[:, 0:8, :]).then_inc(ba_sem["ba_out"], 16)
            pool.wait_ge(ba_sem["ba_out"], 64)

        @block.tensor
        def _(pe):
            pe.sem_inc(mm_free, 2)
            pe.sem_inc(mm_ready, 2)

            def main(n, u):
                pe.wait_ge(wl_ready, n + 3)
                pe.wait_ge(mm_free, n + 1)
                for b in range(DB):
                    for wpart, hparts in ((Wh[u], (k["hT_hi"], k["hT_lo"])), (Wl[u], (k["hT_hi"],))):
                        for hpart in hparts:
                            for c in range(PIECES):
                                last = nc.tensor.matmul(M[u][:, c, 0:PIECE], wpart[:, b, :],
                                                        hpart[:, b, c * PIECE:(c + 1) * PIECE],
                                                        start=(b == 0 and wpart is Wh[u] and hpart is k["hT_hi"]),
                                                        stop=(b == DB - 1 and wpart is Wl[u]))
                last.then_inc(mm_ready, 1)

            def norm(n, u):
                pe.wait_ge(sq_ready, n + 1)
                for c in range(PIECES):
                    last = nc.tensor.matmul(M[u][:, c, 0:PIECE], k["ones"][:], SQ[:, c * PIECE:(c + 1) * PIECE], start=True, stop=True)
                last.then_inc(norm_ready, 1)

            main(0, 0)
            main(1, 1)
            norm(0, 0)
            with pe.Fori(1, BLK_V // 2) as r:
                main(2 * r, 0)
                norm(2 * r - 1, 1)
                main(2 * r + 1, 1)
                norm(2 * r, 0)
            main(BLK_V, 0)
            norm(BLK_V - 1, 1)
            main(BLK_V + 1, 1)
            with pe.Fori(BLK_V // 2 + 1, N_BLK // 2) as r:
                for u in range(2):
                    main(2 * r + u, u)
            pe.wait_ge(ba_sem["ba_split"], 2)
            pe.wait_ge(mm_free, N_BLK + 2)
            for b in range(DB):
                for c in range(PIECES):
                    cols = slice(c * PIECE, (c + 1) * PIECE)
                    last = mm3(nc, M[0][0:16, c, 0:PIECE], (wbah[:, b, :], wbal[:, b, :]), (k["hT_hi"][:, b, cols], k["hT_lo"][:, b, cols]), b == 0, b == DB - 1)
            last.then_inc(ba_sem["ba_mm"], 1)
            pe.wait_ge(ba_sem["ba_rows"], 1)
            for t in range(XT):
                nc.tensor.transpose(M[1][:, 0, t * 16:(t + 1) * 16], ba[:, N_META + t * P:N_META + (t + 1) * P], k["ident"][0:16, 0:16])
            nc.tensor.transpose(M[1][0:N_META, 0, XT * 16:(XT + 1) * 16], ba[:, 0:N_META], k["ident"][0:16, 0:16]).then_inc(ba_sem["ba_t"], 1)

        @block.scalar
        def _(act):
            act.wait_ge(setup, 4)
            act.wait_ge(consts_in, 80)

            def take(n, u):
                act.wait_ge(mm_ready, n + 3)
                act.wait_ge(c_ready, n + 1)
                nc.scalar.copy(pieces(Y[u][:, TAPS - 1:]), banks(u)).then_inc(y_ready, 1)

            def silu_square(n, u):
                act.wait_ge(c_ready, n + 3)
                nc.scalar.activation(C[u][:], C[u][:], ACT.Silu).then_inc(silu_ready, 1)
                act.wait_ge(silu_ready, n + 1)
                nc.scalar.activation(SQ[:], C[u][:], ACT.Square).then_inc(sq_ready, 1)

            def root(n, r, u, scale, eps):
                act.wait_ge(norm_ready, n + 1)
                act.wait_ge(y_out[u], 16 * (r + 1))
                nc.scalar.activation(pieces(S[u][:]), banks(u), ACT.Sqrt, bias=eps[:], scale=scale).then_inc(root_ready, 1)
                act.wait_ge(root_ready, n + 1)
                act.sem_inc(mm_free, 1)

            take(0, 0)
            silu_square(0, 0)
            for first, last, scale, eps in ((BLK_Q, BLK_K, float(HD), epsq), (BLK_K, BLK_V, 1.0, epsk)):
                with act.Fori(first // 2, last // 2 - 1) as r:
                    take(2 * r + 1, 1)
                    root(2 * r, r, 0, scale, eps)
                    silu_square(2 * r + 1, 1)
                    take(2 * r + 2, 0)
                    root(2 * r + 1, r, 1, scale, eps)
                    silu_square(2 * r + 2, 0)
                take(last - 1, 1)
                root(last - 2, last // 2 - 1, 0, scale, eps)
                silu_square(last - 1, 1)
                take(last, 0)
                root(last - 1, last // 2 - 1, 1, scale, eps)
                if last < BLK_V:
                    silu_square(last, 0)

            def rest(kind, n, r, u, taken=False):
                if kind == "v":
                    if not taken:
                        take(n, u)
                    act.wait_ge(y_ready, n + 1)
                    act.sem_inc(mm_free, 1)
                    act.wait_ge(c_ready, n + 3)
                    act.wait_ge(y_out[u], 16 * (r + 1))
                    nc.scalar.activation(S[u][:], C[u][:], ACT.Silu).then_inc(s_ready[u], 1)
                    return
                act.wait_ge(mm_ready, n + 3)
                act.wait_ge(y_out[u], 16 * (r + 1))
                if kind == "z":
                    nc.scalar.activation(pieces(C[u][:]), banks(u), ACT.Silu).then_inc(silu_ready, 1)
                    act.wait_ge(silu_ready, n + 1 - HEADS)
                    act.sem_inc(mm_free, 1)
                    nc.scalar.mul(S[u][:], C[u][:], onorm[:]).then_inc(s_ready[u], 1)
                else:
                    func = ACT.Sigmoid if kind == "gate" else ACT.Copy
                    nc.scalar.activation(pieces(S[u][:]), banks(u), func).then_inc(s_ready[u], 1)
                    act.wait_ge(s_ready[u], r + 1)
                    act.sem_inc(mm_free, 1)
            rest("v", BLK_V, BLK_V // 2, 0, taken=True)
            rest("v", BLK_V + 1, BLK_V // 2, 1)
            for kind, first, count in (("v", BLK_V + 2, HEADS - 2), ("z", BLK_Z, HEADS), ("gate", BLK_GATE, 2 * DB), ("pool", BLK_POOL, POOL_GROUPS)):
                with act.Fori(first // 2, (first + count) // 2) as r:
                    for u in range(2):
                        rest(kind, 2 * r + u, r, u)
            nc.scalar.copy(wbah[:], wba[:]).then_inc(ba_sem["ba_split"], 1)
            act.wait_ge(ba_sem["ba_mm"], 1)
            nc.scalar.copy(pieces(ba[:]), M[0][0:16, :, 0:PIECE]).then_inc(ba_sem["ba_rows"], 1)
            act.wait_ge(ba_sem["ba_copy"], 1)
            nc.scalar.activation(beta[:], bat[:, :, 0:8], ACT.Exp, scale=-1.0).then_inc(ba_sem["ba_act"], 1)
            act.wait_ge(ba_sem["ba_dve"], 1)
            nc.scalar.activation(gate[:], ea[:], ACT.Abs).then_inc(ba_sem["ba_act"], 1)
            act.wait_ge(ba_sem["ba_act"], 2)
            nc.scalar.activation(gate[:], gate[:], ACT.Exp, scale=-1.0).then_inc(ba_sem["ba_act"], 1)
            nc.scalar.activation(aexp[:], aexp[:], ACT.Exp).then_inc(ba_sem["ba_act"], 1)
            act.wait_ge(ba_sem["ba_act"], 4)
            nc.scalar.activation(gate[:], gate[:], ACT.Ln, bias=1.0).then_inc(ba_sem["ba_act"], 1)

        @block.vector
        def _(dve):
            ch = Chain(dve, own)
            dve.sem_inc(c_ready, 2)
            for u in range(2):
                dve.sem_inc(y_out[u], 16)
            dve.wait_ge(consts_in, 80)

            def convolve(n, r, u):
                tap = lambda j: taps[:, bass.ds(n, 1), j:j + 1].rearrange("p a b -> p (a b)")
                dve.wait_ge(y_ready, n + 1)
                dve.wait_ge(y_out[u], 16 * (r + 1))
                ch.step(nc.vector.tensor_scalar(C[u][:], Y[u][:, 0:T], tap(0), None, ALU.mult))
                for j in range(1, TAPS):
                    ins = nc.vector.scalar_tensor_tensor(out=C[u][:], in0=Y[u][:, j:j + T], scalar=tap(j), in1=C[u][:], op0=ALU.mult, op1=ALU.add)
                    if j < TAPS - 1:
                        ch.step(ins)
                ins.then_inc(c_ready, 1)
                ch.restart()

            def normalise(n, u):
                dve.wait_ge(root_ready, n + 1)
                ch.step(nc.vector.reciprocal(S[u][:], S[u][:]))
                nc.vector.tensor_tensor(S[u][:], S[u][:], C[u][:], ALU.mult).then_inc(s_ready[u], 1)
                ch.restart()

            convolve(0, 0, 0)
            with dve.Fori(0, BLK_V // 2 - 1) as r:
                convolve(2 * r + 1, r, 1)
                normalise(2 * r, 0)
                convolve(2 * r + 2, r + 1, 0)
                normalise(2 * r + 1, 1)
            convolve(BLK_V - 1, BLK_V // 2 - 1, 1)
            normalise(BLK_V - 2, 0)
            convolve(BLK_V, BLK_V // 2, 0)
            normalise(BLK_V - 1, 1)
            convolve(BLK_V + 1, BLK_V // 2, 1)
            with dve.Fori(BLK_V // 2 + 1, BLK_Z // 2) as r:
                for u in range(2):
                    convolve(2 * r + u, r, u)
            dve.wait_ge(ba_sem["ba_split"], 1)
            nc.vector.tensor_tensor(wbal[:], wba[:], wbah[:].bitcast(F32), ALU.subtract).then_inc(ba_sem["ba_split"], 1)
            dve.wait_ge(ba_sem["ba_t"], 1)
            ch.step(nc.vector.memset(bat[:, XT, :], 0.0))
            nc.vector.tensor_copy(bat[0:N_META, XT, :], M[1][0:N_META, 0, XT * 16:(XT + 1) * 16])
            nc.vector.tensor_copy(bat[:, 0:XT, :], M[1][:, 0, 0:XT * 16].rearrange("p (t c) -> p t c", c=16)).then_inc(ba_sem["ba_copy"], 1)
            dve.wait_ge(ba_sem["ba_copy"], 1)
            nc.vector.tensor_tensor(ea[:], bat[:, :, 8:16], dtb[:].unsqueeze(1).to_broadcast([P, XT + 1, 8]), ALU.add).then_inc(ba_sem["ba_dve"], 1)
            dve.wait_ge(ba_sem["ba_act"], 5)
            ch.step(nc.vector.tensor_scalar(ea[:], ea[:], 0.0, None, ALU.max))
            ch.step(nc.vector.tensor_tensor(gate[:], gate[:], ea[:], ALU.add))
            ch.step(nc.vector.tensor_scalar(aexp[:], aexp[:], -1.0, None, ALU.mult))
            nc.vector.tensor_tensor(gate[:], gate[:], aexp[:].unsqueeze(1).to_broadcast([P, XT + 1, 8]), ALU.mult).then_inc(ba_sem["ba_dve"], 2)
            ch.step(nc.vector.tensor_scalar(beta[:], beta[:], 1.0, None, ALU.add))
            nc.vector.reciprocal(beta[:], beta[:]).then_inc(ba_sem["ba_dve"], 2)


def delta_phase(nc, k, io):
    CH = CHUNK
    with Phase(nc, "delta") as ph:
        W = PAIRS * P
        pair3 = lambda ap: ap.rearrange("p (m e) -> p m e", m=PAIRS)

        def two(name, shape=(P, W)):
            return [ph.sb(f"{name}{u}", list(shape)) for u in range(2)]

        KT, QT, VT = (two(n, (P, HEADS, CH)) for n in ("kT", "qT", "vT"))
        BG = two("bg", (P, 16))
        GP, BP = two("g_pair", (P, PAIRS)), two("beta_pair", (P, PAIRS))
        KR, VR = two("k_rows"), two("v_rows")
        R, E1, E2, ECB = two("r"), two("e1"), two("e2"), two("ecb")
        CUM = two("cum", (P, 2 * PAIRS))
        EC, KS, BE = two("exp_cum", (P, PAIRS)), two("k_scale", (P, PAIRS)), two("beta_exp", (P, PAIRS))
        A, AT_T, QD = two("a"), two("attn_t"), two("q_dec")
        KBE, KD, VB = two("kbe"), two("k_dec"), two("vb")
        Dm, DT, M32, M64, Z = two("d"), two("dT"), two("m32"), two("m64"), two("z")
        PW, PWT = two("pw"), two("pwT")
        U, WT, VN, O = two("u"), two("wT"), two("vn"), two("o")
        S = ph.sb("state", [P, HEADS, HD])
        BANK = ph.ps("bank", [P, 8, 512])
        X = lambda u, j: BANK[:, 3 * u + j, :]
        WS = BANK[:, 6, :]

        loaded, o_out = ph.sems("loaded"), ph.sems("o_out")
        own = ph.sem("dve_own")

        signals = {n: ph.sems(n) for n in ("gates_in", "r_ready", "kv_rows", "k_copied", "v_copied", "decay_raw", "cum_ready", "diff_ready", "exp_ready",
                  "grams", "masked1", "a_ready", "attn_ready", "qd_ready", "rows_scaled", "at_raw", "d_ready",
                  "sq1", "p2", "p2t", "sq2", "z2", "p4", "p4t", "sq3", "z4", "p8", "sq4", "z8",
                  "lv1", "x1", "t1", "lv1b", "z32", "lv2", "x2", "t2", "lv2b", "z64", "uw_raw", "u_ready", "w_ready",
                  "ws_raw", "vn_ready", "out_raw", "o_ready", "upd_raw", "state_done")}
        zeroed = ph.sem("zeroed")
        block = ph.block()

        def chunks(eng, body):
            body(0, {1: 1}, (1,))
            with eng.Fori(0, (N_CHUNKS - 1) // 2) as r:
                body(2 * r + 1, {0: r + 1, 1: r + 2}, (0, 1))

        @block.sync
        def _(sp):
            sp.wait_ge(zeroed, 5)
            for dst, first in ((KT, BLK_K), (QT, BLK_Q), (VT, BLK_V)):
                sp.dma_start(dst[1][:, :, PAD:CH], io["proj"][first:first + HEADS, :, 0:N_META].rearrange("h p t -> p h t")).then_inc(loaded[1], 16)
            for half in range(2):
                sp.dma_start(BG[1][half * CH + PAD:(half + 1) * CH, :], io["bg"][0:N_META, :]).then_inc(loaded[1], 16)
            with sp.Fori(0, (N_CHUNKS - 1) // 2) as r:
                for u, n in ((0, r + 1), (1, r + 2)):
                    t0 = (2 * r + u) * CH + N_META
                    sp.wait_ge(signals["state_done"][u], n)
                    for dst, first in ((KT, BLK_K), (QT, BLK_Q), (VT, BLK_V)):
                        sp.dma_start(dst[u][:], io["proj"][first:first + HEADS, :, bass.ds(t0, CH)].rearrange("h p t -> p h t")).then_inc(loaded[u], 16)
                    for half in range(2):
                        sp.dma_start(BG[u][half * CH:(half + 1) * CH, :], io["bg"][bass.ds(t0, CH), :]).then_inc(loaded[u], 16)

        @block.gpsimd
        def _(pool):
            pool.memset(S[:], 0.0).then_inc(zeroed, 1)
            for t in (KT[1], QT[1], VT[1], BG[1]):
                pool.memset(t[:], 0.0).then_inc(zeroed, 1)
            mul = lambda out, a, b: nc.gpsimd.tensor_tensor(out, a, b, ALU.mult)

            def body(c, n, slots):
                for u in slots:
                    pool.wait_ge(signals["gates_in"][u], n[u])
                    mul(pair3(R[u][:]), k["upper"][:].unsqueeze(1).to_broadcast([P, PAIRS, P]),
                        GP[u][:].unsqueeze(2).to_broadcast([P, PAIRS, P])).then_inc(signals["r_ready"][u], 1)
                for u in slots:
                    pool.wait_ge(signals["exp_ready"][u], n[u])
                    mul(pair3(E1[u][:]), pair3(E1[u][:]), k["upper"][:].unsqueeze(1).to_broadcast([P, PAIRS, P])).then_inc(signals["masked1"][u], 1)
                    mul(BE[u][:], BP[u][:], EC[u][:]).then_inc(signals["qd_ready"][u], 1)
                    mul(QD[u][:], QT[u][:].rearrange("p h t -> p (h t)"), ECB[u][:]).then_inc(signals["qd_ready"][u], 1)
                    wide = lambda s: s[:].unsqueeze(2).to_broadcast([P, PAIRS, P])
                    pool.wait_ge(signals["v_copied"][u], n[u])
                    mul(pair3(VB[u][:]), pair3(VR[u][:]), wide(BP[u])).then_inc(signals["rows_scaled"][u], 1)
                    mul(pair3(KD[u][:]), pair3(KR[u][:]), wide(KS[u])).then_inc(signals["rows_scaled"][u], 1)
                    pool.wait_ge(signals["qd_ready"][u], 2 * n[u])
                    mul(pair3(KBE[u][:]), pair3(KR[u][:]), wide(BE[u])).then_inc(signals["rows_scaled"][u], 1)
            chunks(pool, body)

        @block.tensor
        def _(pe):
            def pairs(fn, out, a, b=None, lo=True):
                for m in range(PAIRS):
                    cs = slice(m * P, (m + 1) * P)
                    if b is None:
                        last = nc.tensor.transpose(out[:, cs], a[:, cs], k["ident"][:])
                    else:
                        last = nc.tensor.matmul(out[:, cs], a[:, cs], b[:, cs], start=True, stop=True)
                return last

            def body(c, n, slots):
                on = lambda name, u: pe.wait_ge(signals[name][u], n[u])
                flat = lambda t: t[:].rearrange("p h t -> p (h t)")
                for u in slots:
                    pe.wait_ge(loaded[u], 80 * n[u])
                    pe.wait_ge(signals["state_done"][u], n[u])
                    pairs(None, X(u, 0), flat(KT[u]))
                    pairs(None, X(u, 1), flat(VT[u])).then_inc(signals["kv_rows"][u], 1)
                for u in slots:
                    on("r_ready", u)
                    nc.tensor.matmul(X(u, 2), k["ones"][:], R[u][:], start=True, stop=True)
                    on("k_copied", u)
                    nc.tensor.matmul(X(u, 0)[:, 0:PAIRS], k["upper"][:], GP[u][:], start=True, stop=True)
                    nc.tensor.matmul(X(u, 0)[:, PAIRS:2 * PAIRS], k["same_head"][:], GP[u][:], start=True, stop=True).then_inc(signals["decay_raw"][u], 1)
                for u in slots:
                    on("cum_ready", u)
                    on("v_copied", u)
                    pairs(None, X(u, 0), flat(KT[u]), flat(KT[u]))
                    pairs(None, X(u, 1), flat(KT[u]), flat(QT[u])).then_inc(signals["grams"][u], 1)
                for u in slots:
                    on("a_ready", u)
                    pairs(None, X(u, 2), A[u]).then_inc(signals["at_raw"][u], 1)
                for u in slots:
                    on("d_ready", u)
                    on("attn_ready", u)
                    pairs(None, X(u, 0), DT[u], Dm[u])
                    pairs(None, X(u, 1), Dm[u], DT[u]).then_inc(signals["sq1"][u], 1)
                for u in slots:
                    on("p2", u)
                    on("p2t", u)
                    pairs(None, X(u, 2), PW[u], Z[u])
                    pairs(None, X(u, 0), PWT[u], PW[u])
                    pairs(None, X(u, 1), PW[u], PWT[u]).then_inc(signals["sq2"][u], 1)
                for u in slots:
                    on("p4", u)
                    on("p4t", u)
                    on("z2", u)
                    pairs(None, X(u, 2), PW[u], Z[u])
                    pairs(None, X(u, 0), PWT[u], PW[u]).then_inc(signals["sq3"][u], 1)
                for u in slots:
                    on("p8", u)
                    on("z4", u)
                    pairs(None, X(u, 2), PW[u], Z[u]).then_inc(signals["sq4"][u], 1)
                for before, M, products, xs, ts, joined in (("z8", M32, "lv1", "x1", "t1", "lv1b"), ("z32", M64, "lv2", "x2", "t2", "lv2b")):
                    for u in slots:
                        on(before, u)
                        pairs(None, X(u, 0), Z[u])
                        pairs(None, X(u, 1), M[u], Z[u]).then_inc(signals[products][u], 1)
                    for u in slots:
                        on(xs, u)
                        on(ts, u)
                        pairs(None, X(u, 2), PW[u], PWT[u]).then_inc(signals[joined][u], 1)
                for u in slots:
                    on("z64", u)
                    pe.wait_ge(signals["rows_scaled"][u], 3 * n[u])
                    pairs(None, X(u, 0), Z[u], VB[u])
                    pairs(None, X(u, 1), KBE[u], Z[u]).then_inc(signals["uw_raw"][u], 1)
                for u in slots:
                    on("w_ready", u)
                    pe.wait_ge(signals["state_done"][1 - u], n[u] + (u == 0))
                    for h in range(HEADS):
                        m, half = h // 2, h % 2
                        last = nc.tensor.matmul(WS[half * CH:(half + 1) * CH, m * P:(m + 1) * P], WT[u][:, h * CH:(h + 1) * CH],
                                                S[:, h, :], start=True, stop=True)
                    last.then_inc(signals["ws_raw"][u], 1)
                    pe.wait_ge(signals["qd_ready"][u], 2 * n[u])
                    for m in range(PAIRS):
                        cs = slice(m * P, (m + 1) * P)
                        for half in range(2):
                            h = 2 * m + half
                            nc.tensor.matmul(X(u, 2)[half * CH:(half + 1) * CH, cs], QD[u][:, h * CH:(h + 1) * CH], S[:, h, :],
                                             start=True, stop=False, skip_group_check=True)
                        if m == 0:
                            on("vn_ready", u)
                        last = nc.tensor.matmul(X(u, 2)[:, cs], AT_T[u][:, cs], VN[u][:, cs], start=False, stop=True, skip_group_check=True)
                    last.then_inc(signals["out_raw"][u], 1)
                    for h in range(HEADS):
                        m, rows = h // 2, slice((h % 2) * CH, (h % 2 + 1) * CH)
                        last = nc.tensor.matmul(X(u, h % 2)[:, m * P:(m + 1) * P], KD[u][rows, m * P:(m + 1) * P],
                                                VN[u][rows, m * P:(m + 1) * P], start=True, stop=True)
                    last.then_inc(signals["upd_raw"][u], 1)
            chunks(pe, body)

        @block.scalar
        def _(act):
            def body(c, n, slots):
                on = lambda name, u: act.wait_ge(signals[name][u], n[u])
                for u in slots:
                    on("kv_rows", u)
                    nc.scalar.copy(KR[u][:], X(u, 0)).then_inc(signals["k_copied"][u], 1)
                    nc.scalar.copy(VR[u][:], X(u, 1)).then_inc(signals["v_copied"][u], 1)
                for u in slots:
                    on("diff_ready", u)
                    nc.scalar.activation(ECB[u][:], X(u, 2), ACT.Exp)
                    nc.scalar.activation(E1[u][:], E1[u][:], ACT.Exp)
                    nc.scalar.activation(E2[u][:], E2[u][:], ACT.Exp, scale=-1.0)
                    nc.scalar.activation(EC[u][:], CUM[u][:, 0:PAIRS], ACT.Exp)
                    nc.scalar.activation(KS[u][:], KS[u][:], ACT.Exp).then_inc(signals["exp_ready"][u], 1)
                for src, done in (("sq1", "p2"), ("sq2", "p4"), ("sq3", "p8")):
                    for u in slots:
                        on(src, u)
                        nc.scalar.copy(PW[u][:], X(u, 0)).then_inc(signals[done][u], 1)
                for src, done in (("lv1", "x1"), ("lv2", "x2")):
                    for u in slots:
                        on(src, u)
                        nc.scalar.copy(PW[u][:], X(u, 0)).then_inc(signals[done][u], 1)
                for u in slots:
                    on("uw_raw", u)
                    nc.scalar.copy(WT[u][:], X(u, 1)).then_inc(signals["w_ready"][u], 1)
                for u in slots:
                    on("out_raw", u)
                    if slots == (0, 1):
                        act.wait_ge(o_out[u], 16 * n[0])
                    nc.scalar.copy(O[u][:], X(u, 2)).then_inc(signals["o_ready"][u], 1)
                    if slots == (0, 1):
                        on("o_ready", u)
                        act.dma_start(io["o_rows"][bass.ds(c + u - 1, 1)].rearrange("a p e -> (a p) e"), O[u][:]).then_inc(o_out[u], 16)
            for u in range(2):
                act.sem_inc(o_out[u], 16)
            chunks(act, body)
            for u in range(2):
                act.wait_ge(o_out[u], 16 * ((N_CHUNKS - 1) // 2 + 1))

        @block.vector
        def _(dve):
            ch = Chain(dve, own)
            tt = nc.vector.tensor_tensor
            for u in range(2):
                dve.sem_inc(signals["state_done"][u], 1)
            dve.wait_ge(zeroed, 5)

            def body(c, n, slots):
                on = lambda name, u: dve.wait_ge(signals[name][u], n[u])
                over_pairs = lambda m: m[:].unsqueeze(1).to_broadcast([P, PAIRS, P])
                wide = lambda s: s.unsqueeze(2).to_broadcast([P, PAIRS, P])
                for u in slots:
                    dve.wait_ge(loaded[u], 80 * n[u])
                    for half in range(2):
                        rows = slice(half * CH, (half + 1) * CH)
                        of_pair = lambda c0: BG[u][rows, c0:c0 + 8].rearrange("p (m e) -> p e m", e=2)[:, half, :]
                        nc.vector.tensor_copy(BP[u][rows, :], of_pair(0))
                        last = nc.vector.tensor_copy(GP[u][rows, :], of_pair(8))
                    last.then_inc(signals["gates_in"][u], 1)
                for u in slots:
                    on("decay_raw", u)
                    nc.vector.tensor_copy(CUM[u][:], X(u, 0)[:, 0:2 * PAIRS]).then_inc(signals["cum_ready"][u], 1)
                    on("cum_ready", u)
                    cum, whole = CUM[u][:, 0:PAIRS], CUM[u][:, PAIRS:]
                    tt(KS[u][:], whole, cum, ALU.subtract)
                    ch.step(tt(pair3(E2[u][:]), pair3(X(u, 2)), wide(cum), ALU.subtract))
                    nc.vector.tensor_scalar(E1[u][:], E2[u][:], 0.0, None, ALU.min)
                    nc.vector.tensor_scalar(E2[u][:], E2[u][:], 0.0, None, ALU.max).then_inc(signals["diff_ready"][u], 1)
                for u in slots:
                    on("exp_ready", u)
                    ch.step(tt(pair3(E2[u][:]), pair3(E2[u][:]), over_pairs(k["lower"]), ALU.mult))
                    ch.step(tt(pair3(E2[u][:]), pair3(E2[u][:]), wide(BP[u][:]), ALU.mult))
                    on("grams", u)
                    tt(A[u][:], X(u, 0), E2[u][:], ALU.mult).then_inc(signals["a_ready"][u], 1)
                    on("masked1", u)
                    tt(AT_T[u][:], X(u, 1), E1[u][:], ALU.mult).then_inc(signals["attn_ready"][u], 1)
                    on("a_ready", u)
                    tt(pair3(Dm[u][:]), pair3(A[u][:]), over_pairs(k["in16"]), ALU.mult)
                    ch.step(tt(pair3(M32[u][:]), pair3(A[u][:]), over_pairs(k["in32"]), ALU.mult))
                    tt(M64[u][:], A[u][:], M32[u][:], ALU.subtract)
                    ch.step(tt(M32[u][:], M32[u][:], Dm[u][:], ALU.subtract))
                for u in slots:
                    on("at_raw", u)
                    ch.step(tt(pair3(DT[u][:]), pair3(X(u, 2)), over_pairs(k["in16"]), ALU.mult))
                    tt(pair3(Z[u][:]), over_pairs(k["ident"]), pair3(DT[u][:]), ALU.subtract).then_inc(signals["d_ready"][u], 1)
                for u in slots:
                    on("sq1", u)
                    nc.vector.tensor_copy(PWT[u][:], X(u, 1)).then_inc(signals["p2t"][u], 1)
                for u in slots:
                    on("sq2", u)
                    nc.vector.tensor_copy(PWT[u][:], X(u, 1)).then_inc(signals["p4t"][u], 1)
                    tt(Z[u][:], X(u, 2), Z[u][:], ALU.add).then_inc(signals["z2"][u], 1)
                for src, done in (("sq3", "z4"), ("sq4", "z8")):
                    for u in slots:
                        on(src, u)
                        tt(Z[u][:], X(u, 2), Z[u][:], ALU.add).then_inc(signals[done][u], 1)
                for products, ts, joined, done in (("lv1", "t1", "lv1b", "z32"), ("lv2", "t2", "lv2b", "z64")):
                    for u in slots:
                        on(products, u)
                        nc.vector.tensor_copy(PWT[u][:], X(u, 1)).then_inc(signals[ts][u], 1)
                    for u in slots:
                        on(joined, u)
                        tt(Z[u][:], Z[u][:], X(u, 2), ALU.subtract).then_inc(signals[done][u], 1)
                for u in slots:
                    on("uw_raw", u)
                    nc.vector.tensor_copy(U[u][:], X(u, 0)).then_inc(signals["u_ready"][u], 1)
                for u in slots:
                    on("ws_raw", u)
                    on("u_ready", u)
                    tt(VN[u][:], U[u][:], WS, ALU.subtract).then_inc(signals["vn_ready"][u], 1)
                    on("upd_raw", u)
                    whole = ECB[u][:].rearrange("p (h t) -> p h t", t=CH)[:, :, CH - 1:CH].to_broadcast([P, HEADS, HD])
                    ch.step(tt(S[:], S[:], whole, ALU.mult))
                    on("o_ready", u)
                    by_half = S[:].rearrange("p (m b) e -> p b m e", b=2)
                    tt(by_half, by_half, BANK[:, 3 * u:3 * u + 2, :].rearrange("p b (m e) -> p b m e", e=HD), ALU.add).then_inc(signals["state_done"][u], 1)
                ch.restart()
            chunks(dve, body)


def split_on_pool(nc, pool, raw, hi, lo, hi_ready, count, lo_ready, passed=None):
    if passed is not None:
        pool.sem_inc(passed, 1)
    nc.gpsimd.tensor_copy(hi, raw).then_inc(hi_ready, 1)
    pool.wait_ge(hi_ready, count)
    return nc.gpsimd.tensor_tensor(lo, raw, hi.bitcast(F32), ALU.subtract).then_inc(lo_ready, 1)


def branch_phase(nc, k, io):
    NG, NC = POOL_GROUPS, SEQ // CHUNK
    LEAD = max(POOL_WINDOWS)
    HALVES = SEQ // 512
    with Phase(nc, "branch") as ph:
        oT = [ph.sb(f"oT_{p}", [P, HEADS, SEQ], F32R) for p in ("hi", "lo")]
        yp = [ph.sb(f"yp_{p}", [P, NG, SEQ], F32R) for p in ("hi", "lo")]
        with ExitStack() as first_scope:
            ph1 = Phase(nc, "brin")
            first_scope.enter_context(ph1)
            XP = [ph1.sb(f"xp{u}", [P, LEAD + T]) for u in range(2)]
            SA, SB = ph1.sb("sa", [P, LEAD + T]), ph1.sb("sb", [P, LEAD + T])
            PL = ph1.sb("pooled", [P, SEQ])
            PLs = [ph1.sb(f"pooled_{p}", [P, SEQ], F32R) for p in ("hi", "lo")]
            PWr = ph1.sb("pool_w", [P, NG, P])
            PWs = [ph1.sb(f"pool_w_{p}", [P, NG, P], F32R) for p in ("hi", "lo")]
            scale = ph1.sb("pool_scale", [P, NG])
            YP = ph1.sb("yp", [P, SEQ])
            OR = [ph1.sb(f"or{u}", [P, PAIRS * HD]) for u in range(2)]
            ON = [ph1.sb(f"on{u}", [P, PAIRS * HD]) for u in range(2)]
            ZC = [ph1.sb(f"zc{u}", [P, HEADS, CHUNK]) for u in range(2)]
            OZ = [ph1.sb(f"oz{u}", [P, HEADS, CHUNK]) for u in range(2)]
            SQ = ph1.sb("sq", [P, PAIRS * HD])
            ms, root = ph1.sb("ms", [P, PAIRS]), ph1.sb("root", [P, PAIRS])
            MP = ph1.ps("mixed", [P, HALVES, 512])
            TP = [ph1.ps(f"t{u}", [P, PAIRS * P]) for u in range(2)]
            consts_in, pads = ph1.sem("consts_in"), ph1.sem("pads")
            xp_in, o_in = ph1.sems("xp_in"), ph1.sems("o_in")
            names = ("pooled", "pooled_hi", "pooled_lo", "pw_hi", "pw_lo", "mixed", "yp_ready", "yp_hi", "yp_lo",
                     "squared", "ms_ready", "root_ready", "on_ready", "t_ready", "oz_ready", "o_hi", "o_lo")
            sig = {n: ph1.sem(n) for n in names}
            own = ph1.sem("dve_own")
            block = ph1.block()

            @block.sync
            def _(sp):
                sp.dma_start(PWr[:], io["pool_w"].rearrange("p (g c) -> p g c", g=NG)).then_inc(consts_in, 16)
                sp.dma_start(scale[:], io["pool_scale"]).then_inc(consts_in, 16)
                for g in range(NG):
                    if g >= 2:
                        sp.wait_ge(sig["pooled"], g - 1)
                    sp.dma_start(XP[g % 2][:, LEAD:], io["proj"][BLK_POOL + g]).then_inc(xp_in[g % 2], 16)
                with sp.Fori(0, NC // 2) as r:
                    for u in range(2):
                        n = 2 * r + u
                        sp.wait_ge(sig["oz_ready"], n + 1)
                        sp.dma_start(OR[u][:], io["o_rows"][bass.ds(n, 1)].rearrange("a p e -> (a p) e")).then_inc(o_in[u], 16)
                        sp.dma_start(ZC[u][:], io["proj"][BLK_Z:BLK_Z + HEADS, :, bass.ds(n * CHUNK + N_META, CHUNK)].rearrange("h p t -> p h t")).then_inc(o_in[u], 16)

            @block.gpsimd
            def _(pool):
                for u in range(2):
                    pool.memset(XP[u][:, 0:LEAD], 0.0).then_inc(pads, 1)
                pool.wait_ge(consts_in, 32)
                split_on_pool(nc, pool, PWr[:], PWs[0][:], PWs[1][:], sig["pw_hi"], 1, sig["pw_lo"])

            @block.vector
            def _(dve):
                ch = Chain(dve, own)
                tt = nc.vector.tensor_tensor
                dve.sem_inc(sig["oz_ready"], 2)
                dve.sem_inc(sig["o_lo"], 2)
                dve.wait_ge(pads, 2)
                for g, w in enumerate(POOL_WINDOWS):
                    x = XP[g % 2]
                    dve.wait_ge(xp_in[g % 2], 16 * (g // 2 + 1))
                    src, size = x, 1
                    while size < w:
                        dst = SA if src is not SA else SB
                        first = 2 * size - 1
                        ch.step(tt(dst[:, first:], src[:, first:], src[:, first - size:LEAD + T - size], ALU.add))
                        src, size = dst, 2 * size
                    cols = slice(LEAD + N_META, LEAD + T)
                    if g:
                        dve.wait_ge(sig["pooled_lo"], g)
                    nc.vector.scalar_tensor_tensor(out=PL[:], in0=src[:, cols], scalar=1.0 / w, in1=x[:, cols],
                                                   op0=ALU.mult, op1=ALU.subtract).then_inc(sig["pooled"], 1)
                    dve.wait_ge(sig["pooled_hi"], g + 1)
                    tt(PLs[1][:], PL[:], PLs[0][:].bitcast(F32), ALU.subtract).then_inc(sig["pooled_lo"], 1)
                    dve.wait_ge(sig["yp_hi"], g + 1)
                    tt(yp[1][:, g, :], YP[:], yp[0][:, g, :].bitcast(F32), ALU.subtract).then_inc(sig["yp_lo"], 1)
                ch.restart()
                pairs = lambda t: t[:].rearrange("p (m e) -> p m e", e=HD)
                with dve.Fori(0, NC // 2) as r:
                    for u in range(2):
                        n = 2 * r + u
                        dve.wait_ge(sig["squared"], n + 1)
                        ch.step(nc.vector.tensor_reduce(ms[:], pairs(SQ), AX.X, ALU.add))
                        nc.vector.tensor_scalar(ms[:], ms[:], 1.0 / HD, RMS_EPS, ALU.mult, ALU.add).then_inc(sig["ms_ready"], 1)
                        dve.wait_ge(sig["root_ready"], n + 1)
                        ch.step(nc.vector.reciprocal(root[:], root[:]))
                        dve.wait_ge(sig["oz_ready"], n + 1)
                        tt(pairs(ON[u]), pairs(OR[u]), root[:].unsqueeze(2).to_broadcast([P, PAIRS, HD]), ALU.mult).then_inc(sig["on_ready"], 1)
                        dve.wait_ge(sig["t_ready"], n + 1)
                        dve.wait_ge(sig["o_lo"], n + 1)
                        tt(OZ[u][:].rearrange("p h t -> p (h t)"), TP[u][:], ZC[u][:].rearrange("p h t -> p (h t)"), ALU.mult).then_inc(sig["oz_ready"], 1)
                        dve.wait_ge(sig["o_hi"], n + 1)
                        cols = bass.ds(n * CHUNK, CHUNK)
                        tt(oT[1][:, :, cols], OZ[u][:], oT[0][:, :, cols].bitcast(F32), ALU.subtract).then_inc(sig["o_lo"], 1)
                        ch.restart()

            @block.scalar
            def _(act):
                act.wait_ge(consts_in, 32)
                for g in range(NG):
                    act.wait_ge(sig["pooled"], g + 1)
                    if g:
                        act.wait_ge(sig["mixed"], g)
                    nc.scalar.copy(PLs[0][:], PL[:]).then_inc(sig["pooled_hi"], 1)
                    act.wait_ge(sig["mixed"], g + 1)
                    if g:
                        act.wait_ge(sig["yp_lo"], g)
                    nc.scalar.mul(YP[:].rearrange("p (a b) -> p a b", a=HALVES), MP[:], scale[:, g:g + 1]).then_inc(sig["yp_ready"], 1)
                    act.wait_ge(sig["yp_ready"], g + 1)
                    nc.scalar.copy(yp[0][:, g, :], YP[:]).then_inc(sig["yp_hi"], 1)
                with act.Fori(0, NC // 2) as r:
                    for u in range(2):
                        n = 2 * r + u
                        act.wait_ge(o_in[u], 32 * (r + 1))
                        nc.scalar.activation(SQ[:], OR[u][:], ACT.Square).then_inc(sig["squared"], 1)
                        act.wait_ge(sig["ms_ready"], n + 1)
                        nc.scalar.activation(root[:], ms[:], ACT.Sqrt).then_inc(sig["root_ready"], 1)
                        act.wait_ge(sig["oz_ready"], n + 3)
                        nc.scalar.copy(oT[0][:, :, bass.ds(n * CHUNK, CHUNK)], OZ[u][:]).then_inc(sig["o_hi"], 1)

            @block.tensor
            def _(pe):
                pe.wait_ge(sig["pw_lo"], 1)
                for g in range(NG):
                    pe.wait_ge(sig["pooled_lo"], g + 1)
                    if g:
                        pe.wait_ge(sig["yp_ready"], g)
                    for c in range(HALVES):
                        cs = slice(c * 512, (c + 1) * 512)
                        last = mm3(nc, MP[:, c, :], (PWs[0][:, g, :], PWs[1][:, g, :]), (PLs[0][:, cs], PLs[1][:, cs]))
                    last.then_inc(sig["mixed"], 1)
                with pe.Fori(0, NC // 2) as r:
                    for u in range(2):
                        n = 2 * r + u
                        pe.wait_ge(sig["on_ready"], n + 1)
                        pe.wait_ge(sig["oz_ready"], n + 1)
                        for m in range(PAIRS):
                            last = nc.tensor.transpose(TP[u][:, m * P:(m + 1) * P], ON[u][:, m * P:(m + 1) * P], k["ident"][:])
                        last.then_inc(sig["t_ready"], 1)

        ph2 = Phase(nc, "brout")
        with ph2:
            NB = HEADS + NG
            Wr = [ph2.sb(f"w{u}", [P, NB, P]) for u in range(2)]
            Ws = [[ph2.sb(f"w{p}{u}", [P, NB, P], F32R) for p in ("hi", "lo")] for u in range(2)]
            GP = [ph2.sb(f"gp{u}", [P, SEQ]) for u in range(2)]
            GD = [ph2.sb(f"gd{u}", [P, SEQ]) for u in range(2)]
            YA = [ph2.ps(f"ya{u}", [P, HALVES, 512]) for u in range(2)]
            YB = [ph2.ps(f"yb{u}", [P, HALVES, 512]) for u in range(2)]
            loaded, stored = ph2.sems("loaded"), ph2.sems("stored")
            w_hi, w_lo, passed, products, merged = (ph2.sem(n) for n in ("w_hi", "w_lo", "passed", "products", "merged"))
            own = ph2.sem("dve_own")
            block = ph2.block()

            @block.sync
            def _(sp):
                with sp.Fori(0, DB // 2) as r:
                    for u in range(2):
                        n = 2 * r + u
                        sp.wait_ge(w_lo, n + 1)
                        sp.dma_start(Wr[u][:], io["w_branches"][bass.ds(n, 1)].rearrange("a p (b c) -> (a p) b c", c=P)).then_inc(loaded[u], 16)
                        sp.wait_ge(stored[u], 16 * (r + 1))
                        sp.dma_start(GP[u][:], io["proj"][bass.ds(n + BLK_GATE, 1), :, N_META:T].rearrange("a p t -> (a p) t")).then_inc(loaded[u], 16)
                        sp.dma_start(GD[u][:], io["proj"][bass.ds(n + BLK_GATE + DB, 1), :, N_META:T].rearrange("a p t -> (a p) t")).then_inc(loaded[u], 16)

            @block.gpsimd
            def _(pool):
                pool.sem_inc(w_lo, 2)
                with pool.Fori(0, DB // 2) as r:
                    for u in range(2):
                        n = 2 * r + u
                        pool.wait_ge(loaded[u], 48 * (r + 1))
                        pool.wait_ge(products, n + 1)
                        split_on_pool(nc, pool, Wr[u][:], Ws[u][0][:], Ws[u][1][:], w_hi, n + 1, w_lo, passed)

            @block.tensor
            def _(pe):
                pe.sem_inc(products, 2)
                with pe.Fori(0, DB // 2) as r:
                    for u in range(2):
                        n = 2 * r + u
                        pe.wait_ge(w_lo, n + 3)
                        pe.wait_ge(merged, n + 1)
                        for dst, src, b0, count in ((YA[u], yp, HEADS, NG), (YB[u], oT, 0, HEADS)):
                            for b in range(count):
                                for c in range(HALVES):
                                    cs = slice(c * 512, (c + 1) * 512)
                                    last = mm3(nc, dst[:, c, :], (Ws[u][0][:, b0 + b, :], Ws[u][1][:, b0 + b, :]),
                                               (src[0][:, b, cs], src[1][:, b, cs]), b == 0, b == count - 1)
                        last.then_inc(products, 1)

            @block.vector
            def _(dve):
                ch = Chain(dve, own)
                dve.sem_inc(merged, 2)
                with dve.Fori(0, DB // 2) as r:
                    for u in range(2):
                        n = 2 * r + u
                        halves = lambda t: t[:].rearrange("p (a b) -> p a b", a=HALVES)
                        dve.wait_ge(loaded[u], 48 * (r + 1))
                        dve.wait_ge(products, n + 3)
                        ch.mark(nc.vector.tensor_tensor(halves(GP[u]), YA[u][:], halves(GP[u]), ALU.mult))
                        ch.step(nc.vector.tensor_tensor(halves(GD[u]), YB[u][:], halves(GD[u]), ALU.mult))
                        nc.vector.tensor_tensor(GP[u][:], GP[u][:], GD[u][:], ALU.add).then_inc(merged, 1)
                        ch.restart()

            @block.scalar
            def _(act):
                for u in range(2):
                    act.sem_inc(stored[u], 16)
                with act.Fori(0, DB // 2) as r:
                    for u in range(2):
                        n = 2 * r + u
                        act.wait_ge(merged, n + 3)
                        act.dma_start(io["merged"][bass.ds(n, 1)].rearrange("a p t -> (a p) t"), GP[u][:]).then_inc(stored[u], 16)
                for u in range(2):
                    act.wait_ge(stored[u], 16 * (DB // 2 + 1))


def mix_phase(nc, k, io):
    NH = D // 512
    with Phase(nc, "mix") as ph:
        Wr = [ph.sb(f"w{u}", [P, D]) for u in range(2)]
        Ws = [ph.sb(f"w_{p}", [P, DB, D], F32R) for p in ("hi", "lo")]
        gain, bias = ph.sb("gain", [P, D]), ph.sb("bias", [P, D])
        MR = [ph.sb(f"m{u}", [P, DB, P]) for u in range(2)]
        MS = [[ph.sb(f"m{p}{u}", [P, DB, P], F32R) for p in ("hi", "lo")] for u in range(2)]
        HR = [ph.sb(f"h{u}", [P, D]) for u in range(2)]
        HT = [ph.sb(f"hT{u}", [P, DB, P]) for u in range(2)]
        stats, mv = ph.sb("stats", [P, NH, 6]), ph.sb("mv", [P, 2])
        std, rstd = ph.sb("std", [P, 1]), ph.sb("rstd", [P, 1])
        MX = [ph.ps(f"mx{u}", [P, NH, 512]) for u in range(2)]
        TP = [ph.ps(f"t{u}", [P, DB, P]) for u in range(2)]
        consts_in = ph.sem("consts_in")
        w_in, m_in, h_in, rows_out, t_out = (ph.sems(n) for n in ("w_in", "m_in", "h_in", "rows_out", "t_out"))
        sig = {n: ph.sem(n) for n in ("w_hi", "w_lo", "m_hi", "m_lo", "passed", "mixed", "summed", "var_ready", "std_ready", "h_ready", "t_ready", "t_copied")}
        own = ph.sem("dve_own")
        block = ph.block()

        def tiles(eng, body):
            with eng.Fori(0, XT // 2) as r:
                for u in range(2):
                    body(2 * r + u, r, u)

        @block.sync
        def _(sp):
            sp.dma_start(gain[:], row_bcast(io["ln1_g"])).then_inc(consts_in, 16)
            sp.dma_start(bias[:], row_bcast(io["ln1_b"])).then_inc(consts_in, 16)
            for b in range(DB):
                if b >= 2:
                    sp.wait_ge(sig["w_lo"], b - 1)
                sp.dma_start(Wr[b % 2][:], io["w_out"][b * P:(b + 1) * P, :]).then_inc(w_in[b % 2], 16)

            def body(n, r, u):
                sp.wait_ge(sig["m_lo"], n + 1)
                sp.dma_start(MR[u][:], io["merged"][:, :, bass.ts(n, P)].rearrange("b p t -> p b t")).then_inc(m_in[u], 16)
                sp.wait_ge(rows_out[u], 16 * (r + 1))
                sp.wait_ge(sig["t_ready"], n + 1)
                sp.dma_start(HR[u][:], io["h_rows"][bass.ts(n, P), :]).then_inc(h_in[u], 16)
            tiles(sp, body)

        @block.gpsimd
        def _(pool):
            pool.sem_inc(sig["m_lo"], 2)
            for b in range(DB):
                pool.wait_ge(w_in[b % 2], 16 * (b // 2 + 1))
                split_on_pool(nc, pool, Wr[b % 2][:], Ws[0][:, b, :], Ws[1][:, b, :], sig["w_hi"], b + 1, sig["w_lo"])

            def body(n, r, u):
                pool.wait_ge(m_in[u], 16 * (r + 1))
                pool.wait_ge(sig["mixed"], n + 1)
                split_on_pool(nc, pool, MR[u][:], MS[u][0][:], MS[u][1][:], sig["m_hi"], n + 1, sig["m_lo"], sig["passed"])
            tiles(pool, body)

        @block.tensor
        def _(pe):
            pe.sem_inc(sig["mixed"], 2)
            pe.sem_inc(sig["t_ready"], 2)
            pe.wait_ge(sig["w_lo"], DB)

            def body(n, r, u):
                pe.wait_ge(sig["m_lo"], n + 3)
                pe.wait_ge(sig["summed"], n + 1)
                for c in range(NH):
                    for b in range(DB):
                        last = mm3(nc, MX[u][:, c, :], (MS[u][0][:, b, :], MS[u][1][:, b, :]),
                                   (Ws[0][:, b, c * 512:(c + 1) * 512], Ws[1][:, b, c * 512:(c + 1) * 512]), b == 0, b == DB - 1)
                last.then_inc(sig["mixed"], 1)
                pe.wait_ge(sig["h_ready"], n + 1)
                pe.wait_ge(sig["t_copied"], n + 1)
                for b in range(DB):
                    last = nc.tensor.transpose(TP[u][:, b, :], HR[u][:, b * P:(b + 1) * P], k["ident"][:])
                last.then_inc(sig["t_ready"], 1)
            tiles(pe, body)

        @block.vector
        def _(dve):
            ch = Chain(dve, own)
            dve.sem_inc(sig["summed"], 2)
            dve.wait_ge(consts_in, 32)

            def body(n, r, u):
                h = HR[u][:]
                halves = h.rearrange("p (a b) -> p a b", a=NH)
                dve.wait_ge(h_in[u], 16 * (r + 1))
                dve.wait_ge(sig["mixed"], n + 3)
                nc.vector.scalar_tensor_tensor(out=halves, in0=halves, scalar=ALPHA, in1=MX[u][:], op0=ALU.mult, op1=ALU.add).then_inc(sig["summed"], 1)
                dve.wait_ge(sig["summed"], n + 3)
                for s in range(NH):
                    ch.mark(nc.vector.bn_stats(stats[:, s, :], h[:, s * 512:(s + 1) * 512]))
                ch.wait()
                ch.step(nc.vector.bn_aggr(mv[:], stats[:]))
                nc.vector.tensor_scalar(std[:], mv[:, 1:2], LN_EPS, None, ALU.add).then_inc(sig["var_ready"], 1)
                dve.wait_ge(sig["std_ready"], n + 1)
                ch.step(nc.vector.reciprocal(rstd[:], std[:]))
                ch.step(nc.vector.tensor_scalar(h, h, mv[:, 0:1], rstd[:], ALU.subtract, ALU.mult))
                ch.step(nc.vector.tensor_tensor(h, h, gain[:], ALU.mult))
                nc.vector.tensor_tensor(h, h, bias[:], ALU.add).then_inc(sig["h_ready"], 1)
                ch.restart()
            tiles(dve, body)

        @block.scalar
        def _(act):
            act.sem_inc(sig["t_copied"], 2)
            for u in range(2):
                act.sem_inc(rows_out[u], 16)
                act.sem_inc(t_out[u], 16)

            def body(n, r, u):
                act.wait_ge(sig["var_ready"], n + 1)
                nc.scalar.activation(std[:], std[:], ACT.Sqrt).then_inc(sig["std_ready"], 1)
                act.wait_ge(sig["h_ready"], n + 1)
                act.dma_start(io["h1_rows"][bass.ts(n, P), :], HR[u][:]).then_inc(rows_out[u], 16)
                act.wait_ge(sig["t_ready"], n + 3)
                act.wait_ge(t_out[u], 16 * (r + 1))
                nc.scalar.copy(HT[u][:], TP[u][:]).then_inc(sig["t_copied"], 1)
                act.wait_ge(sig["t_copied"], n + 3)
                act.dma_start(io["h1_t"][:, :, bass.ts(n, P)].rearrange("b p t -> p b t"), HT[u][:]).then_inc(t_out[u], 16)
            tiles(act, body)
            for u in range(2):
                act.wait_ge(rows_out[u], 16 * (XT // 2 + 1))
                act.wait_ge(t_out[u], 16 * (XT // 2 + 1))


def query_phase(nc, k, io):
    NQ = 2 * HEADS
    K = TOPK
    HALVES = SEQ // 512
    with Phase(nc, "query") as ph:
        XS = [ph.sb(f"x_{p}", [P, DB, SEQ], F32R) for p in ("hi", "lo")]
        XR = [ph.sb(f"xr{u}", [P, SEQ]) for u in range(2)]
        W = [ph.sb(f"w{u}", [P, DB, P]) for u in range(2)]
        WS = [[ph.sb(f"w{p}{u}", [P, DB, P], F32R) for p in ("hi", "lo")] for u in range(2)]
        KEYS = ph.sb("keys", [P, NQ, P])
        QT = [ph.sb(f"q{u}", [P, SEQ]) for u in range(2)]
        SC = [ph.sb(f"s{u}", [P, XT, P]) for u in range(2)]
        REST = ph.sb("rest", [P, XT, P])
        V, I, IF = ph.sb("v", [P, 2, XT, K]), ph.sb("i", [P, 2, XT, K], U32), ph.sb("i_half", [P, 2, XT, K], F16)
        CAND, CREST = ph.sb("cand", [P, XT, K * K]), ph.sb("cand_rest", [P, XT, K * K])
        SO, CI = ph.sb("score", [P, XT, K]), ph.sb("ci", [P, XT, K], U32)
        AB, ABF = ph.sb("ab_int", [P, 2, XT, K], U32), ph.sb("ab_half", [P, 2, XT, K], F16)
        EQ = ph.sb("eq", [P, 2, XT, K, K], F16)
        TOP, SUM = ph.sb("top", [P, XT]), ph.sb("sum", [P, XT])
        iota_i, iota = ph.sb("iota_int", [P, K, K], mybir.dt.int32), ph.sb("iota", [P, K, K], F16)
        SEL = k["sel"]
        QP = [ph.ps(f"qp{u}", [P, HALVES, 512]) for u in range(2)]
        SP_ = [ph.ps(f"sp{u}", [P, XT, P]) for u in range(2)]
        keys_in = ph.sem("keys_in")
        x_in, w_in = ph.sems("x_in"), ph.sems("w_in")
        sig = {n: ph.sem(n) for n in ("x_hi", "x_lo", "w_hi", "w_lo", "passed", "q_raw", "q_ready", "s_raw", "s_ready", "s_read",
                                      "places", "picked", "score_ready", "exp_ready", "iota_ready", "dve_passed")}
        own = ph.sem("dve_own")
        block = ph.block()

        @block.sync
        def _(sp):
            for b in range(DB):
                if b >= 2:
                    sp.wait_ge(sig["x_lo"], b - 1)
                sp.dma_start(XR[b % 2][:], io["h1_t"][b]).then_inc(x_in[b % 2], 16)
            sp.dma_start(KEYS[:], io["keys"].rearrange("n c e -> c n e")).then_inc(keys_in, 16)
            with sp.Fori(0, NQ // 2) as r:
                for u in range(2):
                    sp.wait_ge(sig["w_lo"], 2 * r + u + 1)
                    sp.dma_start(W[u][:], io["wq_blocks"][bass.ds(2 * r + u, 1)].rearrange("a p (b c) -> (a p) b c", c=P)).then_inc(w_in[u], 16)

        @block.gpsimd
        def _(pool):
            pool.sem_inc(sig["w_lo"], 2)
            nc.gpsimd.iota(iota_i[:], pattern=[[1, K], [0, K]], base=0, channel_multiplier=0).then_inc(sig["iota_ready"], 1)

            def split(n, u, r_u):
                pool.wait_ge(w_in[u], 16 * r_u)
                pool.wait_ge(sig["q_raw"], n + 1)
                split_on_pool(nc, pool, W[u][:], WS[u][0][:], WS[u][1][:], sig["w_hi"], n + 1, sig["w_lo"], sig["passed"])

            def pick(h):
                for s in range(2):
                    pool.wait_ge(sig["places"], 2 * h + s + 1)
                    nc.gpsimd.tensor_tensor(EQ[:, s], EQ[:, s], IF[:, s].unsqueeze(3).to_broadcast([P, XT, K, K]), ALU.mult).then_inc(sig["picked"], 1)

            for n in range(4):
                split(n, n % 2, n // 2 + 1)
            with pool.Fori(0, HEADS - 2) as h:
                for u in range(2):
                    split(2 * h + 4 + u, u, h + 3)
                pick(h)
            pick(HEADS - 2)
            pick(HEADS - 1)

        @block.tensor
        def _(pe):
            pe.sem_inc(sig["q_raw"], 2)
            pe.wait_ge(sig["x_lo"], DB)
            pe.wait_ge(keys_in, 16)

            def queries(n, u):
                pe.wait_ge(sig["w_lo"], n + 3)
                pe.wait_ge(sig["q_ready"], n + 1)
                for b in range(DB):
                    for c in range(HALVES):
                        cs = slice(c * 512, (c + 1) * 512)
                        last = mm3(nc, QP[u][:, c, :], (WS[u][0][:, b, :], WS[u][1][:, b, :]), (XS[0][:, b, cs], XS[1][:, b, cs]), b == 0, b == DB - 1)
                last.then_inc(sig["q_raw"], 1)

            def scores(n, u):
                pe.wait_ge(sig["q_ready"], n + 3)
                pe.wait_ge(sig["s_ready"], n + 1)
                for t in range(XT):
                    keys = KEYS[:, bass.ds(n, 1), :].rearrange("p a e -> p (a e)")
                    last = nc.tensor.matmul(SP_[u][:, t, :], QT[u][:, t * P:(t + 1) * P], keys, start=True, stop=True)
                last.then_inc(sig["s_raw"], 1)

            queries(0, 0)
            with pe.Fori(0, NQ // 2 - 1) as r:
                queries(2 * r + 1, 1)
                scores(2 * r, 0)
                queries(2 * r + 2, 0)
                scores(2 * r + 1, 1)
            queries(NQ - 1, 1)
            scores(NQ - 2, 0)
            scores(NQ - 1, 1)

        @block.scalar
        def _(act):
            act.sem_inc(sig["q_ready"], 2)
            for b in range(DB):
                act.wait_ge(x_in[b % 2], 16 * (b // 2 + 1))
                nc.scalar.copy(XS[0][:, b, :], XR[b % 2][:]).then_inc(sig["x_hi"], 1)

            def copy(n, u):
                act.wait_ge(sig["q_raw"], n + 3)
                act.wait_ge(sig["s_raw"], n + 1)
                nc.scalar.copy(QT[u][:].rearrange("p (a b) -> p a b", a=HALVES), QP[u][:]).then_inc(sig["q_ready"], 1)

            def take(n, u):
                act.wait_ge(sig["s_raw"], n + 3)
                act.wait_ge(sig["s_read"], n + 1)
                nc.scalar.copy(SC[u][:], SP_[u][:]).then_inc(sig["s_ready"], 1)

            def exp(h):
                act.wait_ge(sig["score_ready"], h + 1)
                nc.scalar.activation(SO[:], SO[:], ACT.Exp).then_inc(sig["exp_ready"], 1)

            def body(h):
                copy(2 * h + 1, 1)
                take(2 * h, 0)
                copy(2 * h + 2, 0)
                take(2 * h + 1, 1)

            copy(0, 0)
            body(0)
            with act.Fori(1, HEADS - 1) as h:
                body(h)
                exp(h - 1)
            copy(NQ - 1, 1)
            take(NQ - 2, 0)
            take(NQ - 1, 1)
            exp(HEADS - 2)
            exp(HEADS - 1)

        @block.vector
        def _(dve):
            ch = Chain(dve, own)
            tt, ts = nc.vector.tensor_tensor, nc.vector.tensor_scalar
            dve.sem_inc(sig["s_raw"], 2)
            dve.sem_inc(sig["s_ready"], 2)
            dve.sem_inc(sig["s_read"], 2)
            for b in range(DB):
                dve.wait_ge(sig["x_hi"], b + 1)
                nc.vector.tensor_tensor(XS[1][:, b, :], XR[b % 2][:], XS[0][:, b, :].bitcast(F32), ALU.subtract).then_inc(sig["x_lo"], 1)

            def top16(src, rest, v, i):
                for t in range(XT):
                    ch.mark(nc.vector.max(v[:, t, 0:8], src[:, t, :]))
                ch.wait()
                for t in range(XT):
                    ch.mark(nc.vector.max_index(i[:, t, 0:8], v[:, t, 0:8], src[:, t, :]))
                    ch.mark(nc.vector.match_replace(rest[:, t, :], v[:, t, 0:8], src[:, t, :], LOWEST))
                ch.wait()
                for t in range(XT):
                    ch.mark(nc.vector.max(v[:, t, 8:16], rest[:, t, :]))
                ch.wait()
                for t in range(XT):
                    ch.mark(nc.vector.max_index(i[:, t, 8:16], v[:, t, 8:16], rest[:, t, :]))
                ch.wait()

            def keys_of_sides(h):
                for s in range(2):
                    dve.wait_ge(sig["s_ready"], 2 * h + s + 3)
                    dve.sem_inc(sig["dve_passed"], 1)
                    top16(SC[s], REST, V[:, s], I[:, s])
                    dve.sem_inc(sig["s_read"], 1)

            def pairs(h):
                ch.step(tt(CAND[:].rearrange("p t (a b) -> p t a b", a=K), V[:, 0].unsqueeze(3).to_broadcast([P, XT, K, K]),
                           V[:, 1].unsqueeze(2).to_broadcast([P, XT, K, K]), ALU.add))
                top16(CAND, CREST, SO, CI)
                ch.mark(nc.vector.tensor_copy(IF[:], I[:]))
                ch.mark(ts(AB[:, 0], CI[:], 4, None, ALU.logical_shift_right))
                ch.mark(ts(AB[:, 1], CI[:], K - 1, None, ALU.bitwise_and))
                ch.step(nc.vector.tensor_copy(TOP[:], SO[:, :, 0:1].rearrange("p t a -> p (t a)")))
                ch.step(nc.vector.tensor_copy(ABF[:], AB[:]))
                tt(SO[:], SO[:], TOP[:].unsqueeze(2).to_broadcast([P, XT, K]), ALU.subtract).then_inc(sig["score_ready"], 1)
                for s in range(2):
                    tt(EQ[:, s], ABF[:, s].unsqueeze(2).to_broadcast([P, XT, K, K]), iota[:].unsqueeze(1).to_broadcast([P, XT, K, K]), ALU.is_equal).then_inc(sig["places"], 1)

            def select(h):
                slots = bass.ds(h * K, K)
                for s in range(2):
                    dve.wait_ge(sig["picked"], 2 * h + s + 1)
                    ch.mark(nc.vector.tensor_reduce(SEL[:, :, s, slots], EQ[:, s].rearrange("p t a k -> p t k a"), AX.X, ALU.add))
                dve.wait_ge(sig["exp_ready"], h + 1)
                ch.step(nc.vector.tensor_reduce(SUM[:], SO[:], AX.X, ALU.add))
                ch.step(nc.vector.reciprocal(SUM[:], SUM[:]))
                ch.mark(tt(SEL[:, :, 2, slots], SO[:], SUM[:].unsqueeze(2).to_broadcast([P, XT, K]), ALU.mult))

            dve.wait_ge(sig["iota_ready"], 1)
            ch.mark(nc.vector.tensor_copy(iota[:], iota_i[:]))
            keys_of_sides(0)
            pairs(0)
            ch.restart()
            with dve.Fori(1, HEADS) as h:
                keys_of_sides(h)
                select(h - 1)
                ch.wait()
                pairs(h)
                ch.restart()
            select(HEADS - 1)
            ch.wait()


def gates_phase(nc, k, io):
    UNIT = 16
    HALF = UNIT // 2
    ROUNDS = P // UNIT
    GATE_SCALE = 2.0 ** 14
    SEL = k["sel"]
    with Phase(nc, "gates") as ph:
        keys_i, iota = ph.sb("keys_int", [P, P], mybir.dt.int32), ph.sb("iota", [P, P, UNIT], F16)
        IJ = ph.sb("ij_half", [P, 2, SEQ], F16)
        GH = ph.sb("gate_half", [P, 2, SEQ], F16)
        GF = [ph.sb(f"gate{u}", [P, P]) for u in range(2)]
        OH = [ph.sb(f"onehot{u}", [P, 4, P, UNIT], F16) for u in range(2)]
        GS = [ph.sb(f"g{v}", [P, P, P]) for v in range(2)]
        TP = [ph.ps(f"t{u}", [P, 3, P]) for u in range(2)]
        GP = [ph.ps(f"gp{s}", [P, HALF, P]) for s in range(2)]
        g_out = ph.sems("g_out")
        sig = {n: ph.sem(n) for n in ("t_ready", "t_read", "onehots", "g_raw", "g_copied", "iota_ready", "equal")}
        own = ph.sem("dve_own")
        block = ph.block()

        @block.sync
        def _(sp):
            with sp.Fori(0, XT // 2) as r:
                for v in range(2):
                    n = 2 * r + v
                    sp.wait_ge(sig["g_copied"], 2 * ROUNDS * (n + 1) + 2)
                    sp.dma_start(io["g"][bass.ds(n, 1)].rearrange("a i j t -> (a i) j t"), GS[v][:]).then_inc(g_out[v], 16)
            for v in range(2):
                sp.wait_ge(g_out[v], 16 * (XT // 2 + 1))

        @block.gpsimd
        def _(pool):
            nc.gpsimd.iota(keys_i[:], pattern=[[1, P]], base=0, channel_multiplier=0).then_inc(sig["iota_ready"], 1)

        @block.vector
        def _(dve):
            ch = Chain(dve, own)
            tt, ts = nc.vector.tensor_tensor, nc.vector.tensor_scalar
            dve.wait_ge(sig["iota_ready"], 1)
            ch.mark(nc.vector.tensor_copy(iota[:], keys_i[:].unsqueeze(2).to_broadcast([P, P, UNIT])))
            for n in range(XT):
                u, cols = n % 2, slice(n * P, (n + 1) * P)
                dve.wait_ge(sig["t_ready"], n + 1)
                ch.mark(ts(GF[u][:], TP[u][:, 2, :], GATE_SCALE, None, ALU.mult))
                ch.step(nc.vector.tensor_copy(IJ[:, :, cols], TP[u][:, 0:2, :]))
                dve.sem_inc(sig["t_read"], 1)
                ch.step(nc.vector.tensor_copy(GH[:, 0, cols], GF[u][:]))
                ch.mark(tt(GH[:, 1, cols], GF[u][:], GH[:, 0, cols], ALU.subtract))
            ch.wait()
            over_keys = lambda row: row.unsqueeze(1).to_broadcast([P, P, UNIT])
            with dve.Fori(0, XT * ROUNDS // 2) as i:
                for u in range(2):
                    dve.wait_ge(sig["g_raw"], 2 * (2 * i + u) + 2)
                    cols = bass.ds((2 * i + u) * UNIT, UNIT)
                    for s in (1, 0):
                        tt(OH[u][:, s], iota[:], over_keys(IJ[:, s, cols]), ALU.is_equal).then_inc(sig["equal"], 1)
                    dve.wait_ge(sig["equal"], 2 * (2 * i + u) + 1)
                    for s in range(2):
                        last = tt(OH[u][:, 2 + s], OH[u][:, 1], over_keys(GH[:, s, cols]), ALU.mult)
                    last.then_inc(sig["onehots"], 1)

        @block.scalar
        def _(act):
            act.sem_inc(sig["g_copied"], 2)
            for v in range(2):
                act.sem_inc(g_out[v], 16)
            with act.Fori(0, XT // 2) as r:
                for v in range(2):
                    act.wait_ge(g_out[v], 16 * (r + 1))
                    with act.Fori(0, ROUNDS) as i:
                        for s in range(2):
                            act.wait_ge(sig["g_raw"], 2 * ROUNDS * (2 * r + v) + 2 * i + s + 5)
                            nc.scalar.mul(GS[v][:, :, bass.ds(i * UNIT + s * HALF, HALF)].rearrange("p j t -> p t j"), GP[s][:], 1.0 / GATE_SCALE).then_inc(sig["g_copied"], 1)

        @block.tensor
        def _(pe):
            pe.sem_inc(sig["g_raw"], 4)
            for n in range(XT):
                if n >= 2:
                    pe.wait_ge(sig["t_read"], n - 1)
                for s in range(3):
                    last = nc.tensor.transpose(TP[n % 2][:, s, :], SEL[:, n, s, :], k["ident"][:])
                last.then_inc(sig["t_ready"], 1)
            with pe.Fori(0, XT * ROUNDS // 2) as i:
                for u in range(2):
                    done = 2 * i + u
                    pe.wait_ge(sig["onehots"], done + 1)
                    for s in range(2):
                        pe.wait_ge(sig["g_copied"], 2 * done + s + 1)
                        for t in range(HALF):
                            tok = s * HALF + t
                            for q in range(2):
                                last = nc.tensor.matmul(GP[s][:, t, :], OH[u][:, 0, :, tok], OH[u][:, 2 + q, :, tok], start=q == 0, stop=q == 1)
                        last.then_inc(sig["g_raw"], 1)


def experts_phase(nc, k, io, half):
    J = 4
    GROUPS = N_KEYS // J
    HT = 512
    NT = HT // P
    NH = D // 512
    COMBOS = NT * NH
    OUT_BANKS = 4
    with Phase(nc, f"experts{half}") as ph:
        XS = [ph.sb(f"x_{p}", [P, DB, HT], F32R) for p in ("hi", "lo")]
        ACC = ph.sb("acc", [P, NT, D])
        UR = [ph.sb(f"u{s}", [P, DB, P]) for s in range(2)]
        VR = [ph.sb(f"v{s}", [P, D]) for s in range(2)]
        GR = [ph.sb(f"g{s}", [P, NT, P]) for s in range(2)]
        US = [[ph.sb(f"u{p}{s}", [P, DB, P], F32R) for p in ("hi", "lo")] for s in range(2)]
        VS = [[ph.sb(f"v{p}{s}", [P, J, D], F32R) for p in ("hi", "lo")] for s in range(2)]
        AS = [[ph.sb(f"a{p}{s}", [P, J, HT], F32R) for p in ("hi", "lo")] for s in range(2)]
        AC = [ph.sb(f"act{s}", [P, HT]) for s in range(2)]
        gain, bias = ph.sb("gain", [P, D]), ph.sb("bias", [P, D])
        stats, mv, std = ph.sb("stats", [P, NH, 6]), ph.sb("mv", [P, 2]), ph.sb("std", [P, 1])
        HID = [ph.ps(f"hid{s}", [P, HT]) for s in range(2)]
        OUT = [ph.ps(f"out{q}", [P, 512]) for q in range(OUT_BANKS)]
        x_in, u_in, v_in, g_in = (ph.sems(n) for n in ("x_in", "u_in", "v_in", "g_in"))
        start_in, out_stored = ph.sem("start_in"), ph.sem("out_stored")
        names = ("x_hi", "x_lo", "acc_ready", "u_hi", "v_hi", "u_lo", "v_lo", "hid", "gelu", "gated", "a_hi", "a_lo",
                 "out", "out_group", "added", "var_ready", "std_ready", "rows_ready")
        sig = {n: ph.sem(n) for n in names}
        own = ph.sem("dve_own")
        block = ph.block()
        tok = slice(half * HT, (half + 1) * HT)

        def groups(eng, body):
            for p in range(2):
                body(p, 0, p, True)
            with eng.Fori(1, GROUPS // 2) as r:
                for p in range(2):
                    body(2 * r + p, r, p, False)

        @block.sync
        def _(sp):
            sp.dma_start(gain[:], row_bcast(io["ln2_g"])).then_inc(start_in, 16)
            sp.dma_start(bias[:], row_bcast(io["ln2_b"])).then_inc(start_in, 16)
            sp.dma_start(ACC[:], io["h1_rows"][tok, :].rearrange("(n p) d -> p n d", p=P)).then_inc(start_in, 16)
            for q in range(DB // 2):
                if q >= 2:
                    sp.wait_ge(sig["x_lo"], q - 1)
                sp.dma_start(UR[q % 2][:].rearrange("p (a b) c -> p a (b c)", a=2), io["h1_t"][2 * q:2 * q + 2, :, tok].rearrange("b p t -> p b t")).then_inc(x_in[q % 2], 16)
            sp.wait_ge(sig["x_lo"], DB // 2)
            with sp.Fori(0, N_KEYS // 2) as r:
                for s in range(2):
                    m = 2 * r + s
                    sp.wait_ge(sig["u_lo"], m + 1)
                    sp.dma_start(UR[s][:], io["u_blocks"][bass.ds(m, 1)].rearrange("a p (b c) -> (a p) b c", c=P)).then_inc(u_in[s], 16)
                    sp.wait_ge(sig["v_lo"], m + 1)
                    sp.dma_start(VR[s][:], io["v_blocks"][bass.ds(m, 1)].rearrange("a p d -> (a p) d")).then_inc(v_in[s], 16)
            for n in range(NT):
                sp.wait_ge(sig["rows_ready"], n + 1)
                sp.dma_start(io["out"][half * HT + n * P:half * HT + (n + 1) * P, :], ACC[:, n, :]).then_inc(out_stored, 16)
            sp.wait_ge(out_stored, 16 * NT)

        @block.gpsimd
        def _(pool):
            with pool.Fori(0, N_KEYS // (2 * J)) as r:
                for e in range(2 * J):
                    m, s, p, j = 2 * J * r + e, e % 2, e // J, e % J
                    pool.wait_ge(sig["gated"], m + 1)
                    pool.dma_start(GR[s][:], io["g"][half * NT:(half + 1) * NT, :, bass.ds(m, 1), :].rearrange("n i j t -> i (n j) t")).then_inc(g_in[s], 16)
                    pool.wait_ge(sig["v_hi"], m + 1)
                    nc.gpsimd.tensor_tensor(VS[p][1][:, j, :], VR[s][:], VS[p][0][:, j, :].bitcast(F32), ALU.subtract).then_inc(sig["v_lo"], 1)

        @block.tensor
        def _(pe):
            pe.sem_inc(sig["hid"], 2)
            pe.sem_inc(sig["out_group"], 2)
            pe.wait_ge(sig["x_lo"], DB // 2)

            def hidden(m, s):
                pe.wait_ge(sig["u_lo"], m + 3)
                pe.wait_ge(sig["gelu"], m + 1)
                for b in range(DB):
                    last = mm3(nc, HID[s][:], (US[s][0][:, b, :], US[s][1][:, b, :]), (XS[0][:, b, :], XS[1][:, b, :]), b == 0, b == DB - 1)
                last.then_inc(sig["hid"], 1)

            def outputs(g, p):
                pe.wait_ge(sig["a_lo"], J * (g + 1))
                pe.wait_ge(sig["v_lo"], J * (g + 1) + 2)
                for q in range(COMBOS):
                    n, c = q // NH, q % NH
                    pe.wait_ge(sig["added"], COMBOS * g + q + 1)
                    for j in range(J):
                        last = mm3(nc, OUT[q % OUT_BANKS][:], (AS[p][0][:, j, n * P:(n + 1) * P], AS[p][1][:, j, n * P:(n + 1) * P]),
                                   (VS[p][0][:, j, c * 512:(c + 1) * 512], VS[p][1][:, j, c * 512:(c + 1) * 512]), j == 0, j == J - 1)
                    last.then_inc(sig["out"], 1)
                pe.wait_ge(sig["out"], COMBOS * (g + 1))
                pe.sem_inc(sig["out_group"], 1)

            def body(g, r, p, first):
                for j in range(J):
                    hidden(J * g + j, j % 2)
                if not (first and p == 0):
                    outputs(g - 1, 1 - p)
            groups(pe, body)
            outputs(GROUPS - 1, 1)

        @block.scalar
        def _(act):
            act.sem_inc(sig["gelu"], 2)
            act.wait_ge(start_in, 48)
            nc.scalar.mul(ACC[:], ACC[:], ALPHA).then_inc(sig["acc_ready"], 1)
            for q in range(DB // 2):
                act.wait_ge(x_in[q % 2], 16 * (q // 2 + 1))
                nc.scalar.copy(XS[0][:, 2 * q:2 * q + 2, :], UR[q % 2][:].rearrange("p (a b) c -> p a (b c)", a=2)).then_inc(sig["x_hi"], 1)

            def split_u(m, r_s, s):
                act.wait_ge(u_in[s], 16 * r_s)
                act.wait_ge(sig["hid"], m + 1)
                nc.scalar.copy(US[s][0][:], UR[s][:]).then_inc(sig["u_hi"], 1)

            def split_v(m, r_s, s, g, p, j):
                act.wait_ge(v_in[s], 16 * r_s)
                if j == 0:
                    act.wait_ge(sig["out_group"], g + 1)
                nc.scalar.copy(VS[p][0][:, j, :], VR[s][:]).then_inc(sig["v_hi"], 1)

            def activate(m, s, p, j):
                act.wait_ge(sig["hid"], m + 3)
                act.wait_ge(sig["a_lo"], m - 1) if not isinstance(m, int) or m >= 2 else None
                nc.scalar.activation(AC[s][:], HID[s][:], ACT.Gelu).then_inc(sig["gelu"], 1)
                act.wait_ge(sig["gated"], m + 3)
                nc.scalar.copy(AS[p][0][:, j, :], AC[s][:]).then_inc(sig["a_hi"], 1)

            def body(g, r, p, first):
                for j in range(J):
                    m = J * g + j
                    split_u(m, J // 2 * g + j // 2 + 1, j % 2)
                    if j:
                        activate(m - 1, (j - 1) % 2, p, j - 1)
                    elif not (first and p == 0):
                        activate(m - 1, 1, 1 - p, J - 1)
                    split_v(m, J // 2 * g + j // 2 + 1, j % 2, g, p, j)
            groups(act, body)
            activate(N_KEYS - 1, 1, 1, J - 1)
            for n in range(NT):
                act.wait_ge(sig["var_ready"], n + 1)
                nc.scalar.activation(std[:], std[:], ACT.Sqrt).then_inc(sig["std_ready"], 1)

        @block.vector
        def _(dve):
            ch = Chain(dve, own)
            tt = nc.vector.tensor_tensor
            dve.sem_inc(sig["v_lo"], 2)
            dve.sem_inc(sig["u_lo"], 2)
            dve.sem_inc(sig["gated"], 2)
            dve.sem_inc(sig["added"], OUT_BANKS)
            for q in range(DB // 2):
                dve.wait_ge(sig["x_hi"], q + 1)
                tt(XS[1][:, 2 * q:2 * q + 2, :], UR[q % 2][:].rearrange("p (a b) c -> p a (b c)", a=2),
                   XS[0][:, 2 * q:2 * q + 2, :].bitcast(F32), ALU.subtract).then_inc(sig["x_lo"], 1)
            dve.wait_ge(sig["acc_ready"], 1)

            def split_u(m, s):
                dve.wait_ge(sig["u_hi"], m + 1)
                tt(US[s][1][:], UR[s][:], US[s][0][:].bitcast(F32), ALU.subtract).then_inc(sig["u_lo"], 1)

            def gate(m, r_s, s, p, j):
                dve.wait_ge(g_in[s], 16 * r_s)
                dve.wait_ge(sig["gelu"], m + 3)
                tt(AC[s][:], AC[s][:], GR[s][:].rearrange("p n t -> p (n t)"), ALU.mult).then_inc(sig["gated"], 1)
                dve.wait_ge(sig["a_hi"], m + 1)
                tt(AS[p][1][:, j, :], AC[s][:], AS[p][0][:, j, :].bitcast(F32), ALU.subtract).then_inc(sig["a_lo"], 1)

            def add(g):
                for q in range(COMBOS):
                    rows = ACC[:, q // NH, (q % NH) * 512:(q % NH + 1) * 512]
                    dve.wait_ge(sig["out"], COMBOS * g + q + 1)
                    tt(rows, OUT[q % OUT_BANKS][:], rows, ALU.add).then_inc(sig["added"], 1)

            def body(g, r, p, first):
                for j in range(J):
                    m = J * g + j
                    split_u(m, j % 2)
                    if j:
                        gate(m - 1, J // 2 * g + (j - 1) // 2 + 1, (j - 1) % 2, p, j - 1)
                    elif not (first and p == 0):
                        gate(m - 1, J // 2 * g, 1, 1 - p, J - 1)
                        if not first:
                            add(g - 2)
            groups(dve, body)
            gate(N_KEYS - 1, N_KEYS // 2, 1, 1, J - 1)
            add(GROUPS - 2)
            add(GROUPS - 1)
            dve.wait_ge(sig["added"], COMBOS * GROUPS + OUT_BANKS)
            for n in range(NT):
                h = ACC[:, n, :]
                for c in range(NH):
                    ch.mark(nc.vector.bn_stats(stats[:, c, :], h[:, c * 512:(c + 1) * 512]))
                ch.wait()
                ch.step(nc.vector.bn_aggr(mv[:], stats[:]))
                nc.vector.tensor_scalar(std[:], mv[:, 1:2], LN_EPS, None, ALU.add).then_inc(sig["var_ready"], 1)
                dve.wait_ge(sig["std_ready"], n + 1)
                ch.step(nc.vector.reciprocal(std[:], std[:]))
                ch.step(nc.vector.tensor_scalar(h, h, mv[:, 0:1], std[:], ALU.subtract, ALU.mult))
                ch.step(tt(h, h, gain[:], ALU.mult))
                tt(h, h, bias[:], ALU.add).then_inc(sig["rows_ready"], 1)


def build(nc, io):
    with ExitStack() as ctx:
        def keep(scope, name, shape, dt=F32):
            return scope.enter_context(nc.sbuf_tensor(name, shape, dt))

        k = {m: keep(ctx, f"const_{m}", [P, P]) for m in ("ident", "ones", "upper", "lower", "same_head", "in16", "in32")}
        make_constants(nc, k)
        with ExitStack() as h_scope:
            k["hT_hi"], k["hT_lo"] = (keep(h_scope, f"hT_{p}", [P, DB, T], F32R) for p in ("hi", "lo"))
            embed_norm_phase(nc, k, io)
            project_phase(nc, k, io)
        delta_phase(nc, k, io)
        branch_phase(nc, k, io)
        mix_phase(nc, k, io)
        with ExitStack() as sel_scope:
            k["sel"] = keep(sel_scope, "sel", [P, XT, 3, HEADS * TOPK])
            query_phase(nc, k, io)
            gates_phase(nc, k, io)
        for half in range(2):
            experts_phase(nc, k, io, half)


SCRATCH = {
    "h_rows": (SEQ, D),
    "proj": (N_BLK, P, T),
    "bg": (T, 16),
    "o_rows": (SEQ // CHUNK, P, PAIRS * HD),
    "merged": (DB, P, SEQ),
    "h1_rows": (SEQ, D),
    "h1_t": (DB, P, SEQ),
    "g": (XT, P, P, P),
}
INPUTS = ("x", "meta", "ln0_g", "ln0_b", "w_blocks", "conv_taps", "w_ba", "a_log", "dt_bias", "onorm_g",
          "pool_w", "pool_scale", "w_branches", "w_out", "ln1_g", "ln1_b", "wq_blocks", "keys", "u_blocks", "v_blocks", "ln2_g", "ln2_b")


def lay_out(x, meta, ln0_g, ln0_b, w_in, pool_w, pool_scale, w_br_pool, conv_w, a_log, dt_bias, onorm_g, w_br_delta,
            w_out, ln1_g, ln1_b, peer_wq, peer_k1, peer_k2, peer_u, peer_v, ln2_g, ln2_b):
    a = {}
    a["x"], a["meta"] = x[0], meta
    a["ln0_g"], a["ln0_b"] = ln0_g, ln0_b
    w = w_in[0]
    pw, dw = POOL_GROUPS * P, HEADS * HD
    q0, z0 = pw, pw + 3 * dw
    b0 = z0 + dw
    g0 = b0 + 2 * HEADS
    cols = np.concatenate([w[:, q0:z0], w[:, z0:b0], w[:, g0:], w[:, :pw]], axis=1)
    blocks = lambda m: m.reshape(-1, P, m.shape[1] // P, P).transpose(2, 1, 0, 3).reshape(m.shape[1] // P, P, -1)
    a["w_blocks"] = blocks(cols)
    a["w_ba"] = w[:, b0:g0].reshape(DB, P, 16).transpose(1, 0, 2).reshape(P, -1)
    a["conv_taps"] = conv_w[0].reshape(TAPS, 3 * HEADS, P).transpose(2, 1, 0).reshape(P, -1)
    a["a_log"], a["dt_bias"], a["onorm_g"] = a_log[0], dt_bias[0], onorm_g[0]
    a["pool_w"] = pool_w[0].transpose(1, 0, 2).reshape(P, -1)
    a["pool_scale"] = pool_scale[0].reshape(POOL_GROUPS, P).T
    a["w_branches"] = blocks(np.concatenate([w_br_delta[0], w_br_pool[0]], axis=0))
    a["w_out"], a["ln1_g"], a["ln1_b"] = w_out[0], ln1_g[0], ln1_b[0]
    a["wq_blocks"] = blocks(peer_wq[0])
    a["keys"] = np.stack([peer_k1[0], peer_k2[0]], axis=1).reshape(2 * HEADS, N_KEYS, P).transpose(0, 2, 1)
    a["u_blocks"] = peer_u[0].reshape(P, P, DB, P).transpose(1, 3, 2, 0).reshape(P, P, -1)
    a["v_blocks"] = peer_v[0].reshape(P, P, D).transpose(1, 0, 2)
    a["ln2_g"], a["ln2_b"] = ln2_g[0], ln2_b[0]
    return a


def kernel(**inputs):
    import concourse.bacc as bacc
    from concourse.bass_utils import run_bass_kernel_spmd

    nc = bacc.Bacc("TRN2", target_bir_lowering=False, num_devices=1)
    laid = lay_out(**{n: np.asarray(v) for n, v in inputs.items()})
    tensors, arrays = {}, {}
    for name in INPUTS:
        arrays[f"in_{name}"] = np.ascontiguousarray(laid[name])
        tensors[name] = nc.dram_tensor(f"in_{name}", arrays[f"in_{name}"].shape, F32, kind="ExternalInput").ap()
    for name, shape in SCRATCH.items():
        tensors[name] = nc.dram_tensor(name, shape, F32, kind="Internal").ap()
    tensors["out"] = nc.dram_tensor("out", (SEQ, D), F32, kind="ExternalOutput").ap()
    build(nc, tensors)
    r = run_bass_kernel_spmd(nc, [arrays], core_ids=[0])
    return r.results[0]["out"].reshape(1, SEQ, D)
```

```python
from contextlib import ExitStack

import numpy as np
import concourse.bass as bass
from concourse import mybir

F32 = mybir.dt.float32
F32R = mybir.dt.float32r
F16 = mybir.dt.float16
U32 = mybir.dt.uint32
ACT = mybir.ActivationFunctionType
ALU = mybir.AluOpType
AX = mybir.AxisListType

P = 128
D = 1024
DB = D // P
N_META = 16
SEQ = 1024
T = N_META + SEQ
XT = SEQ // P
HEADS = 8
HD = 128
PAIRS = HEADS // 2
CHUNK = 64
PAD = CHUNK - N_META
N_CHUNKS = (T + PAD) // CHUNK
POOL_GROUPS = 4
POOL_WINDOWS = (2, 4, 8, 16)
TAPS = 4
N_KEYS = 128
TOPK = 16
ALPHA = 2.0 ** 0.25
LN_EPS, RMS_EPS, L2_EPS = 1e-5, 1e-6, 1e-6
LOWEST = -3.0e38

BLK_Q, BLK_K, BLK_V = 0, HEADS, 2 * HEADS
BLK_POOL = 3 * HEADS
BLK_Z = BLK_POOL + POOL_GROUPS
BLK_GATE = BLK_Z + HEADS
N_BLK = BLK_GATE + 2 * DB
N_FIRST = BLK_Z
PIECES = 4
PIECE = T // PIECES


class Chain:

    def __init__(self, eng, sem):
        self.eng, self.sem, self.n = eng, sem, 0

    def step(self, ins):
        self.mark(ins)
        self.wait()

    def mark(self, ins):
        self.n += 1
        ins.then_inc(self.sem, 1)

    def wait(self):
        self.eng.wait_ge(self.sem, self.n)

    def restart(self):
        self.wait()
        self.eng.sem_clear(self.sem)
        self.n = 0


class Phase:

    def __init__(self, nc, name):
        self.nc, self.name, self.ctx, self.taken = nc, name, ExitStack(), []

    def __enter__(self):
        self.ctx.__enter__()
        return self

    def __exit__(self, *a):
        done = self.ctx.__exit__(*a)
        if self.taken:
            self.nc.clear_and_free_semaphores(self.taken)
            self.nc.all_engine_barrier()
        return done

    def sb(self, name, shape, dt=F32):
        return self.ctx.enter_context(self.nc.sbuf_tensor(f"{self.name}_{name}", shape, dt))

    def ps(self, name, shape, dt=F32):
        return self.ctx.enter_context(self.nc.psum_tensor(f"{self.name}_{name}", shape, dt))

    def sem(self, name):
        self.taken.append(self.nc.alloc_semaphore(f"{self.name}_{name}"))
        return self.taken[-1]

    def sems(self, name, n=2):
        return [self.sem(f"{name}{i}") for i in range(n)]

    def block(self):
        return self.ctx.enter_context(self.nc.Block())


def row_bcast(ap, n=P):
    return ap.rearrange("(a k) -> a k", a=1).partition_broadcast(n) if ap.ndim == 1 else ap.partition_broadcast(n)


def make_constants(nc, k):
    with Phase(nc, "const") as ph:
        made = ph.sem("made")
        block = ph.block()

        @block.gpsimd
        def _(pool):
            ch = Chain(pool, made)

            def select(ap, op, fill, base, pattern, mult):
                ch.step(pool.affine_select(out=ap, in_=ap, compare_op=op, fill=fill, base=base,
                                           pattern=pattern, channel_multiplier=mult))

            ch.mark(pool.memset(k["ones"][:], 1.0))
            ch.step(pool.memset(k["ident"][:], 0.0))
            select(k["ident"][:], ALU.not_equal, 1.0, 0, [[-1, P]], 1)

            def keep_blocks(m, size):
                v = m[:].rearrange("p (g e) -> p g e", e=size)
                select(v, ALU.is_ge, 0.0, 0, [[-size, P // size], [0, size]], 1)
                select(v, ALU.is_ge, 0.0, size - 1, [[size, P // size], [0, size]], -1)

            for m in (k["upper"], k["lower"], k["same_head"], k["in16"], k["in32"]):
                ch.step(pool.memset(m[:], 1.0))
            select(k["upper"][:], ALU.is_ge, 0.0, 0, [[1, P]], -1)
            select(k["lower"][:], ALU.is_gt, 0.0, 0, [[-1, P]], 1)
            for m, size in ((k["upper"], CHUNK), (k["lower"], CHUNK), (k["same_head"], CHUNK), (k["in16"], 16), (k["in32"], 32)):
                keep_blocks(m, size)


def embed_norm_phase(nc, k, io):
    with Phase(nc, "ln0") as ph:
        X = [ph.sb(f"x{u}", [P, D]) for u in range(2)]
        H = [ph.sb(f"h{u}", [P, D]) for u in range(2)]
        gain, bias = ph.sb("gain", [P, D]), ph.sb("bias", [P, D])
        stats, mv = ph.sb("stats", [P, 2, 6]), ph.sb("mv", [P, 2])
        veps, std, rstd = ph.sb("veps", [P, 1]), ph.sb("std", [P, 1]), ph.sb("rstd", [P, 1])
        TP = [ph.ps(f"t{u}", [P, DB, P]) for u in range(2)]
        consts_in = ph.sem("consts_in")
        x_in, h_out = ph.sems("x_in"), ph.sems("h_out")
        x_free, var_ready, std_ready, h_ready = (ph.sem(n) for n in ("x_free", "var_ready", "std_ready", "h_ready"))
        t_ready, t_free, hi_ready = (ph.sem(n) for n in ("t_ready", "t_free", "hi_ready"))
        own = ph.sem("dve_own")
        block = ph.block()

        @block.sync
        def _(sp):
            sp.dma_start(gain[:], row_bcast(io["ln0_g"])).then_inc(consts_in, 16)
            sp.dma_start(bias[:], row_bcast(io["ln0_b"])).then_inc(consts_in, 16)
            sp.dma_start(X[1][0:N_META, :], io["meta"][:, :]).then_inc(x_in[1], 16)
            with sp.Fori(0, XT // 2) as i:
                for u in range(2):
                    n = 2 * i + u + 1
                    sp.wait_ge(x_free, n + 1)
                    sp.dma_start(X[u][:], io["x"][bass.ts(n - 1, P), :]).then_inc(x_in[u], 16)

        @block.vector
        def _(dve):
            ch = Chain(dve, own)
            dve.sem_inc(x_free, 2)
            dve.wait_ge(consts_in, 32)

            def lo_part(n, u, rows, cols):
                dve.wait_ge(hi_ready, n + 1)
                nc.vector.tensor_tensor(k["hT_lo"][:, :, cols], TP[u][:, :, 0:rows],
                                        k["hT_hi"][:, :, cols].bitcast(F32), ALU.subtract).then_inc(t_free, 1)

            def tile(n, u, rows, loads):
                x, h = X[u][0:rows, :], H[u][0:rows, :]
                dve.wait_ge(x_in[u], 16 * loads)
                for s in range(2):
                    ch.mark(nc.vector.bn_stats(stats[0:rows, s, :], x[:, s * 512:(s + 1) * 512]))
                ch.wait()
                ch.step(nc.vector.bn_aggr(mv[0:rows, :], stats[0:rows]))
                nc.vector.tensor_scalar(veps[0:rows], mv[0:rows, 1:2], LN_EPS, None, ALU.add).then_inc(var_ready, 1)
                dve.wait_ge(std_ready, n + 1)
                ch.step(nc.vector.reciprocal(rstd[0:rows], std[0:rows]))
                if rows == P:
                    dve.wait_ge(h_out[u], 16 * (loads - u))
                    dve.wait_ge(t_ready, n - 1 + (u == 0))
                nc.vector.tensor_scalar(h, x, mv[0:rows, 0:1], rstd[0:rows], ALU.subtract, ALU.mult).then_inc(x_free, 1)
                dve.wait_ge(x_free, n + 3)
                ch.step(nc.vector.tensor_tensor(h, h, gain[0:rows, :], ALU.mult))
                nc.vector.tensor_tensor(h, h, bias[0:rows, :], ALU.add).then_inc(h_ready, 1)
                ch.restart()

            for u in range(2):
                dve.sem_inc(h_out[u], 16)
            cols = lambda n: bass.ds((n - 1) * P + N_META, P)
            tile(0, 1, N_META, 1)
            tile(1, 0, P, 1)
            lo_part(0, 1, N_META, slice(0, N_META))
            with dve.Fori(0, XT // 2 - 1) as i:
                tile(2 * i + 2, 1, P, i + 2)
                lo_part(2 * i + 1, 0, P, cols(2 * i + 1))
                tile(2 * i + 3, 0, P, i + 2)
                lo_part(2 * i + 2, 1, P, cols(2 * i + 2))
            tile(XT, 1, P, XT // 2 + 1)
            lo_part(XT - 1, 0, P, cols(XT - 1))
            lo_part(XT, 1, P, cols(XT))

        @block.scalar
        def _(act):
            def tile(n, u, rows, cols):
                act.wait_ge(var_ready, n + 1)
                nc.scalar.activation(std[0:rows], veps[0:rows], ACT.Sqrt).then_inc(std_ready, 1)
                if rows == P:
                    act.wait_ge(h_ready, n + 1)
                    act.dma_start(io["h_rows"][bass.ts(n - 1, P), :], H[u][:]).then_inc(h_out[u], 16)
                act.wait_ge(t_ready, n + 1)
                nc.scalar.copy(k["hT_hi"][:, :, cols], TP[u][:, :, 0:rows]).then_inc(hi_ready, 1)

            tile(0, 1, N_META, slice(0, N_META))
            with act.Fori(0, XT // 2) as i:
                for u in range(2):
                    tile(2 * i + u + 1, u, P, bass.ds((2 * i + u) * P + N_META, P))
            for u in range(2):
                act.wait_ge(h_out[u], 16 * (XT // 2 + 1))

        @block.tensor
        def _(pe):
            pe.sem_inc(t_free, 2)

            def tile(n, u, rows):
                pe.wait_ge(h_ready, n + 1)
                pe.wait_ge(t_free, n + 1)
                for b in range(DB):
                    last = nc.tensor.transpose(TP[u][:, b, 0:rows], H[u][0:rows, bass.ts(b, P)], k["ident"][0:rows, 0:rows])
                last.then_inc(t_ready, 1)

            tile(0, 1, N_META)
            with pe.Fori(0, XT // 2) as i:
                for u in range(2):
                    tile(2 * i + u + 1, u, P)


def mm3(nc, out, lhs, rhs, first=True, last=True):
    (lh, ll), (rh, rl) = lhs, rhs
    nc.tensor.matmul(out, lh, rh, start=first, stop=False)
    nc.tensor.matmul(out, lh, rl, start=False, stop=False)
    return nc.tensor.matmul(out, ll, rh, start=False, stop=last)


def project_phase(nc, k, io):
    with Phase(nc, "proj") as ph:
        W = [ph.sb(f"w{u}", [P, DB, P]) for u in range(2)]
        Wh = [ph.sb(f"wh{u}", [P, DB, P], F32R) for u in range(2)]
        Wl = [ph.sb(f"wl{u}", [P, DB, P], F32R) for u in range(2)]
        Y = [ph.sb(f"y{u}", [P, TAPS - 1 + T]) for u in range(2)]
        C = [ph.sb(f"c{u}", [P, T]) for u in range(2)]
        S = [ph.sb(f"s{u}", [P, T]) for u in range(2)]
        SQ = ph.sb("sq", [P, T])
        taps = ph.sb("taps", [P, 3 * HEADS, TAPS])
        epsq, epsk = ph.sb("epsq", [P, 1]), ph.sb("epsk", [P, 1])
        wba = ph.sb("wba", [P, DB, 16])
        wbah, wbal = ph.sb("wbah", [P, DB, 16], F32R), ph.sb("wbal", [P, DB, 16], F32R)
        ba = ph.sb("ba", [16, T])
        bat = ph.sb("bat", [P, 9, 16])
        aexp, dtb, ea = ph.sb("aexp", [P, 8]), ph.sb("dtb", [P, 8]), ph.sb("ea", [P, 9, 8])
        beta, gate = ph.sb("beta", [P, 9, 8]), ph.sb("gate", [P, 9, 8])
        M = [ph.ps(f"m{u}", [P, PIECES, 512]) for u in range(2)]
        consts_in = ph.sem("consts_in")
        w_in, s_ready, y_out = ph.sems("w_in"), ph.sems("s_ready"), ph.sems("y_out")
        wl_ready, mm_ready, c_ready = ph.sem("wl_ready"), ph.sem("mm_ready"), ph.sem("c_ready")
        wh_ready, y_ready, mm_free, silu_ready, sq_ready, norm_ready, root_ready = (
            ph.sem(n) for n in ("wh_ready", "y_ready", "mm_free", "silu_ready", "sq_ready", "norm_ready", "root_ready"))
        own = ph.sem("dve_own")
        ba_sem = {n: ph.sem(n) for n in ("ba_split", "ba_mm", "ba_rows", "ba_t", "ba_copy", "ba_act", "ba_dve", "ba_out")}
        setup, passed = ph.sem("setup"), ph.sem("passed")
        block = ph.block()
        NORM_AT = 6
        pieces = lambda ap: ap.rearrange("p (a b) -> p a b", a=PIECES)
        banks = lambda u: M[u][:, :, 0:PIECE]
        @block.sync
        def _(sp):
            sp.dma_start(taps[:], io["conv_taps"].rearrange("p (n j) -> p n j", j=TAPS)).then_inc(consts_in, 16)
            sp.dma_start(wba[:], io["w_ba"].rearrange("p (b c) -> p b c", c=16)).then_inc(consts_in, 16)
            sp.dma_start(aexp[:], row_bcast(io["a_log"])).then_inc(consts_in, 16)
            sp.dma_start(dtb[:], row_bcast(io["dt_bias"])).then_inc(consts_in, 16)

            with sp.Fori(0, N_FIRST // 2) as r:
                for u in range(2):
                    sp.wait_ge(s_ready[u], r + 1)
                    sp.dma_start(io["proj"][bass.ds(2 * r + u, 1)].rearrange("a p t -> (a p) t"), S[u][:]).then_inc(y_out[u], 16)
            for u in range(2):
                sp.wait_ge(y_out[u], 16 * (N_FIRST // 2 + 1))

        @block.gpsimd
        def _(pool):
            pool.memset(epsq[:], HD * L2_EPS).then_inc(setup, 1)
            pool.memset(epsk[:], L2_EPS).then_inc(setup, 1)
            for u in range(2):
                pool.memset(Y[u][:, 0:TAPS - 1], 0.0).then_inc(setup, 1)
            pool.sem_inc(wl_ready, 2)

            def split(n, r, u):
                pool.wait_ge(w_in[u], 16 * (r + 1))
                pool.wait_ge(mm_ready, n + 1)
                pool.sem_inc(passed, 1)
                nc.gpsimd.tensor_copy(Wh[u][:], W[u][:]).then_inc(wh_ready, 1)
                pool.wait_ge(wh_ready, n + 1)
                nc.gpsimd.tensor_tensor(Wl[u][:], W[u][:], Wh[u][:].bitcast(F32), ALU.subtract).then_inc(wl_ready, 1)

            def load(n, u):
                pool.wait_ge(wl_ready, n + 1)
                pool.dma_start(W[u][:], io["w_blocks"][bass.ds(n, 1)].rearrange("a p (b c) -> (a p) b c", c=P)).then_inc(w_in[u], 16)

            for u in range(2):
                load(u, u)
            with pool.Fori(0, N_FIRST // 2 - 1) as r:
                for u in range(2):
                    split(2 * r + u, r, u)
                    load(2 * r + u + 2, u)
            for u in range(2):
                split(N_FIRST - 2 + u, N_FIRST // 2 - 1, u)
            pool.wait_ge(ba_sem["ba_dve"], 5)
            for src, c0 in ((beta, 0), (gate, 8)):
                dst = io["bg"][:, c0:c0 + 8]
                pool.dma_start(dst[0:N_META, :], src[0:N_META, 8, :]).then_inc(ba_sem["ba_out"], 16)
                pool.dma_start(dst[N_META:T, :].rearrange("(n p) c -> p n c", p=P), src[:, 0:8, :]).then_inc(ba_sem["ba_out"], 16)
            pool.wait_ge(ba_sem["ba_out"], 64)

        @block.tensor
        def _(pe):
            pe.sem_inc(mm_free, 2)
            pe.sem_inc(mm_ready, 2)

            def main(n, u, norm_of=None):
                pe.wait_ge(wl_ready, n + 3)
                pe.wait_ge(mm_free, n + 1)
                for b in range(DB):
                    if b == NORM_AT and norm_of is not None:
                        norm(norm_of, 1 - u)
                    for wpart, hparts in ((Wh[u], (k["hT_hi"], k["hT_lo"])), (Wl[u], (k["hT_hi"],))):
                        for hpart in hparts:
                            for c in range(PIECES):
                                last = nc.tensor.matmul(M[u][:, c, 0:PIECE], wpart[:, b, :],
                                                        hpart[:, b, c * PIECE:(c + 1) * PIECE],
                                                        start=(b == 0 and wpart is Wh[u] and hpart is k["hT_hi"]),
                                                        stop=(b == DB - 1 and wpart is Wl[u]))
                last.then_inc(mm_ready, 1)

            def norm(n, u):
                pe.wait_ge(sq_ready, n + 1)
                for c in range(PIECES):
                    last = nc.tensor.matmul(M[u][:, c, 0:PIECE], k["ones"][:], SQ[:, c * PIECE:(c + 1) * PIECE], start=True, stop=True)
                last.then_inc(norm_ready, 1)

            pe.wait_ge(ba_sem["ba_split"], 2)
            for b in range(DB):
                for c in range(PIECES):
                    cols = slice(c * PIECE, (c + 1) * PIECE)
                    last = mm3(nc, M[0][0:16, c, 0:PIECE], (wbah[:, b, :], wbal[:, b, :]), (k["hT_hi"][:, b, cols], k["hT_lo"][:, b, cols]), b == 0, b == DB - 1)
            last.then_inc(ba_sem["ba_mm"], 1)
            pe.wait_ge(ba_sem["ba_rows"], 1)
            for t in range(XT):
                nc.tensor.transpose(M[1][:, 0, t * 16:(t + 1) * 16], ba[:, N_META + t * P:N_META + (t + 1) * P], k["ident"][0:16, 0:16])
            nc.tensor.transpose(M[1][0:N_META, 0, XT * 16:(XT + 1) * 16], ba[:, 0:N_META], k["ident"][0:16, 0:16]).then_inc(ba_sem["ba_t"], 1)
            main(0, 0)
            pe.wait_ge(ba_sem["ba_copy"], 1)
            main(1, 1, 0)
            with pe.Fori(1, BLK_V // 2) as r:
                main(2 * r, 0, 2 * r - 1)
                main(2 * r + 1, 1, 2 * r)
            main(BLK_V, 0, BLK_V - 1)
            main(BLK_V + 1, 1)
            with pe.Fori(BLK_V // 2 + 1, N_FIRST // 2) as r:
                for u in range(2):
                    main(2 * r + u, u)

        @block.scalar
        def _(act):
            act.wait_ge(setup, 4)
            act.wait_ge(consts_in, 64)

            def take(n, u):
                act.wait_ge(mm_ready, n + 3)
                act.wait_ge(c_ready, n + 1)
                nc.scalar.copy(pieces(Y[u][:, TAPS - 1:]), banks(u)).then_inc(y_ready, 1)

            def silu_square(n, u):
                act.wait_ge(c_ready, n + 3)
                nc.scalar.activation(C[u][:], C[u][:], ACT.Silu).then_inc(silu_ready, 1)
                act.wait_ge(silu_ready, n + 1)
                nc.scalar.activation(SQ[:], C[u][:], ACT.Square).then_inc(sq_ready, 1)

            def root(n, r, u, scale, eps):
                act.wait_ge(norm_ready, n + 1)
                act.wait_ge(y_out[u], 16 * (r + 1))
                nc.scalar.activation(pieces(S[u][:]), banks(u), ACT.Sqrt, bias=eps[:], scale=scale).then_inc(root_ready, 1)
                act.wait_ge(root_ready, n + 1)
                act.sem_inc(mm_free, 1)

            nc.scalar.copy(wbah[:], wba[:]).then_inc(ba_sem["ba_split"], 1)
            act.wait_ge(ba_sem["ba_mm"], 1)
            nc.scalar.copy(pieces(ba[:]), M[0][0:16, :, 0:PIECE]).then_inc(ba_sem["ba_rows"], 1)
            act.wait_ge(ba_sem["ba_copy"], 1)
            nc.scalar.activation(beta[:], bat[:, :, 0:8], ACT.Exp, scale=-1.0).then_inc(ba_sem["ba_act"], 1)
            act.wait_ge(ba_sem["ba_dve"], 1)
            nc.scalar.activation(gate[:], ea[:], ACT.Abs).then_inc(ba_sem["ba_act"], 1)
            act.wait_ge(ba_sem["ba_act"], 2)
            nc.scalar.activation(gate[:], gate[:], ACT.Exp, scale=-1.0).then_inc(ba_sem["ba_act"], 1)
            nc.scalar.activation(aexp[:], aexp[:], ACT.Exp).then_inc(ba_sem["ba_act"], 1)
            act.wait_ge(ba_sem["ba_act"], 4)
            nc.scalar.activation(gate[:], gate[:], ACT.Ln, bias=1.0).then_inc(ba_sem["ba_act"], 1)
            take(0, 0)
            silu_square(0, 0)
            for first, last, scale, eps in ((BLK_Q, BLK_K, float(HD), epsq), (BLK_K, BLK_V, 1.0, epsk)):
                with act.Fori(first // 2, last // 2 - 1) as r:
                    root(2 * r, r, 0, scale, eps)
                    take(2 * r + 1, 1)
                    silu_square(2 * r + 1, 1)
                    root(2 * r + 1, r, 1, scale, eps)
                    take(2 * r + 2, 0)
                    silu_square(2 * r + 2, 0)
                root(last - 2, last // 2 - 1, 0, scale, eps)
                take(last - 1, 1)
                silu_square(last - 1, 1)
                root(last - 1, last // 2 - 1, 1, scale, eps)
                take(last, 0)
                if last < BLK_V:
                    silu_square(last, 0)

            def rest(kind, n, r, u, taken=False):
                if kind == "v":
                    if not taken:
                        take(n, u)
                    act.wait_ge(y_ready, n + 1)
                    act.sem_inc(mm_free, 1)
                    act.wait_ge(c_ready, n + 3)
                    act.wait_ge(y_out[u], 16 * (r + 1))
                    nc.scalar.activation(S[u][:], C[u][:], ACT.Silu).then_inc(s_ready[u], 1)
                    return
                act.wait_ge(mm_ready, n + 3)
                act.wait_ge(y_out[u], 16 * (r + 1))
                nc.scalar.copy(pieces(S[u][:]), banks(u)).then_inc(s_ready[u], 1)
                act.wait_ge(s_ready[u], r + 1)
                act.sem_inc(mm_free, 1)
            rest("v", BLK_V, BLK_V // 2, 0, taken=True)
            rest("v", BLK_V + 1, BLK_V // 2, 1)
            for kind, first, count in (("v", BLK_V + 2, HEADS - 2), ("pool", BLK_POOL, POOL_GROUPS)):
                with act.Fori(first // 2, (first + count) // 2) as r:
                    for u in range(2):
                        rest(kind, 2 * r + u, r, u)

        @block.vector
        def _(dve):
            ch = Chain(dve, own)
            dve.sem_inc(c_ready, 2)
            for u in range(2):
                dve.sem_inc(y_out[u], 16)
            dve.wait_ge(consts_in, 64)

            def convolve(n, r, u):
                tap = lambda j: taps[:, bass.ds(n, 1), j:j + 1].rearrange("p a b -> p (a b)")
                dve.wait_ge(y_ready, n + 1)
                dve.wait_ge(y_out[u], 16 * (r + 1))
                ch.step(nc.vector.tensor_scalar(C[u][:], Y[u][:, 0:T], tap(0), None, ALU.mult))
                for j in range(1, TAPS):
                    ins = nc.vector.scalar_tensor_tensor(out=C[u][:], in0=Y[u][:, j:j + T], scalar=tap(j), in1=C[u][:], op0=ALU.mult, op1=ALU.add)
                    if j < TAPS - 1:
                        ch.step(ins)
                ins.then_inc(c_ready, 1)
                ch.restart()

            def normalise(n, u):
                dve.wait_ge(root_ready, n + 1)
                ch.step(nc.vector.reciprocal(S[u][:], S[u][:]))
                nc.vector.tensor_tensor(S[u][:], S[u][:], C[u][:], ALU.mult).then_inc(s_ready[u], 1)
                ch.restart()

            dve.wait_ge(ba_sem["ba_split"], 1)
            nc.vector.tensor_tensor(wbal[:], wba[:], wbah[:].bitcast(F32), ALU.subtract).then_inc(ba_sem["ba_split"], 1)
            dve.wait_ge(ba_sem["ba_t"], 1)
            ch.step(nc.vector.memset(bat[:, XT, :], 0.0))
            nc.vector.tensor_copy(bat[0:N_META, XT, :], M[1][0:N_META, 0, XT * 16:(XT + 1) * 16])
            nc.vector.tensor_copy(bat[:, 0:XT, :], M[1][:, 0, 0:XT * 16].rearrange("p (t c) -> p t c", c=16)).then_inc(ba_sem["ba_copy"], 1)
            dve.wait_ge(ba_sem["ba_copy"], 1)
            nc.vector.tensor_tensor(ea[:], bat[:, :, 8:16], dtb[:].unsqueeze(1).to_broadcast([P, XT + 1, 8]), ALU.add).then_inc(ba_sem["ba_dve"], 1)
            dve.wait_ge(ba_sem["ba_act"], 5)
            ch.step(nc.vector.tensor_scalar(ea[:], ea[:], 0.0, None, ALU.max))
            ch.step(nc.vector.tensor_tensor(gate[:], gate[:], ea[:], ALU.add))
            ch.step(nc.vector.tensor_scalar(aexp[:], aexp[:], -1.0, None, ALU.mult))
            nc.vector.tensor_tensor(gate[:], gate[:], aexp[:].unsqueeze(1).to_broadcast([P, XT + 1, 8]), ALU.mult).then_inc(ba_sem["ba_dve"], 2)
            ch.step(nc.vector.tensor_scalar(beta[:], beta[:], 1.0, None, ALU.add))
            nc.vector.reciprocal(beta[:], beta[:]).then_inc(ba_sem["ba_dve"], 2)
            ch.restart()
            convolve(0, 0, 0)
            with dve.Fori(0, BLK_V // 2 - 1) as r:
                convolve(2 * r + 1, r, 1)
                normalise(2 * r, 0)
                convolve(2 * r + 2, r + 1, 0)
                normalise(2 * r + 1, 1)
            convolve(BLK_V - 1, BLK_V // 2 - 1, 1)
            normalise(BLK_V - 2, 0)
            convolve(BLK_V, BLK_V // 2, 0)
            normalise(BLK_V - 1, 1)
            convolve(BLK_V + 1, BLK_V // 2, 1)
            with dve.Fori(BLK_V // 2 + 1, BLK_POOL // 2) as r:
                for u in range(2):
                    convolve(2 * r + u, r, u)


def delta_phase(nc, k, io):
    CH = CHUNK
    with Phase(nc, "delta") as ph:
        W = PAIRS * P
        pair3 = lambda ap: ap.rearrange("p (m e) -> p m e", m=PAIRS)

        def two(name, shape=(P, W)):
            return [ph.sb(f"{name}{u}", list(shape)) for u in range(2)]

        KT, QT, VT = (two(n, (P, HEADS, CH)) for n in ("kT", "qT", "vT"))
        BG = two("bg", (P, 16))
        GP, BP = two("g_pair", (P, PAIRS)), two("beta_pair", (P, PAIRS))
        KR, VR = two("k_rows"), two("v_rows")
        R, E1, E2, ECB = two("r"), two("e1"), two("e2"), two("ecb")
        CUM = two("cum", (P, 2 * PAIRS))
        EC, KS, BE = two("exp_cum", (P, PAIRS)), two("k_scale", (P, PAIRS)), two("beta_exp", (P, PAIRS))
        A, AT_T, QD = two("a"), two("attn_t"), two("q_dec")
        KBE, KD, VB = two("kbe"), two("k_dec"), two("vb")
        Dm, DT, M32, M64, Z = two("d"), two("dT"), two("m32"), two("m64"), two("z")
        PW, PWT = two("pw"), two("pwT")
        U, WT, VN, O = two("u"), two("wT"), two("vn"), two("o")
        S = ph.sb("state", [P, HEADS, HD])
        BANK = ph.ps("bank", [P, 8, 512])
        X = lambda u, j: BANK[:, 3 * u + j, :]
        WS = BANK[:, 6, :]
        SIDE = BANK[:, 7, :]
        WR = ph.sb("side_w", [P, DB, P])
        SW = [[ph.sb(f"side_w{p}{u}", [P, DB, P], F32R) for p in ("hi", "lo")] for u in range(2)]
        SIDE_SILU, SIDE_OUT, onorm = ph.sb("side_silu", [P, W]), two("side_out"), ph.sb("onorm", [P, 1])
        JOBS = 3
        UNITS = 2 * JOBS
        side_block = lambda r, j: BLK_Z + r if j == 0 else BLK_GATE + 2 * r + j - 1
        side_buf = lambda j: j % 2
        side_in, onorm_in, side_stored = ph.sem("side_in"), ph.sem("onorm_in"), ph.sems("side_stored")
        side = {n: ph.sem(f"side_{n}") for n in ("hi", "lo", "passed", "raw", "read", "scaled")}

        loaded, o_out = ph.sems("loaded"), ph.sems("o_out")
        own = ph.sem("dve_own")

        signals = {n: ph.sems(n) for n in ("gates_in", "r_ready", "kv_rows", "k_copied", "v_copied", "decay_raw", "cum_ready", "diff_ready", "exp_ready",
                  "grams", "masked1", "a_ready", "attn_ready", "qd_ready", "rows_scaled", "at_raw", "d_ready",
                  "sq1", "p2", "p2t", "sq2", "z2", "p4", "p4t", "sq3", "z4", "p8", "sq4", "z8",
                  "lv1", "x1", "t1", "lv1b", "z32", "lv2", "x2", "t2", "lv2b", "z64", "uw_raw", "u_ready", "w_ready",
                  "ws_raw", "vn_ready", "out_raw", "o_ready", "upd_raw", "state_done", "inputs_used")}
        zeroed = ph.sem("zeroed")
        block = ph.block()

        def chunks(eng, body):
            body(0, {1: 1}, (1,), None)
            with eng.Fori(0, (N_CHUNKS - 1) // 2) as r:
                body(2 * r + 1, {0: r + 1, 1: r + 2}, (0, 1), r)

        @block.sync
        def _(sp):
            sp.wait_ge(zeroed, 5)
            sp.dma_start(onorm[:], io["onorm_g"].rearrange("(p a) -> p a", a=1)).then_inc(onorm_in, 16)
            for dst, first in ((KT, BLK_K), (QT, BLK_Q), (VT, BLK_V)):
                sp.dma_start(dst[1][:, :, PAD:CH], io["proj"][first:first + HEADS, :, 0:N_META].rearrange("h p t -> p h t")).then_inc(loaded[1], 16)
            for half in range(2):
                sp.dma_start(BG[1][half * CH + PAD:(half + 1) * CH, :], io["bg"][0:N_META, :]).then_inc(loaded[1], 16)
            with sp.Fori(0, (N_CHUNKS - 1) // 2) as r:
                for u, n in ((0, r + 1), (1, r + 2)):
                    t0 = (2 * r + u) * CH + N_META
                    sp.wait_ge(signals["inputs_used"][u], n)
                    for dst, first in ((KT, BLK_K), (QT, BLK_Q), (VT, BLK_V)):
                        sp.dma_start(dst[u][:], io["proj"][first:first + HEADS, :, bass.ds(t0, CH)].rearrange("h p t -> p h t")).then_inc(loaded[u], 16)
                    for half in range(2):
                        sp.dma_start(BG[u][half * CH:(half + 1) * CH, :], io["bg"][bass.ds(t0, CH), :]).then_inc(loaded[u], 16)

        @block.gpsimd
        def _(pool):
            pool.memset(S[:], 0.0).then_inc(zeroed, 1)
            for t in (KT[1], QT[1], VT[1], BG[1]):
                pool.memset(t[:], 0.0).then_inc(zeroed, 1)
            mul = lambda out, a, b: nc.gpsimd.tensor_tensor(out, a, b, ALU.mult)

            def load_side(block):
                pool.dma_start(WR[:], io["w_blocks"][bass.ds(block, 1)].rearrange("a p (b c) -> (a p) b c", c=P)).then_inc(side_in, 16)

            def split_side(r, j):
                hi, lo = SW[side_buf(j)]
                job = JOBS * r + j
                pool.wait_ge(side_in, 16 * (job + 1))
                pool.wait_ge(side["raw"], UNITS * r + (4 if j == 2 else 2))
                split_on_pool(nc, pool, WR[:], hi[:], lo[:], side["hi"], job + 1, side["lo"], side["passed"])
                pool.wait_ge(side["lo"], job + 1)
                load_side(side_block(r, j + 1) if j < JOBS - 1 else side_block(r + 1, 0))
            load_side(BLK_Z)
            for u in range(2):
                pool.sem_inc(signals["inputs_used"][u], 1)

            def body(c, n, slots, r):
                for u in slots:
                    pool.wait_ge(signals["gates_in"][u], n[u])
                    mul(pair3(R[u][:]), k["upper"][:].unsqueeze(1).to_broadcast([P, PAIRS, P]),
                        GP[u][:].unsqueeze(2).to_broadcast([P, PAIRS, P])).then_inc(signals["r_ready"][u], 1)
                if r is not None:
                    split_side(r, 0)
                for u in slots:
                    pool.wait_ge(signals["exp_ready"][u], n[u])
                    mul(pair3(E1[u][:]), pair3(E1[u][:]), k["upper"][:].unsqueeze(1).to_broadcast([P, PAIRS, P])).then_inc(signals["masked1"][u], 1)
                    mul(BE[u][:], BP[u][:], EC[u][:]).then_inc(signals["qd_ready"][u], 1)
                    mul(QD[u][:], QT[u][:].rearrange("p h t -> p (h t)"), ECB[u][:]).then_inc(signals["qd_ready"][u], 1)
                    wide = lambda s: s[:].unsqueeze(2).to_broadcast([P, PAIRS, P])
                    pool.wait_ge(signals["v_copied"][u], n[u])
                    mul(pair3(VB[u][:]), pair3(VR[u][:]), wide(BP[u])).then_inc(signals["rows_scaled"][u], 1)
                    mul(pair3(KD[u][:]), pair3(KR[u][:]), wide(KS[u])).then_inc(signals["rows_scaled"][u], 1)
                    pool.wait_ge(signals["qd_ready"][u], 2 * n[u])
                    mul(pair3(KBE[u][:]), pair3(KR[u][:]), wide(BE[u])).then_inc(signals["rows_scaled"][u], 1)
                    pool.wait_ge(signals["attn_ready"][u], n[u])
                    pool.sem_inc(signals["inputs_used"][u], 1)
                    if r is not None:
                        split_side(r, 1 + u)
            chunks(pool, body)
            pool.wait_ge(side_in, 16 * (JOBS * (N_CHUNKS - 1) // 2 + 1))

        @block.tensor
        def _(pe):
            def pairs(fn, out, a, b=None, lo=True):
                for m in range(PAIRS):
                    cs = slice(m * P, (m + 1) * P)
                    if b is None:
                        last = nc.tensor.transpose(out[:, cs], a[:, cs], k["ident"][:])
                    else:
                        last = nc.tensor.matmul(out[:, cs], a[:, cs], b[:, cs], start=True, stop=True)
                return last

            pe.sem_inc(side["raw"], 2)

            def side_part(r, i):
                if r is None:
                    return
                unit = i // 2
                j, c = unit // 2, unit % 2
                cols = slice(N_META + c * W, N_META + (c + 1) * W)
                if i % 2 == 0:
                    pe.wait_ge(side["lo"], JOBS * r + j + 1)
                    pe.wait_ge(side["read"], UNITS * r + unit + 1)
                hi, lo = SW[side_buf(j)]
                for b in range(i % 2 * DB // 2, (i % 2 + 1) * DB // 2):
                    last = mm3(nc, SIDE, (hi[:, b, :], lo[:, b, :]), (k["hT_hi"][:, b, cols], k["hT_lo"][:, b, cols]), b == 0, b == DB - 1)
                if i % 2:
                    last.then_inc(side["raw"], 1)

            def body(c, n, slots, r):
                on = lambda name, u: pe.wait_ge(signals[name][u], n[u])
                flat = lambda t: t[:].rearrange("p h t -> p (h t)")
                for u in slots:
                    pe.wait_ge(loaded[u], 80 * n[u])
                    pe.wait_ge(signals["state_done"][u], n[u])
                    pairs(None, X(u, 0), flat(KT[u]))
                    pairs(None, X(u, 1), flat(VT[u])).then_inc(signals["kv_rows"][u], 1)
                for u in slots:
                    on("r_ready", u)
                    nc.tensor.matmul(X(u, 2), k["ones"][:], R[u][:], start=True, stop=True)
                    on("k_copied", u)
                    nc.tensor.matmul(X(u, 0)[:, 0:PAIRS], k["upper"][:], GP[u][:], start=True, stop=True)
                    nc.tensor.matmul(X(u, 0)[:, PAIRS:2 * PAIRS], k["same_head"][:], GP[u][:], start=True, stop=True).then_inc(signals["decay_raw"][u], 1)
                for u in slots:
                    on("cum_ready", u)
                    on("v_copied", u)
                    pairs(None, X(u, 0), flat(KT[u]), flat(KT[u]))
                    pairs(None, X(u, 1), flat(KT[u]), flat(QT[u])).then_inc(signals["grams"][u], 1)
                side_part(r, 0)
                side_part(r, 1)
                for u in slots:
                    on("a_ready", u)
                    pairs(None, X(u, 2), A[u]).then_inc(signals["at_raw"][u], 1)
                side_part(r, 2)
                side_part(r, 3)
                for u in slots:
                    on("d_ready", u)
                    on("attn_ready", u)
                    pairs(None, X(u, 0), DT[u], Dm[u])
                    pairs(None, X(u, 1), Dm[u], DT[u]).then_inc(signals["sq1"][u], 1)
                for u in slots:
                    on("p2", u)
                    on("p2t", u)
                    pairs(None, X(u, 2), PW[u], Z[u])
                    pairs(None, X(u, 0), PWT[u], PW[u])
                    pairs(None, X(u, 1), PW[u], PWT[u]).then_inc(signals["sq2"][u], 1)
                side_part(r, 4)
                for u in slots:
                    on("p4", u)
                    on("p4t", u)
                    on("z2", u)
                    pairs(None, X(u, 2), PW[u], Z[u])
                    pairs(None, X(u, 0), PWT[u], PW[u]).then_inc(signals["sq3"][u], 1)
                for u in slots:
                    on("p8", u)
                    on("z4", u)
                    pairs(None, X(u, 2), PW[u], Z[u]).then_inc(signals["sq4"][u], 1)
                side_part(r, 5)
                for before, M, products, xs, ts, joined in (("z8", M32, "lv1", "x1", "t1", "lv1b"), ("z32", M64, "lv2", "x2", "t2", "lv2b")):
                    for u in slots:
                        on(before, u)
                        pairs(None, X(u, 0), Z[u])
                        pairs(None, X(u, 1), M[u], Z[u]).then_inc(signals[products][u], 1)
                    for u in slots:
                        on(xs, u)
                        on(ts, u)
                        pairs(None, X(u, 2), PW[u], PWT[u]).then_inc(signals[joined][u], 1)
                    side_part(r, 6 if before == "z8" else 7)
                for u in slots:
                    on("z64", u)
                    pe.wait_ge(signals["rows_scaled"][u], 3 * n[u])
                    pairs(None, X(u, 0), Z[u], VB[u])
                    pairs(None, X(u, 1), KBE[u], Z[u]).then_inc(signals["uw_raw"][u], 1)
                side_part(r, 8)
                for u in slots:
                    on("w_ready", u)
                    pe.wait_ge(signals["state_done"][1 - u], n[u] + (u == 0))
                    for h in range(HEADS):
                        m, half = h // 2, h % 2
                        last = nc.tensor.matmul(WS[half * CH:(half + 1) * CH, m * P:(m + 1) * P], WT[u][:, h * CH:(h + 1) * CH],
                                                S[:, h, :], start=True, stop=True)
                    last.then_inc(signals["ws_raw"][u], 1)
                    pe.wait_ge(signals["qd_ready"][u], 2 * n[u])
                    for m in range(PAIRS):
                        cs = slice(m * P, (m + 1) * P)
                        for half in range(2):
                            h = 2 * m + half
                            nc.tensor.matmul(X(u, 2)[half * CH:(half + 1) * CH, cs], QD[u][:, h * CH:(h + 1) * CH], S[:, h, :],
                                             start=True, stop=False, skip_group_check=True)
                        if m == 0:
                            if u == 0:
                                side_part(r, 9)
                            on("vn_ready", u)
                        last = nc.tensor.matmul(X(u, 2)[:, cs], AT_T[u][:, cs], VN[u][:, cs], start=False, stop=True, skip_group_check=True)
                    last.then_inc(signals["out_raw"][u], 1)
                    for h in range(HEADS):
                        m, rows = h // 2, slice((h % 2) * CH, (h % 2 + 1) * CH)
                        last = nc.tensor.matmul(X(u, h % 2)[:, m * P:(m + 1) * P], KD[u][rows, m * P:(m + 1) * P],
                                                VN[u][rows, m * P:(m + 1) * P], start=True, stop=True)
                    last.then_inc(signals["upd_raw"][u], 1)
                    side_part(r, 10 + u)
            chunks(pe, body)

        @block.scalar
        def _(act):
            act.sem_inc(side["read"], 1)
            act.wait_ge(onorm_in, 16)

            def take_side(r, unit):
                if r is None:
                    return
                out = SIDE_OUT[unit % 2]
                act.wait_ge(side["raw"], UNITS * r + unit + 3)
                if unit < 2:
                    nc.scalar.activation(SIDE_SILU[:], SIDE, ACT.Silu).then_inc(side["read"], 1)
                    act.wait_ge(side["read"], UNITS * r + unit + 2)
                    act.wait_ge(side_stored[unit % 2], 16 * (JOBS * r + unit // 2 + 1))
                    nc.scalar.mul(out[:], SIDE_SILU[:], onorm[:]).then_inc(side["scaled"], 1)
                    act.wait_ge(side["scaled"], 2 * r + unit + 1)
                else:
                    act.wait_ge(side_stored[unit % 2], 16 * (JOBS * r + unit // 2 + 1))
                    nc.scalar.activation(out[:], SIDE, ACT.Sigmoid).then_inc(side["read"], 1)
                    act.wait_ge(side["read"], UNITS * r + unit + 2)
                c = unit % 2
                act.dma_start(io["proj"][bass.ds(side_block(r, unit // 2), 1), :, N_META + c * W:N_META + (c + 1) * W].rearrange("a p t -> (a p) t"),
                              out[:]).then_inc(side_stored[c], 16)

            def body(c, n, slots, r):
                on = lambda name, u: act.wait_ge(signals[name][u], n[u])
                for u in slots:
                    on("kv_rows", u)
                    nc.scalar.copy(KR[u][:], X(u, 0)).then_inc(signals["k_copied"][u], 1)
                    nc.scalar.copy(VR[u][:], X(u, 1)).then_inc(signals["v_copied"][u], 1)
                for u in slots:
                    on("diff_ready", u)
                    nc.scalar.activation(ECB[u][:], X(u, 2), ACT.Exp)
                    nc.scalar.activation(E1[u][:], E1[u][:], ACT.Exp)
                    nc.scalar.activation(E2[u][:], E2[u][:], ACT.Exp, scale=-1.0)
                    nc.scalar.activation(EC[u][:], CUM[u][:, 0:PAIRS], ACT.Exp)
                    nc.scalar.activation(KS[u][:], KS[u][:], ACT.Exp).then_inc(signals["exp_ready"][u], 1)
                take_side(r, 0)
                take_side(r, 1)
                for src, done in (("sq1", "p2"), ("sq2", "p4"), ("sq3", "p8")):
                    for u in slots:
                        on(src, u)
                        nc.scalar.copy(PW[u][:], X(u, 0)).then_inc(signals[done][u], 1)
                take_side(r, 2)
                for src, done in (("lv1", "x1"), ("lv2", "x2")):
                    for u in slots:
                        on(src, u)
                        nc.scalar.copy(PW[u][:], X(u, 0)).then_inc(signals[done][u], 1)
                take_side(r, 3)
                for u in slots:
                    on("uw_raw", u)
                    nc.scalar.copy(WT[u][:], X(u, 1)).then_inc(signals["w_ready"][u], 1)
                take_side(r, 4)
                for u in slots:
                    on("out_raw", u)
                    if slots == (0, 1):
                        act.wait_ge(o_out[u], 16 * n[0])
                    nc.scalar.copy(O[u][:], X(u, 2)).then_inc(signals["o_ready"][u], 1)
                    if slots == (0, 1):
                        on("o_ready", u)
                        act.dma_start(io["o_rows"][bass.ds(c + u - 1, 1)].rearrange("a p e -> (a p) e"), O[u][:]).then_inc(o_out[u], 16)
                take_side(r, 5)
            for u in range(2):
                act.sem_inc(o_out[u], 16)
                act.sem_inc(side_stored[u], 16)
            chunks(act, body)
            for u in range(2):
                act.wait_ge(o_out[u], 16 * ((N_CHUNKS - 1) // 2 + 1))
                act.wait_ge(side_stored[u], 16 * (JOBS * (N_CHUNKS - 1) // 2 + 1))

        @block.vector
        def _(dve):
            ch = Chain(dve, own)
            tt = nc.vector.tensor_tensor
            for u in range(2):
                dve.sem_inc(signals["state_done"][u], 1)
            dve.wait_ge(zeroed, 5)

            def body(c, n, slots, r):
                on = lambda name, u: dve.wait_ge(signals[name][u], n[u])
                over_pairs = lambda m: m[:].unsqueeze(1).to_broadcast([P, PAIRS, P])
                wide = lambda s: s.unsqueeze(2).to_broadcast([P, PAIRS, P])
                for u in slots:
                    dve.wait_ge(loaded[u], 80 * n[u])
                    for half in range(2):
                        rows = slice(half * CH, (half + 1) * CH)
                        of_pair = lambda c0: BG[u][rows, c0:c0 + 8].rearrange("p (m e) -> p e m", e=2)[:, half, :]
                        nc.vector.tensor_copy(BP[u][rows, :], of_pair(0))
                        last = nc.vector.tensor_copy(GP[u][rows, :], of_pair(8))
                    last.then_inc(signals["gates_in"][u], 1)
                for u in slots:
                    on("decay_raw", u)
                    nc.vector.tensor_copy(CUM[u][:], X(u, 0)[:, 0:2 * PAIRS]).then_inc(signals["cum_ready"][u], 1)
                    on("cum_ready", u)
                    cum, whole = CUM[u][:, 0:PAIRS], CUM[u][:, PAIRS:]
                    tt(KS[u][:], whole, cum, ALU.subtract)
                    ch.step(tt(pair3(E2[u][:]), pair3(X(u, 2)), wide(cum), ALU.subtract))
                    nc.vector.tensor_scalar(E1[u][:], E2[u][:], 0.0, None, ALU.min)
                    nc.vector.tensor_scalar(E2[u][:], E2[u][:], 0.0, None, ALU.max).then_inc(signals["diff_ready"][u], 1)
                for u in slots:
                    on("exp_ready", u)
                    ch.step(tt(pair3(E2[u][:]), pair3(E2[u][:]), over_pairs(k["lower"]), ALU.mult))
                    ch.step(tt(pair3(E2[u][:]), pair3(E2[u][:]), wide(BP[u][:]), ALU.mult))
                    on("grams", u)
                    tt(A[u][:], X(u, 0), E2[u][:], ALU.mult).then_inc(signals["a_ready"][u], 1)
                    on("masked1", u)
                    tt(AT_T[u][:], X(u, 1), E1[u][:], ALU.mult).then_inc(signals["attn_ready"][u], 1)
                    on("a_ready", u)
                    tt(pair3(Dm[u][:]), pair3(A[u][:]), over_pairs(k["in16"]), ALU.mult)
                    ch.step(tt(pair3(M32[u][:]), pair3(A[u][:]), over_pairs(k["in32"]), ALU.mult))
                    tt(M64[u][:], A[u][:], M32[u][:], ALU.subtract)
                    ch.step(tt(M32[u][:], M32[u][:], Dm[u][:], ALU.subtract))
                for u in slots:
                    on("at_raw", u)
                    ch.step(tt(pair3(DT[u][:]), pair3(X(u, 2)), over_pairs(k["in16"]), ALU.mult))
                    tt(pair3(Z[u][:]), over_pairs(k["ident"]), pair3(DT[u][:]), ALU.subtract).then_inc(signals["d_ready"][u], 1)
                for u in slots:
                    on("sq1", u)
                    nc.vector.tensor_copy(PWT[u][:], X(u, 1)).then_inc(signals["p2t"][u], 1)
                for u in slots:
                    on("sq2", u)
                    nc.vector.tensor_copy(PWT[u][:], X(u, 1)).then_inc(signals["p4t"][u], 1)
                    tt(Z[u][:], X(u, 2), Z[u][:], ALU.add).then_inc(signals["z2"][u], 1)
                for src, done in (("sq3", "z4"), ("sq4", "z8")):
                    for u in slots:
                        on(src, u)
                        tt(Z[u][:], X(u, 2), Z[u][:], ALU.add).then_inc(signals[done][u], 1)
                for products, ts, joined, done in (("lv1", "t1", "lv1b", "z32"), ("lv2", "t2", "lv2b", "z64")):
                    for u in slots:
                        on(products, u)
                        nc.vector.tensor_copy(PWT[u][:], X(u, 1)).then_inc(signals[ts][u], 1)
                    for u in slots:
                        on(joined, u)
                        tt(Z[u][:], Z[u][:], X(u, 2), ALU.subtract).then_inc(signals[done][u], 1)
                for u in slots:
                    on("uw_raw", u)
                    nc.vector.tensor_copy(U[u][:], X(u, 0)).then_inc(signals["u_ready"][u], 1)
                for u in slots:
                    on("ws_raw", u)
                    on("u_ready", u)
                    tt(VN[u][:], U[u][:], WS, ALU.subtract).then_inc(signals["vn_ready"][u], 1)
                    on("upd_raw", u)
                    whole = ECB[u][:].rearrange("p (h t) -> p h t", t=CH)[:, :, CH - 1:CH].to_broadcast([P, HEADS, HD])
                    ch.step(tt(S[:], S[:], whole, ALU.mult))
                    on("o_ready", u)
                    by_half = S[:].rearrange("p (m b) e -> p b m e", b=2)
                    tt(by_half, by_half, BANK[:, 3 * u:3 * u + 2, :].rearrange("p b (m e) -> p b m e", e=HD), ALU.add).then_inc(signals["state_done"][u], 1)
                ch.restart()
            chunks(dve, body)


def split_on_pool(nc, pool, raw, hi, lo, hi_ready, count, lo_ready, passed=None):
    if passed is not None:
        pool.sem_inc(passed, 1)
    nc.gpsimd.tensor_copy(hi, raw).then_inc(hi_ready, 1)
    pool.wait_ge(hi_ready, count)
    return nc.gpsimd.tensor_tensor(lo, raw, hi.bitcast(F32), ALU.subtract).then_inc(lo_ready, 1)


def branch_phase(nc, k, io):
    NG = POOL_GROUPS
    LEAD = max(POOL_WINDOWS)
    HALVES = SEQ // 512
    with Phase(nc, "branch") as ph:
        oT = [ph.sb(f"oT_{p}", [P, HEADS, SEQ], F32R) for p in ("hi", "lo")]
        yp = [ph.sb(f"yp_{p}", [P, NG, SEQ], F32R) for p in ("hi", "lo")]
        with ExitStack() as first_scope:
            ph1 = Phase(nc, "brin")
            first_scope.enter_context(ph1)
            XP = [ph1.sb(f"xp{u}", [P, LEAD + T]) for u in range(2)]
            SA, SB = ph1.sb("sa", [P, LEAD + T]), ph1.sb("sb", [P, LEAD + T])
            PL = [ph1.sb(f"pooled{u}", [P, SEQ]) for u in range(2)]
            PLs = [[ph1.sb(f"pooled_{p}{u}", [P, SEQ], F32R) for p in ("hi", "lo")] for u in range(2)]
            PWr = ph1.sb("pool_w", [P, NG, P])
            PWs = [ph1.sb(f"pool_w_{p}", [P, NG, P], F32R) for p in ("hi", "lo")]
            scale = ph1.sb("pool_scale", [P, NG])
            YP = [ph1.sb(f"yp{u}", [P, SEQ]) for u in range(2)]
            OR = [ph1.sb(f"or{u}", [P, 2, PAIRS * HD]) for u in range(2)]
            ON = [ph1.sb(f"on{u}", [P, 2, PAIRS * HD]) for u in range(2)]
            ZC = [ph1.sb(f"zc{u}", [P, HEADS, P]) for u in range(2)]
            OZ = [ph1.sb(f"oz{u}", [P, HEADS, P]) for u in range(2)]
            SQ = ph1.sb("sq", [P, 2 * PAIRS, HD])
            ms = [ph1.sb(f"ms{u}", [P, 2 * PAIRS]) for u in range(2)]
            root = [ph1.sb(f"root{u}", [P, 2 * PAIRS]) for u in range(2)]
            MP = [ph1.ps(f"mixed{u}", [P, HALVES, 512]) for u in range(2)]
            TP = [ph1.ps(f"t{u}", [P, 2, PAIRS * P]) for u in range(2)]
            consts_in, pads = ph1.sem("consts_in"), ph1.sem("pads")
            xp_in, o_in, z_in = ph1.sems("xp_in"), ph1.sems("o_in"), ph1.sems("z_in")
            names = ("pooled", "pooled_hi", "pooled_lo", "pw_hi", "pw_lo", "mixed", "yp_ready", "yp_hi", "yp_lo",
                     "squared", "ms_ready", "root_ready", "on_ready", "t_ready", "oz_ready", "o_hi", "o_lo")
            sig = {n: ph1.sem(n) for n in names}
            own = ph1.sem("dve_own")
            block = ph1.block()

            @block.sync
            def _(sp):
                sp.dma_start(PWr[:], io["pool_w"].rearrange("p (g c) -> p g c", g=NG)).then_inc(consts_in, 16)
                sp.dma_start(scale[:], io["pool_scale"]).then_inc(consts_in, 16)
                for g in range(NG):
                    if g >= 2:
                        sp.wait_ge(sig["pooled"], g - 1)
                    sp.dma_start(XP[g % 2][:, LEAD:], io["proj"][BLK_POOL + g]).then_inc(xp_in[g % 2], 16)
                with sp.Fori(0, XT // 2) as r:
                    for u in range(2):
                        n = 2 * r + u
                        sp.wait_ge(sig["on_ready"], n + 1)
                        sp.dma_start(OR[u][:], io["o_rows"][bass.ds(2 * n, 2)].rearrange("c p e -> p c e")).then_inc(o_in[u], 16)
                        sp.wait_ge(sig["oz_ready"], n + 1)
                        sp.dma_start(ZC[u][:], io["proj"][BLK_Z:BLK_Z + HEADS, :, bass.ds(n * P + N_META, P)].rearrange("h p t -> p h t")).then_inc(z_in[u], 16)

            @block.gpsimd
            def _(pool):
                for u in range(2):
                    pool.memset(XP[u][:, 0:LEAD], 0.0).then_inc(pads, 1)
                pool.wait_ge(consts_in, 32)
                split_on_pool(nc, pool, PWr[:], PWs[0][:], PWs[1][:], sig["pw_hi"], 1, sig["pw_lo"])
                for g in range(NG):
                    pool.wait_ge(sig["yp_hi"], g + 1)
                    nc.gpsimd.tensor_tensor(yp[1][:, g, :], YP[g % 2][:], yp[0][:, g, :].bitcast(F32), ALU.subtract).then_inc(sig["yp_lo"], 1)
                with pool.Fori(0, XT // 2) as r:
                    for u in range(2):
                        n = 2 * r + u
                        cols = bass.ds(n * P, P)
                        pool.wait_ge(sig["o_hi"], n + 1)
                        nc.gpsimd.tensor_tensor(oT[1][:, :, cols], OZ[u][:], oT[0][:, :, cols].bitcast(F32), ALU.subtract).then_inc(sig["o_lo"], 1)

            @block.vector
            def _(dve):
                ch = Chain(dve, own)
                tt = nc.vector.tensor_tensor
                for name in ("on_ready", "oz_ready", "o_lo"):
                    dve.sem_inc(sig[name], 2)
                dve.wait_ge(pads, 2)
                for g, w in enumerate(POOL_WINDOWS):
                    x = XP[g % 2]
                    dve.wait_ge(xp_in[g % 2], 16 * (g // 2 + 1))
                    src, size = x, 1
                    while size < w:
                        dst = SA if src is not SA else SB
                        first = 2 * size - 1
                        ch.step(tt(dst[:, first:], src[:, first:], src[:, first - size:LEAD + T - size], ALU.add))
                        src, size = dst, 2 * size
                    cols = slice(LEAD + N_META, LEAD + T)
                    pl, parts = PL[g % 2], PLs[g % 2]
                    if g >= 2:
                        dve.wait_ge(sig["pooled_lo"], g - 1)
                    nc.vector.scalar_tensor_tensor(out=pl[:], in0=src[:, cols], scalar=1.0 / w, in1=x[:, cols],
                                                   op0=ALU.mult, op1=ALU.subtract).then_inc(sig["pooled"], 1)
                    dve.wait_ge(sig["pooled_hi"], g + 1)
                    tt(parts[1][:], pl[:], parts[0][:].bitcast(F32), ALU.subtract).then_inc(sig["pooled_lo"], 1)
                ch.restart()
                pairs = lambda t: t[:].rearrange("p c (m e) -> p (c m) e", e=HD)

                def mean_square(n, u):
                    dve.wait_ge(sig["squared"], n + 1)
                    ch.step(nc.vector.tensor_reduce(ms[u][:], SQ[:], AX.X, ALU.add))
                    nc.vector.tensor_scalar(ms[u][:], ms[u][:], 1.0 / HD, RMS_EPS, ALU.mult, ALU.add).then_inc(sig["ms_ready"], 1)

                def normalise(n, u):
                    dve.wait_ge(sig["root_ready"], n + 1)
                    ch.step(nc.vector.reciprocal(root[u][:], root[u][:]))
                    dve.wait_ge(sig["t_ready"], n + 1)
                    tt(pairs(ON[u]), pairs(OR[u]), root[u][:].unsqueeze(2).to_broadcast([P, 2 * PAIRS, HD]), ALU.mult).then_inc(sig["on_ready"], 1)

                def gate(n, r_u, u):
                    dve.wait_ge(sig["t_ready"], n + 3)
                    dve.wait_ge(z_in[u], 16 * r_u)
                    dve.wait_ge(sig["o_lo"], n + 1)
                    by_chunk = lambda t: t[:].rearrange("p h (c t) -> p c h t", c=2)
                    tt(by_chunk(OZ[u]), TP[u][:].rearrange("p c (h t) -> p c h t", t=CHUNK), by_chunk(ZC[u]), ALU.mult).then_inc(sig["oz_ready"], 1)

                mean_square(0, 0)
                normalise(0, 0)
                ch.restart()
                with dve.Fori(0, XT // 2 - 1) as r:
                    mean_square(2 * r + 1, 1)
                    gate(2 * r, r + 1, 0)
                    normalise(2 * r + 1, 1)
                    mean_square(2 * r + 2, 0)
                    gate(2 * r + 1, r + 1, 1)
                    normalise(2 * r + 2, 0)
                    ch.restart()
                mean_square(XT - 1, 1)
                gate(XT - 2, XT // 2, 0)
                normalise(XT - 1, 1)
                gate(XT - 1, XT // 2, 1)

            @block.scalar
            def _(act):
                act.wait_ge(consts_in, 32)

                def pooled_hi(g):
                    act.wait_ge(sig["pooled"], g + 1)
                    if g >= 2:
                        act.wait_ge(sig["mixed"], g - 1)
                    nc.scalar.copy(PLs[g % 2][0][:], PL[g % 2][:]).then_inc(sig["pooled_hi"], 1)

                pooled_hi(0)
                for g in range(NG):
                    if g < NG - 1:
                        pooled_hi(g + 1)
                    act.wait_ge(sig["mixed"], g + 1)
                    if g >= 2:
                        act.wait_ge(sig["yp_lo"], g - 1)
                    nc.scalar.mul(YP[g % 2][:].rearrange("p (a b) -> p a b", a=HALVES), MP[g % 2][:], scale[:, g:g + 1]).then_inc(sig["yp_ready"], 1)
                    act.wait_ge(sig["yp_ready"], g + 1)
                    nc.scalar.copy(yp[0][:, g, :], YP[g % 2][:]).then_inc(sig["yp_hi"], 1)

                def square(n, r_u, u):
                    act.wait_ge(o_in[u], 16 * r_u)
                    nc.scalar.activation(SQ[:].rearrange("p (c m) e -> p c (m e)", c=2), OR[u][:], ACT.Square).then_inc(sig["squared"], 1)

                def take_root(n, u):
                    act.wait_ge(sig["ms_ready"], n + 1)
                    nc.scalar.activation(root[u][:], ms[u][:], ACT.Sqrt).then_inc(sig["root_ready"], 1)

                def oz_hi(n, u):
                    act.wait_ge(sig["oz_ready"], n + 3)
                    nc.scalar.copy(oT[0][:, :, bass.ds(n * P, P)], OZ[u][:]).then_inc(sig["o_hi"], 1)

                square(0, 1, 0)
                take_root(0, 0)
                square(1, 1, 1)
                with act.Fori(0, XT // 2 - 1) as r:
                    take_root(2 * r + 1, 1)
                    square(2 * r + 2, r + 2, 0)
                    oz_hi(2 * r, 0)
                    take_root(2 * r + 2, 0)
                    square(2 * r + 3, r + 2, 1)
                    oz_hi(2 * r + 1, 1)
                take_root(XT - 1, 1)
                oz_hi(XT - 2, 0)
                oz_hi(XT - 1, 1)

            @block.tensor
            def _(pe):
                pe.sem_inc(sig["t_ready"], 2)
                pe.wait_ge(sig["pw_lo"], 1)
                for g in range(NG):
                    pe.wait_ge(sig["pooled_lo"], g + 1)
                    if g >= 2:
                        pe.wait_ge(sig["yp_ready"], g - 1)
                    parts = PLs[g % 2]
                    for c in range(HALVES):
                        cs = slice(c * 512, (c + 1) * 512)
                        last = mm3(nc, MP[g % 2][:, c, :], (PWs[0][:, g, :], PWs[1][:, g, :]), (parts[0][:, cs], parts[1][:, cs]))
                    last.then_inc(sig["mixed"], 1)
                with pe.Fori(0, XT // 2) as r:
                    for u in range(2):
                        n = 2 * r + u
                        pe.wait_ge(sig["on_ready"], n + 3)
                        pe.wait_ge(sig["oz_ready"], n + 1)
                        for c in range(2):
                            for m in range(PAIRS):
                                cs = slice(m * P, (m + 1) * P)
                                last = nc.tensor.transpose(TP[u][:, c, cs], ON[u][:, c, cs], k["ident"][:])
                        last.then_inc(sig["t_ready"], 1)

        ph2 = Phase(nc, "brout")
        with ph2:
            NB = HEADS + NG
            Wr = [ph2.sb(f"w{u}", [P, NB, P]) for u in range(2)]
            Ws = [[ph2.sb(f"w{p}{u}", [P, NB, P], F32R) for p in ("hi", "lo")] for u in range(2)]
            GP = [ph2.sb(f"gp{u}", [P, SEQ]) for u in range(2)]
            GD = [ph2.sb(f"gd{u}", [P, SEQ]) for u in range(2)]
            YA = [ph2.ps(f"ya{u}", [P, HALVES, 512]) for u in range(2)]
            YB = [ph2.ps(f"yb{u}", [P, HALVES, 512]) for u in range(2)]
            loaded, stored = ph2.sems("loaded"), ph2.sems("stored")
            w_hi, w_lo, passed, products, merged = (ph2.sem(n) for n in ("w_hi", "w_lo", "passed", "products", "merged"))
            own = ph2.sem("dve_own")
            block = ph2.block()

            @block.sync
            def _(sp):
                with sp.Fori(0, DB // 2) as r:
                    for u in range(2):
                        n = 2 * r + u
                        sp.wait_ge(w_lo, n + 1)
                        sp.dma_start(Wr[u][:], io["w_branches"][bass.ds(n, 1)].rearrange("a p (b c) -> (a p) b c", c=P)).then_inc(loaded[u], 16)
                        sp.wait_ge(stored[u], 16 * (r + 1))
                        sp.dma_start(GP[u][:], io["proj"][bass.ds(n + BLK_GATE, 1), :, N_META:T].rearrange("a p t -> (a p) t")).then_inc(loaded[u], 16)
                        sp.dma_start(GD[u][:], io["proj"][bass.ds(n + BLK_GATE + DB, 1), :, N_META:T].rearrange("a p t -> (a p) t")).then_inc(loaded[u], 16)

            @block.gpsimd
            def _(pool):
                pool.sem_inc(w_lo, 2)
                with pool.Fori(0, DB // 2) as r:
                    for u in range(2):
                        n = 2 * r + u
                        pool.wait_ge(loaded[u], 48 * (r + 1))
                        pool.wait_ge(products, n + 1)
                        split_on_pool(nc, pool, Wr[u][:], Ws[u][0][:], Ws[u][1][:], w_hi, n + 1, w_lo, passed)

            @block.tensor
            def _(pe):
                pe.sem_inc(products, 2)
                with pe.Fori(0, DB // 2) as r:
                    for u in range(2):
                        n = 2 * r + u
                        pe.wait_ge(w_lo, n + 3)
                        pe.wait_ge(merged, n + 1)
                        for dst, src, b0, count in ((YA[u], yp, HEADS, NG), (YB[u], oT, 0, HEADS)):
                            for b in range(count):
                                for c in range(HALVES):
                                    cs = slice(c * 512, (c + 1) * 512)
                                    last = mm3(nc, dst[:, c, :], (Ws[u][0][:, b0 + b, :], Ws[u][1][:, b0 + b, :]),
                                               (src[0][:, b, cs], src[1][:, b, cs]), b == 0, b == count - 1)
                        last.then_inc(products, 1)

            @block.vector
            def _(dve):
                ch = Chain(dve, own)
                dve.sem_inc(merged, 2)
                with dve.Fori(0, DB // 2) as r:
                    for u in range(2):
                        n = 2 * r + u
                        halves = lambda t: t[:].rearrange("p (a b) -> p a b", a=HALVES)
                        dve.wait_ge(loaded[u], 48 * (r + 1))
                        dve.wait_ge(products, n + 3)
                        ch.mark(nc.vector.tensor_tensor(halves(GP[u]), YA[u][:], halves(GP[u]), ALU.mult))
                        ch.step(nc.vector.tensor_tensor(halves(GD[u]), YB[u][:], halves(GD[u]), ALU.mult))
                        nc.vector.tensor_tensor(GP[u][:], GP[u][:], GD[u][:], ALU.add).then_inc(merged, 1)
                        ch.restart()

            @block.scalar
            def _(act):
                for u in range(2):
                    act.sem_inc(stored[u], 16)
                with act.Fori(0, DB // 2) as r:
                    for u in range(2):
                        n = 2 * r + u
                        act.wait_ge(merged, n + 3)
                        act.dma_start(io["merged"][bass.ds(n, 1)].rearrange("a p t -> (a p) t"), GP[u][:]).then_inc(stored[u], 16)
                for u in range(2):
                    act.wait_ge(stored[u], 16 * (DB // 2 + 1))


def mix_phase(nc, k, io):
    NH = D // 512
    with Phase(nc, "mix") as ph:
        Wr = [ph.sb(f"w{u}", [P, D]) for u in range(2)]
        Ws = [ph.sb(f"w_{p}", [P, DB, D], F32R) for p in ("hi", "lo")]
        gain, bias = ph.sb("gain", [P, D]), ph.sb("bias", [P, D])
        MR = [ph.sb(f"m{u}", [P, DB, P]) for u in range(2)]
        MS = [[ph.sb(f"m{p}{u}", [P, DB, P], F32R) for p in ("hi", "lo")] for u in range(2)]
        HR = [ph.sb(f"h{u}", [P, D]) for u in range(2)]
        HT = [ph.sb(f"hT{u}", [P, DB, P]) for u in range(2)]
        stats, mv = ph.sb("stats", [P, NH, 6]), ph.sb("mv", [P, 2])
        std, rstd = ph.sb("std", [P, 1]), ph.sb("rstd", [P, 1])
        MX = [ph.ps(f"mx{u}", [P, NH, 512]) for u in range(2)]
        TP = [ph.ps(f"t{u}", [P, DB, P]) for u in range(2)]
        consts_in = ph.sem("consts_in")
        w_in, m_in, h_in, rows_out, t_out = (ph.sems(n) for n in ("w_in", "m_in", "h_in", "rows_out", "t_out"))
        sig = {n: ph.sem(n) for n in ("w_hi", "w_lo", "m_hi", "m_lo", "passed", "mixed", "summed", "var_ready", "std_ready", "h_ready", "t_ready", "t_copied", "x_hi", "x_lo")}
        own = ph.sem("dve_own")
        block = ph.block()

        def tiles(eng, body):
            with eng.Fori(0, XT // 2) as r:
                for u in range(2):
                    body(2 * r + u, r, u)

        @block.sync
        def _(sp):
            for b in range(DB):
                if b >= 2:
                    sp.wait_ge(sig["w_lo"], b - 1)
                sp.dma_start(Wr[b % 2][:], io["w_out"][b * P:(b + 1) * P, :]).then_inc(w_in[b % 2], 16)

            def body(n, r, u):
                sp.wait_ge(sig["m_lo"], n + 1)
                sp.dma_start(MR[u][:], io["merged"][:, :, bass.ts(n, P)].rearrange("b p t -> p b t")).then_inc(m_in[u], 16)
                sp.wait_ge(rows_out[u], 16 * (r + 1))
                sp.wait_ge(sig["t_ready"], n + 1)
                sp.dma_start(HR[u][:], io["h_rows"][bass.ts(n, P), :]).then_inc(h_in[u], 16)
            tiles(sp, body)

        @block.gpsimd
        def _(pool):
            pool.sem_inc(sig["m_lo"], 2)
            pool.dma_start(gain[:], row_bcast(io["ln1_g"])).then_inc(consts_in, 16)
            pool.dma_start(bias[:], row_bcast(io["ln1_b"])).then_inc(consts_in, 16)

            def body(n, r, u):
                pool.wait_ge(m_in[u], 16 * (r + 1))
                pool.wait_ge(sig["mixed"], n + 1)
                split_on_pool(nc, pool, MR[u][:], MS[u][0][:], MS[u][1][:], sig["m_hi"], n + 1, sig["m_lo"], sig["passed"])
            tiles(pool, body)

        @block.tensor
        def _(pe):
            pe.sem_inc(sig["mixed"], 2)
            pe.sem_inc(sig["t_ready"], 2)
            pe.wait_ge(sig["w_lo"], DB)

            def products(n, u):
                pe.wait_ge(sig["m_lo"], n + 3)
                pe.wait_ge(sig["summed"], n + 1)
                for c in range(NH):
                    for b in range(DB):
                        last = mm3(nc, MX[u][:, c, :], (MS[u][0][:, b, :], MS[u][1][:, b, :]),
                                   (Ws[0][:, b, c * 512:(c + 1) * 512], Ws[1][:, b, c * 512:(c + 1) * 512]), b == 0, b == DB - 1)
                last.then_inc(sig["mixed"], 1)

            def transposes(n, u):
                pe.wait_ge(sig["h_ready"], n + 1)
                pe.wait_ge(sig["t_copied"], n + 1)
                for b in range(DB):
                    last = nc.tensor.transpose(TP[u][:, b, :], HR[u][:, b * P:(b + 1) * P], k["ident"][:])
                last.then_inc(sig["t_ready"], 1)

            products(0, 0)
            with pe.Fori(0, XT // 2 - 1) as r:
                products(2 * r + 1, 1)
                transposes(2 * r, 0)
                products(2 * r + 2, 0)
                transposes(2 * r + 1, 1)
            products(XT - 1, 1)
            transposes(XT - 2, 0)
            transposes(XT - 1, 1)

        @block.vector
        def _(dve):
            ch = Chain(dve, own)
            dve.sem_inc(sig["summed"], 2)
            dve.sem_inc(sig["x_lo"], 2)
            for b in range(DB):
                dve.wait_ge(sig["w_hi"], b + 1)
                nc.vector.tensor_tensor(Ws[1][:, b, :], Wr[b % 2][:], Ws[0][:, b, :].bitcast(F32), ALU.subtract).then_inc(sig["w_lo"], 1)
            dve.wait_ge(consts_in, 32)

            def norm(n, r_u, u):
                h = HR[u][:]
                halves = h.rearrange("p (a b) -> p a b", a=NH)
                dve.wait_ge(h_in[u], 16 * r_u)
                dve.wait_ge(sig["mixed"], n + 3)
                nc.vector.scalar_tensor_tensor(out=halves, in0=halves, scalar=ALPHA, in1=MX[u][:], op0=ALU.mult, op1=ALU.add).then_inc(sig["summed"], 1)
                dve.wait_ge(sig["summed"], n + 3)
                for s in range(NH):
                    ch.mark(nc.vector.bn_stats(stats[:, s, :], h[:, s * 512:(s + 1) * 512]))
                ch.wait()
                ch.step(nc.vector.bn_aggr(mv[:], stats[:]))
                nc.vector.tensor_scalar(std[:], mv[:, 1:2], LN_EPS, None, ALU.add).then_inc(sig["var_ready"], 1)
                dve.wait_ge(sig["std_ready"], n + 1)
                ch.step(nc.vector.reciprocal(rstd[:], std[:]))
                ch.step(nc.vector.tensor_scalar(h, h, mv[:, 0:1], rstd[:], ALU.subtract, ALU.mult))
                ch.step(nc.vector.tensor_tensor(h, h, gain[:], ALU.mult))
                nc.vector.tensor_tensor(h, h, bias[:], ALU.add).then_inc(sig["h_ready"], 1)
                ch.restart()

            def lo_part(n, u):
                dve.wait_ge(sig["x_hi"], n + 1)
                cols = bass.ts(n, P)
                nc.vector.tensor_tensor(k["h1T_lo"][:, :, cols], HT[u][:], k["h1T_hi"][:, :, cols].bitcast(F32), ALU.subtract).then_inc(sig["x_lo"], 1)

            norm(0, 1, 0)
            with dve.Fori(0, XT // 2 - 1) as r:
                norm(2 * r + 1, r + 1, 1)
                lo_part(2 * r, 0)
                norm(2 * r + 2, r + 2, 0)
                lo_part(2 * r + 1, 1)
            norm(XT - 1, XT // 2, 1)
            lo_part(XT - 2, 0)
            lo_part(XT - 1, 1)

        @block.scalar
        def _(act):
            act.sem_inc(sig["t_copied"], 2)
            for u in range(2):
                act.sem_inc(rows_out[u], 16)
                act.sem_inc(t_out[u], 16)
            for b in range(DB):
                act.wait_ge(w_in[b % 2], 16 * (b // 2 + 1))
                nc.scalar.copy(Ws[0][:, b, :], Wr[b % 2][:]).then_inc(sig["w_hi"], 1)

            def body(n, r, u):
                act.wait_ge(sig["var_ready"], n + 1)
                nc.scalar.activation(std[:], std[:], ACT.Sqrt).then_inc(sig["std_ready"], 1)
                act.wait_ge(sig["h_ready"], n + 1)
                act.dma_start(io["h1_rows"][bass.ts(n, P), :], HR[u][:]).then_inc(rows_out[u], 16)
                act.wait_ge(sig["t_ready"], n + 3)
                act.wait_ge(t_out[u], 16 * (r + 1))
                act.wait_ge(sig["x_lo"], n + 1)
                nc.scalar.copy(HT[u][:], TP[u][:]).then_inc(sig["t_copied"], 1)
                act.wait_ge(sig["t_copied"], n + 3)
                act.dma_start(io["h1_t"][:, :, bass.ts(n, P)].rearrange("b p t -> p b t"), HT[u][:]).then_inc(t_out[u], 16)
                nc.scalar.copy(k["h1T_hi"][:, :, bass.ts(n, P)], HT[u][:]).then_inc(sig["x_hi"], 1)
            tiles(act, body)
            for u in range(2):
                act.wait_ge(rows_out[u], 16 * (XT // 2 + 1))
                act.wait_ge(t_out[u], 16 * (XT // 2 + 1))


def query_phase(nc, k, io):
    NQ = 2 * HEADS
    K = TOPK
    WHOLE = 4
    NARROW = K // WHOLE
    SPLIT = WHOLE * K
    CANDS = SPLIT + (K - WHOLE) * NARROW
    assert NARROW == 4 and K == 16
    HALVES = SEQ // 512
    with Phase(nc, "query") as ph:
        XS = k["h1T_hi"], k["h1T_lo"]
        W = [ph.sb(f"w{u}", [P, DB, P]) for u in range(2)]
        WS = [[ph.sb(f"w{p}{u}", [P, DB, P], F32R) for p in ("hi", "lo")] for u in range(2)]
        KEYS = ph.sb("keys", [P, NQ, P])
        QT = [ph.sb(f"q{u}", [P, SEQ]) for u in range(2)]
        SC = [ph.sb(f"s{u}", [P, XT, P]) for u in range(2)]
        REST = ph.sb("rest", [P, XT, P])
        V, I, IF = ph.sb("v", [P, 2, XT, K]), ph.sb("i", [P, 2, XT, K], U32), ph.sb("i_half", [P, 2, XT, K], F16)
        CAND, CREST = ph.sb("cand", [P, XT, CANDS]), ph.sb("cand_rest", [P, XT, CANDS])
        SO, CI = ph.sb("score", [P, XT, K]), ph.sb("ci", [P, XT, K], U32)
        BITS, BITF = ph.sb("bits", [P, 4, XT, K], U32), ph.sb("bits_float", [P, 4, XT, K])
        CF, ABF = ph.sb("c_float", [P, XT, K]), ph.sb("ab_half", [P, 2, XT, K], F16)
        EQ = ph.sb("eq", [P, 2, XT, K, K], F16)
        TOP, SUM = ph.sb("top", [P, XT]), ph.sb("sum", [P, XT])
        iota_i, iota = ph.sb("iota_int", [P, K, K], mybir.dt.int32), ph.sb("iota", [P, K, K], F16)
        SEL = k["sel"]
        QP = [ph.ps(f"qp{u}", [P, HALVES, 512]) for u in range(2)]
        SP_ = [ph.ps(f"sp{u}", [P, XT, P]) for u in range(2)]
        keys_in = ph.sem("keys_in")
        w_in = ph.sems("w_in")
        sig = {n: ph.sem(n) for n in ("w_hi", "w_lo", "passed", "q_raw", "q_ready", "s_raw", "s_ready", "s_read",
                                      "places", "picked", "score_ready", "exp_ready", "iota_ready", "dve_passed")}
        own = ph.sem("dve_own")
        block = ph.block()

        @block.sync
        def _(sp):
            with sp.Fori(0, NQ // 2) as r:
                for u in range(2):
                    sp.wait_ge(sig["w_lo"], 2 * r + u + 1)
                    sp.dma_start(W[u][:], io["wq_blocks"][bass.ds(2 * r + u, 1)].rearrange("a p (b c) -> (a p) b c", c=P)).then_inc(w_in[u], 16)

        @block.gpsimd
        def _(pool):
            pool.sem_inc(sig["w_lo"], 2)
            pool.dma_start(KEYS[:], io["keys"].rearrange("n c e -> c n e")).then_inc(keys_in, 16)
            nc.gpsimd.iota(iota_i[:], pattern=[[1, K], [0, K]], base=0, channel_multiplier=0).then_inc(sig["iota_ready"], 1)

            def split(n, u, r_u):
                pool.wait_ge(w_in[u], 16 * r_u)
                pool.wait_ge(sig["q_raw"], n + 1)
                split_on_pool(nc, pool, W[u][:], WS[u][0][:], WS[u][1][:], sig["w_hi"], n + 1, sig["w_lo"], sig["passed"])

            def pick(h):
                for s in range(2):
                    pool.wait_ge(sig["places"], 2 * h + s + 1)
                    nc.gpsimd.tensor_tensor(EQ[:, s], EQ[:, s], IF[:, s].unsqueeze(3).to_broadcast([P, XT, K, K]), ALU.mult).then_inc(sig["picked"], 1)

            for n in range(4):
                split(n, n % 2, n // 2 + 1)
            with pool.Fori(0, HEADS - 2) as h:
                for u in range(2):
                    split(2 * h + 4 + u, u, h + 3)
                pick(h)
            pick(HEADS - 2)
            pick(HEADS - 1)

        @block.tensor
        def _(pe):
            pe.sem_inc(sig["q_raw"], 2)
            def queries(n, u):
                pe.wait_ge(sig["w_lo"], n + 3)
                pe.wait_ge(sig["q_ready"], n + 1)
                for b in range(DB):
                    for c in range(HALVES):
                        cs = slice(c * 512, (c + 1) * 512)
                        last = mm3(nc, QP[u][:, c, :], (WS[u][0][:, b, :], WS[u][1][:, b, :]), (XS[0][:, b, cs], XS[1][:, b, cs]), b == 0, b == DB - 1)
                last.then_inc(sig["q_raw"], 1)

            def scores(n, u):
                pe.wait_ge(sig["q_ready"], n + 3)
                pe.wait_ge(sig["s_ready"], n + 1)
                for t in range(XT):
                    keys = KEYS[:, bass.ds(n, 1), :].rearrange("p a e -> p (a e)")
                    last = nc.tensor.matmul(SP_[u][:, t, :], QT[u][:, t * P:(t + 1) * P], keys, start=True, stop=True)
                last.then_inc(sig["s_raw"], 1)

            queries(0, 0)
            pe.wait_ge(keys_in, 16)
            with pe.Fori(0, NQ // 2 - 1) as r:
                queries(2 * r + 1, 1)
                scores(2 * r, 0)
                queries(2 * r + 2, 0)
                scores(2 * r + 1, 1)
            queries(NQ - 1, 1)
            scores(NQ - 2, 0)
            scores(NQ - 1, 1)

        @block.scalar
        def _(act):
            act.sem_inc(sig["q_ready"], 2)

            def copy(n, u):
                act.wait_ge(sig["q_raw"], n + 3)
                act.wait_ge(sig["s_raw"], n + 1)
                nc.scalar.copy(QT[u][:].rearrange("p (a b) -> p a b", a=HALVES), QP[u][:]).then_inc(sig["q_ready"], 1)

            def take(n, u):
                act.wait_ge(sig["s_raw"], n + 3)
                act.wait_ge(sig["s_read"], n + 1)
                nc.scalar.copy(SC[u][:], SP_[u][:]).then_inc(sig["s_ready"], 1)

            def exp(h):
                act.wait_ge(sig["score_ready"], h + 1)
                nc.scalar.activation(SO[:], SO[:], ACT.Exp).then_inc(sig["exp_ready"], 1)

            def body(h):
                copy(2 * h + 1, 1)
                take(2 * h, 0)
                copy(2 * h + 2, 0)
                take(2 * h + 1, 1)

            copy(0, 0)
            body(0)
            with act.Fori(1, HEADS - 1) as h:
                body(h)
                exp(h - 1)
            copy(NQ - 1, 1)
            take(NQ - 2, 0)
            take(NQ - 1, 1)
            exp(HEADS - 2)
            exp(HEADS - 1)

        @block.vector
        def _(dve):
            ch = Chain(dve, own)
            tt, ts = nc.vector.tensor_tensor, nc.vector.tensor_scalar
            dve.sem_inc(sig["s_raw"], 2)
            dve.sem_inc(sig["s_ready"], 2)
            dve.sem_inc(sig["s_read"], 2)

            def top16(src, rest, v, i):
                for t in range(XT):
                    ch.mark(nc.vector.max(v[:, t, 0:8], src[:, t, :]))
                ch.wait()
                for t in range(XT):
                    ch.mark(nc.vector.max_index(i[:, t, 0:8], v[:, t, 0:8], src[:, t, :]))
                    ch.mark(nc.vector.match_replace(rest[:, t, :], v[:, t, 0:8], src[:, t, :], LOWEST))
                ch.wait()
                for t in range(XT):
                    ch.mark(nc.vector.max(v[:, t, 8:16], rest[:, t, :]))
                ch.wait()
                for t in range(XT):
                    ch.mark(nc.vector.max_index(i[:, t, 8:16], v[:, t, 8:16], rest[:, t, :]))
                ch.wait()

            def keys_of_sides(h):
                for s in range(2):
                    dve.wait_ge(sig["s_ready"], 2 * h + s + 3)
                    dve.sem_inc(sig["dve_passed"], 1)
                    top16(SC[s], REST, V[:, s], I[:, s])
                    dve.sem_inc(sig["s_read"], 1)

            def pairs(h):
                for first, rows, width in ((0, WHOLE, K), (WHOLE, K - WHOLE, NARROW)):
                    start = 0 if first == 0 else SPLIT
                    ch.mark(tt(CAND[:, :, start:start + rows * width].rearrange("p t (a b) -> p t a b", a=rows),
                               V[:, 0, :, first:first + rows].unsqueeze(3).to_broadcast([P, XT, rows, width]),
                               V[:, 1, :, 0:width].unsqueeze(2).to_broadcast([P, XT, rows, width]), ALU.add))
                ch.wait()
                top16(CAND, CREST, SO, CI)
                ch.mark(nc.vector.tensor_copy(IF[:], I[:]))
                ch.mark(nc.vector.tensor_copy(CF[:], CI[:]))
                for j, (bits, op) in enumerate(((4, ALU.logical_shift_right), (2, ALU.logical_shift_right), (K - 1, ALU.bitwise_and), (K - NARROW, ALU.bitwise_and))):
                    ch.mark(ts(BITS[:, j], CI[:], bits, None, op))
                ch.step(nc.vector.tensor_copy(TOP[:], SO[:, :, 0:1].rearrange("p t a -> p (t a)")))
                ch.step(nc.vector.tensor_copy(BITF[:], BITS[:]))
                stt = nc.vector.scalar_tensor_tensor
                ch.mark(stt(out=ABF[:, 0], in0=BITF[:, 1], scalar=float(WHOLE - SPLIT // NARROW), in1=BITF[:, 0], op0=ALU.add, op1=ALU.max))
                ch.step(stt(out=CF[:], in0=CF[:], scalar=float(SPLIT), in1=BITF[:, 3], op0=ALU.is_ge, op1=ALU.mult))
                ch.step(tt(ABF[:, 1], BITF[:, 2], CF[:], ALU.subtract))
                tt(SO[:], SO[:], TOP[:].unsqueeze(2).to_broadcast([P, XT, K]), ALU.subtract).then_inc(sig["score_ready"], 1)
                for s in range(2):
                    tt(EQ[:, s], ABF[:, s].unsqueeze(2).to_broadcast([P, XT, K, K]), iota[:].unsqueeze(1).to_broadcast([P, XT, K, K]), ALU.is_equal).then_inc(sig["places"], 1)

            def select(h):
                slots = bass.ds(h * K, K)
                dve.wait_ge(sig["picked"], 2 * h + 2)
                size = K // 2
                while size > 1:
                    for s in range(2):
                        ch.mark(tt(EQ[:, s, :, 0:size], EQ[:, s, :, 0:size], EQ[:, s, :, size:2 * size], ALU.add))
                    ch.wait()
                    size //= 2
                for s in range(2):
                    ch.mark(tt(SEL[:, :, s, slots], EQ[:, s, :, 0], EQ[:, s, :, 1], ALU.add))
                dve.wait_ge(sig["exp_ready"], h + 1)
                ch.step(nc.vector.tensor_reduce(SUM[:], SO[:], AX.X, ALU.add))
                ch.step(nc.vector.reciprocal(SUM[:], SUM[:]))
                ch.mark(tt(SEL[:, :, 2, slots], SO[:], SUM[:].unsqueeze(2).to_broadcast([P, XT, K]), ALU.mult))

            dve.wait_ge(sig["iota_ready"], 1)
            ch.mark(nc.vector.tensor_copy(iota[:], iota_i[:]))
            keys_of_sides(0)
            pairs(0)
            ch.restart()
            with dve.Fori(1, HEADS) as h:
                keys_of_sides(h)
                select(h - 1)
                ch.wait()
                pairs(h)
                ch.restart()
            select(HEADS - 1)
            ch.wait()


def gates_phase(nc, k, io):
    UNIT = 16
    HALF = UNIT // 2
    ROUNDS = P // UNIT
    GATE_SCALE = 2.0 ** 14
    SEL = k["sel"]
    with Phase(nc, "gates") as ph:
        keys_i, iota = ph.sb("keys_int", [P, P], mybir.dt.int32), ph.sb("iota", [P, P, UNIT], F16)
        IJ = ph.sb("ij_half", [P, 2, SEQ], F16)
        GH = ph.sb("gate_half", [P, 2, SEQ], F16)
        GF = [ph.sb(f"gate{u}", [P, P]) for u in range(2)]
        OH = [ph.sb(f"onehot{u}", [P, 4, P, UNIT], F16) for u in range(2)]
        GS = [ph.sb(f"g{v}", [P, P, P]) for v in range(2)]
        TP = [ph.ps(f"t{u}", [P, 3, P]) for u in range(2)]
        GP = [ph.ps(f"gp{s}", [P, HALF, P]) for s in range(2)]
        g_out = ph.sems("g_out")
        sig = {n: ph.sem(n) for n in ("t_ready", "t_read", "onehots", "g_raw", "g_copied", "iota_ready", "equal")}
        own = ph.sem("dve_own")
        block = ph.block()

        @block.sync
        def _(sp):
            with sp.Fori(0, XT // 2) as r:
                for v in range(2):
                    n = 2 * r + v
                    sp.wait_ge(sig["g_copied"], 2 * ROUNDS * (n + 1) + 2)
                    sp.dma_start(io["g"][bass.ds(n, 1)].rearrange("a i j t -> (a i) j t"), GS[v][:]).then_inc(g_out[v], 16)
            for v in range(2):
                sp.wait_ge(g_out[v], 16 * (XT // 2 + 1))

        @block.gpsimd
        def _(pool):
            nc.gpsimd.iota(keys_i[:], pattern=[[1, P]], base=0, channel_multiplier=0).then_inc(sig["iota_ready"], 1)

        @block.vector
        def _(dve):
            ch = Chain(dve, own)
            tt, ts = nc.vector.tensor_tensor, nc.vector.tensor_scalar
            dve.wait_ge(sig["iota_ready"], 1)
            ch.mark(nc.vector.tensor_copy(iota[:], keys_i[:].unsqueeze(2).to_broadcast([P, P, UNIT])))
            for n in range(XT):
                u, cols = n % 2, slice(n * P, (n + 1) * P)
                dve.wait_ge(sig["t_ready"], n + 1)
                ch.mark(ts(GF[u][:], TP[u][:, 2, :], GATE_SCALE, None, ALU.mult))
                ch.step(nc.vector.tensor_copy(IJ[:, :, cols], TP[u][:, 0:2, :]))
                dve.sem_inc(sig["t_read"], 1)
                ch.step(nc.vector.tensor_copy(GH[:, 0, cols], GF[u][:]))
                ch.mark(tt(GH[:, 1, cols], GF[u][:], GH[:, 0, cols], ALU.subtract))
            ch.wait()
            over_keys = lambda row: row.unsqueeze(1).to_broadcast([P, P, UNIT])
            with dve.Fori(0, XT * ROUNDS // 2) as i:
                for u in range(2):
                    dve.wait_ge(sig["g_raw"], 2 * (2 * i + u) + 2)
                    cols = bass.ds((2 * i + u) * UNIT, UNIT)
                    for s in (1, 0):
                        tt(OH[u][:, s], iota[:], over_keys(IJ[:, s, cols]), ALU.is_equal).then_inc(sig["equal"], 1)
                    dve.wait_ge(sig["equal"], 2 * (2 * i + u) + 1)
                    for s in range(2):
                        last = tt(OH[u][:, 2 + s], OH[u][:, 1], over_keys(GH[:, s, cols]), ALU.mult)
                    last.then_inc(sig["onehots"], 1)

        @block.scalar
        def _(act):
            act.sem_inc(sig["g_copied"], 2)
            for v in range(2):
                act.sem_inc(g_out[v], 16)
            with act.Fori(0, XT // 2) as r:
                for v in range(2):
                    act.wait_ge(g_out[v], 16 * (r + 1))
                    with act.Fori(0, ROUNDS) as i:
                        for s in range(2):
                            act.wait_ge(sig["g_raw"], 2 * ROUNDS * (2 * r + v) + 2 * i + s + 5)
                            nc.scalar.mul(GS[v][:, :, bass.ds(i * UNIT + s * HALF, HALF)].rearrange("p j t -> p t j"), GP[s][:], 1.0 / GATE_SCALE).then_inc(sig["g_copied"], 1)

        @block.tensor
        def _(pe):
            pe.sem_inc(sig["g_raw"], 4)
            for n in range(XT):
                if n >= 2:
                    pe.wait_ge(sig["t_read"], n - 1)
                for s in range(3):
                    last = nc.tensor.transpose(TP[n % 2][:, s, :], SEL[:, n, s, :], k["ident"][:])
                last.then_inc(sig["t_ready"], 1)
            with pe.Fori(0, XT * ROUNDS // 2) as i:
                for u in range(2):
                    done = 2 * i + u
                    pe.wait_ge(sig["onehots"], done + 1)
                    for s in range(2):
                        pe.wait_ge(sig["g_copied"], 2 * done + s + 1)
                        for t in range(HALF):
                            tok = s * HALF + t
                            for q in range(2):
                                last = nc.tensor.matmul(GP[s][:, t, :], OH[u][:, 0, :, tok], OH[u][:, 2 + q, :, tok], start=q == 0, stop=q == 1)
                        last.then_inc(sig["g_raw"], 1)


def experts_phase(nc, k, io, half):
    J = 4
    GROUPS = N_KEYS // J
    HT = 512
    NT = HT // P
    NH = D // 512
    COMBOS = NT * NH
    OUT_BANKS = 4
    with Phase(nc, f"experts{half}") as ph:
        XS = [ph.sb(f"x_{p}", [P, DB, HT], F32R) for p in ("hi", "lo")]
        ACC = ph.sb("acc", [P, NT, D])
        UR = [ph.sb(f"u{s}", [P, DB, P]) for s in range(2)]
        VR = [ph.sb(f"v{s}", [P, D]) for s in range(2)]
        GR = [ph.sb(f"g{s}", [P, NT, P]) for s in range(2)]
        US = [[ph.sb(f"u{p}{s}", [P, DB, P], F32R) for p in ("hi", "lo")] for s in range(2)]
        VS = [[ph.sb(f"v{p}{s}", [P, J, D], F32R) for p in ("hi", "lo")] for s in range(2)]
        AS = [[ph.sb(f"a{p}{s}", [P, J, HT], F32R) for p in ("hi", "lo")] for s in range(2)]
        AC = [ph.sb(f"act{s}", [P, HT]) for s in range(2)]
        gain, bias = ph.sb("gain", [P, D]), ph.sb("bias", [P, D])
        stats, mv, std = ph.sb("stats", [P, NH, 6]), ph.sb("mv", [P, 2]), ph.sb("std", [P, 1])
        HID = [ph.ps(f"hid{s}", [P, HT]) for s in range(2)]
        OUT = [ph.ps(f"out{q}", [P, 512]) for q in range(OUT_BANKS)]
        x_in = ph.sems("x_in", DB // 2)
        x_raw = lambda c: AS[c // 2][0][:, c % 2 * 2:c % 2 * 2 + 2, :].bitcast(F32)
        u_in, v_in, g_in = (ph.sems(n) for n in ("u_in", "v_in", "g_in"))
        start_in, out_stored = ph.sem("start_in"), ph.sem("out_stored")
        names = ("x_hi", "x_lo", "acc_ready", "u_hi", "v_hi", "u_lo", "v_lo", "hid", "gelu", "gated", "a_hi", "a_lo",
                 "out", "out_group", "added", "var_ready", "std_ready", "rows_ready")
        sig = {n: ph.sem(n) for n in names}
        own = ph.sem("dve_own")
        block = ph.block()
        tok = slice(half * HT, (half + 1) * HT)

        def groups(eng, body):
            for p in range(2):
                body(p, 0, p, True)
            with eng.Fori(1, GROUPS // 2) as r:
                for p in range(2):
                    body(2 * r + p, r, p, False)

        @block.sync
        def _(sp):
            for c in range(DB // 2):
                sp.dma_start(x_raw(c), io["h1_t"][2 * c:2 * c + 2, :, tok].rearrange("b p t -> p b t")).then_inc(x_in[c], 16)
            with sp.Fori(0, N_KEYS // 2) as r:
                for s in range(2):
                    m = 2 * r + s
                    sp.wait_ge(sig["u_lo"], m + 1)
                    sp.dma_start(UR[s][:], io["u_blocks"][bass.ds(m, 1)].rearrange("a p (b c) -> (a p) b c", c=P)).then_inc(u_in[s], 16)
                    sp.wait_ge(sig["v_lo"], m + 1)
                    sp.dma_start(VR[s][:], io["v_blocks"][bass.ds(m, 1)].rearrange("a p d -> (a p) d")).then_inc(v_in[s], 16)
            for n in range(NT):
                sp.wait_ge(sig["rows_ready"], n + 1)
                sp.dma_start(io["out"][half * HT + n * P:half * HT + (n + 1) * P, :], ACC[:, n, :]).then_inc(out_stored, 16)
            sp.wait_ge(out_stored, 16 * NT)

        @block.gpsimd
        def _(pool):
            pool.dma_start(ACC[:], io["h1_rows"][tok, :].rearrange("(n p) d -> p n d", p=P)).then_inc(start_in, 16)
            pool.dma_start(gain[:], row_bcast(io["ln2_g"])).then_inc(start_in, 16)
            pool.dma_start(bias[:], row_bcast(io["ln2_b"])).then_inc(start_in, 16)
            with pool.Fori(0, N_KEYS // (2 * J)) as r:
                for e in range(2 * J):
                    m, s, p, j = 2 * J * r + e, e % 2, e // J, e % J
                    pool.wait_ge(sig["gated"], m + 1)
                    pool.dma_start(GR[s][:], io["g"][half * NT:(half + 1) * NT, :, bass.ds(m, 1), :].rearrange("n i j t -> i (n j) t")).then_inc(g_in[s], 16)
                    pool.wait_ge(sig["v_hi"], m + 1)
                    nc.gpsimd.tensor_tensor(VS[p][1][:, j, :], VR[s][:], VS[p][0][:, j, :].bitcast(F32), ALU.subtract).then_inc(sig["v_lo"], 1)

        @block.tensor
        def _(pe):
            pe.sem_inc(sig["hid"], 2)
            pe.sem_inc(sig["out_group"], 2)
            pe.wait_ge(sig["x_lo"], DB // 2)

            def hidden(m, s):
                pe.wait_ge(sig["u_lo"], m + 3)
                pe.wait_ge(sig["gelu"], m + 1)
                for b in range(DB):
                    last = mm3(nc, HID[s][:], (US[s][0][:, b, :], US[s][1][:, b, :]), (XS[0][:, b, :], XS[1][:, b, :]), b == 0, b == DB - 1)
                last.then_inc(sig["hid"], 1)

            def outputs(g, p):
                pe.wait_ge(sig["a_lo"], J * (g + 1))
                pe.wait_ge(sig["v_lo"], J * (g + 1) + 2)
                for q in range(COMBOS):
                    n, c = q // NH, q % NH
                    pe.wait_ge(sig["added"], COMBOS * g + q + 1)
                    for j in range(J):
                        last = mm3(nc, OUT[q % OUT_BANKS][:], (AS[p][0][:, j, n * P:(n + 1) * P], AS[p][1][:, j, n * P:(n + 1) * P]),
                                   (VS[p][0][:, j, c * 512:(c + 1) * 512], VS[p][1][:, j, c * 512:(c + 1) * 512]), j == 0, j == J - 1)
                    last.then_inc(sig["out"], 1)
                pe.wait_ge(sig["out"], COMBOS * (g + 1))
                pe.sem_inc(sig["out_group"], 1)

            def body(g, r, p, first):
                for j in range(J):
                    hidden(J * g + j, j % 2)
                if not (first and p == 0):
                    outputs(g - 1, 1 - p)
            groups(pe, body)
            outputs(GROUPS - 1, 1)

        @block.scalar
        def _(act):
            act.sem_inc(sig["gelu"], 2)
            for c in range(DB // 2):
                act.wait_ge(x_in[c], 16)
                nc.scalar.copy(XS[0][:, 2 * c:2 * c + 2, :], x_raw(c)).then_inc(sig["x_hi"], 1)

            def split_u(m, r_s, s):
                act.wait_ge(u_in[s], 16 * r_s)
                act.wait_ge(sig["hid"], m + 1)
                nc.scalar.copy(US[s][0][:], UR[s][:]).then_inc(sig["u_hi"], 1)

            def split_v(m, r_s, s, g, p, j):
                act.wait_ge(v_in[s], 16 * r_s)
                if j == 0:
                    act.wait_ge(sig["out_group"], g + 1)
                nc.scalar.copy(VS[p][0][:, j, :], VR[s][:]).then_inc(sig["v_hi"], 1)

            def activate(m, s, p, j):
                act.wait_ge(sig["hid"], m + 3)
                act.wait_ge(sig["a_lo"], m - 1) if not isinstance(m, int) or m >= 2 else None
                nc.scalar.activation(AC[s][:], HID[s][:], ACT.Gelu).then_inc(sig["gelu"], 1)
                act.wait_ge(sig["gated"], m + 3)
                nc.scalar.copy(AS[p][0][:, j, :], AC[s][:]).then_inc(sig["a_hi"], 1)

            def body(g, r, p, first):
                for j in range(J):
                    m = J * g + j
                    split_u(m, J // 2 * g + j // 2 + 1, j % 2)
                    if j:
                        activate(m - 1, (j - 1) % 2, p, j - 1)
                    elif not (first and p == 0):
                        activate(m - 1, 1, 1 - p, J - 1)
                    split_v(m, J // 2 * g + j // 2 + 1, j % 2, g, p, j)
                    if first and p == 0 and j == J - 1:
                        act.wait_ge(start_in, 48)
                        nc.scalar.mul(ACC[:], ACC[:], ALPHA).then_inc(sig["acc_ready"], 1)
            groups(act, body)
            activate(N_KEYS - 1, 1, 1, J - 1)
            for n in range(NT):
                act.wait_ge(sig["var_ready"], n + 1)
                nc.scalar.activation(std[:], std[:], ACT.Sqrt).then_inc(sig["std_ready"], 1)

        @block.vector
        def _(dve):
            ch = Chain(dve, own)
            tt = nc.vector.tensor_tensor
            dve.sem_inc(sig["v_lo"], 2)
            dve.sem_inc(sig["u_lo"], 2)
            dve.sem_inc(sig["gated"], 2)
            dve.sem_inc(sig["added"], OUT_BANKS)
            for c in range(DB // 2):
                dve.wait_ge(sig["x_hi"], c + 1)
                tt(XS[1][:, 2 * c:2 * c + 2, :], x_raw(c), XS[0][:, 2 * c:2 * c + 2, :].bitcast(F32), ALU.subtract).then_inc(sig["x_lo"], 1)

            def split_u(m, s):
                dve.wait_ge(sig["u_hi"], m + 1)
                tt(US[s][1][:], UR[s][:], US[s][0][:].bitcast(F32), ALU.subtract).then_inc(sig["u_lo"], 1)

            def gate(m, r_s, s, p, j):
                dve.wait_ge(g_in[s], 16 * r_s)
                dve.wait_ge(sig["gelu"], m + 3)
                tt(AC[s][:], AC[s][:], GR[s][:].rearrange("p n t -> p (n t)"), ALU.mult).then_inc(sig["gated"], 1)
                dve.wait_ge(sig["a_hi"], m + 1)
                tt(AS[p][1][:, j, :], AC[s][:], AS[p][0][:, j, :].bitcast(F32), ALU.subtract).then_inc(sig["a_lo"], 1)

            def add(g, banks=range(COMBOS)):
                for q in banks:
                    rows = ACC[:, q // NH, (q % NH) * 512:(q % NH + 1) * 512]
                    dve.wait_ge(sig["out"], COMBOS * g + q + 1)
                    tt(rows, OUT[q % OUT_BANKS][:], rows, ALU.add).then_inc(sig["added"], 1)

            def body(g, r, p, first):
                for j in range(J):
                    m = J * g + j
                    split_u(m, j % 2)
                    if j:
                        gate(m - 1, J // 2 * g + (j - 1) // 2 + 1, (j - 1) % 2, p, j - 1)
                    elif not (first and p == 0):
                        gate(m - 1, J // 2 * g, 1, 1 - p, J - 1)
                        if first:
                            dve.wait_ge(sig["acc_ready"], 1)
                        if not first:
                            add(g - 2)
            groups(dve, body)
            gate(N_KEYS - 1, N_KEYS // 2, 1, 1, J - 1)
            add(GROUPS - 2)
            for n in range(NT):
                add(GROUPS - 1, range(NH * n, NH * (n + 1)))
                dve.wait_ge(sig["added"], COMBOS * (GROUPS - 1) + NH * (n + 1) + OUT_BANKS)
                h = ACC[:, n, :]
                for c in range(NH):
                    ch.mark(nc.vector.bn_stats(stats[:, c, :], h[:, c * 512:(c + 1) * 512]))
                ch.wait()
                ch.step(nc.vector.bn_aggr(mv[:], stats[:]))
                nc.vector.tensor_scalar(std[:], mv[:, 1:2], LN_EPS, None, ALU.add).then_inc(sig["var_ready"], 1)
                dve.wait_ge(sig["std_ready"], n + 1)
                ch.step(nc.vector.reciprocal(std[:], std[:]))
                ch.step(nc.vector.tensor_scalar(h, h, mv[:, 0:1], std[:], ALU.subtract, ALU.mult))
                ch.step(tt(h, h, gain[:], ALU.mult))
                tt(h, h, bias[:], ALU.add).then_inc(sig["rows_ready"], 1)


def build(nc, io):
    with ExitStack() as ctx:
        def keep(scope, name, shape, dt=F32):
            return scope.enter_context(nc.sbuf_tensor(name, shape, dt))

        k = {m: keep(ctx, f"const_{m}", [P, P]) for m in ("ident", "ones", "upper", "lower", "same_head", "in16", "in32")}
        make_constants(nc, k)
        with ExitStack() as h_scope:
            k["hT_hi"], k["hT_lo"] = (keep(h_scope, f"hT_{p}", [P, DB, T], F32R) for p in ("hi", "lo"))
            embed_norm_phase(nc, k, io)
            project_phase(nc, k, io)
            delta_phase(nc, k, io)
        branch_phase(nc, k, io)
        with ExitStack() as sel_scope:
            k["sel"] = keep(sel_scope, "sel", [P, XT, 3, HEADS * TOPK])
            with ExitStack() as h1_scope:
                k["h1T_hi"], k["h1T_lo"] = (keep(h1_scope, f"h1T_{p}", [P, DB, SEQ], F32R) for p in ("hi", "lo"))
                mix_phase(nc, k, io)
                query_phase(nc, k, io)
            gates_phase(nc, k, io)
        for half in range(2):
            experts_phase(nc, k, io, half)


SCRATCH = {
    "h_rows": (SEQ, D),
    "proj": (N_BLK, P, T),
    "bg": (T, 16),
    "o_rows": (SEQ // CHUNK, P, PAIRS * HD),
    "merged": (DB, P, SEQ),
    "h1_rows": (SEQ, D),
    "h1_t": (DB, P, SEQ),
    "g": (XT, P, P, P),
}
INPUTS = ("x", "meta", "ln0_g", "ln0_b", "w_blocks", "conv_taps", "w_ba", "a_log", "dt_bias", "onorm_g",
          "pool_w", "pool_scale", "w_branches", "w_out", "ln1_g", "ln1_b", "wq_blocks", "keys", "u_blocks", "v_blocks", "ln2_g", "ln2_b")


def lay_out(x, meta, ln0_g, ln0_b, w_in, pool_w, pool_scale, w_br_pool, conv_w, a_log, dt_bias, onorm_g, w_br_delta,
            w_out, ln1_g, ln1_b, peer_wq, peer_k1, peer_k2, peer_u, peer_v, ln2_g, ln2_b):
    a = {}
    a["x"], a["meta"] = x[0], meta
    a["ln0_g"], a["ln0_b"] = ln0_g, ln0_b
    w = w_in[0]
    pw, dw = POOL_GROUPS * P, HEADS * HD
    q0, z0 = pw, pw + 3 * dw
    b0 = z0 + dw
    g0 = b0 + 2 * HEADS
    cols = np.concatenate([w[:, q0:z0], w[:, :pw], w[:, z0:b0], w[:, g0:]], axis=1)
    blocks = lambda m: m.reshape(-1, P, m.shape[1] // P, P).transpose(2, 1, 0, 3).reshape(m.shape[1] // P, P, -1)
    a["w_blocks"] = blocks(cols)
    a["w_ba"] = w[:, b0:g0].reshape(DB, P, 16).transpose(1, 0, 2).reshape(P, -1)
    a["conv_taps"] = conv_w[0].reshape(TAPS, 3 * HEADS, P).transpose(2, 1, 0).reshape(P, -1)
    a["a_log"], a["dt_bias"], a["onorm_g"] = a_log[0], dt_bias[0], onorm_g[0]
    a["pool_w"] = pool_w[0].transpose(1, 0, 2).reshape(P, -1)
    a["pool_scale"] = pool_scale[0].reshape(POOL_GROUPS, P).T
    a["w_branches"] = blocks(np.concatenate([w_br_delta[0], w_br_pool[0]], axis=0))
    a["w_out"], a["ln1_g"], a["ln1_b"] = w_out[0], ln1_g[0], ln1_b[0]
    a["wq_blocks"] = blocks(peer_wq[0])
    a["keys"] = np.stack([peer_k1[0], peer_k2[0]], axis=1).reshape(2 * HEADS, N_KEYS, P).transpose(0, 2, 1)
    a["u_blocks"] = peer_u[0].reshape(P, P, DB, P).transpose(1, 3, 2, 0).reshape(P, P, -1)
    a["v_blocks"] = peer_v[0].reshape(P, P, D).transpose(1, 0, 2)
    a["ln2_g"], a["ln2_b"] = ln2_g[0], ln2_b[0]
    return a


def kernel(**inputs):
    import concourse.bacc as bacc
    from concourse.bass_utils import run_bass_kernel_spmd

    nc = bacc.Bacc("TRN2", target_bir_lowering=False, num_devices=1)
    laid = lay_out(**{n: np.asarray(v) for n, v in inputs.items()})
    tensors, arrays = {}, {}
    for name in INPUTS:
        arrays[f"in_{name}"] = np.ascontiguousarray(laid[name])
        tensors[name] = nc.dram_tensor(f"in_{name}", arrays[f"in_{name}"].shape, F32, kind="ExternalInput").ap()
    for name, shape in SCRATCH.items():
        tensors[name] = nc.dram_tensor(name, shape, F32, kind="Internal").ap()
    tensors["out"] = nc.dram_tensor("out", (SEQ, D), F32, kind="ExternalOutput").ap()
    build(nc, tensors)
    r = run_bass_kernel_spmd(nc, [arrays], core_ids=[0])
    return r.results[0]["out"].reshape(1, SEQ, D)
```
